# Optimizing a Trainium2 kernel written in Bass

```python
import math, functools
import jax, jax.numpy as jnp
from jax import lax
import numpy as np

D_MODEL = 1024
BATCH = 1
SEQ = 2048
DEPTH = 1
DEC_BATCH = 8
DEC_SEQ = 1
PAST_LEN = 4096
PAGE_SIZE = 128

N_META = 16
D_MIX = D_MODEL
D_ATT = D_MIX // 2
D_RNN = D_MIX - D_ATT
HEAD_DIM = 64
N_ATT_HEADS = D_ATT // HEAD_DIM
N_RNN_BLOCKS = 8
RNN_BLOCK = D_RNN // N_RNN_BLOCKS
RNN_CONV = 4
RG_C = 8.0
D_FF = 11 * D_MODEL // 4
FFN_CONV = 3
Q_BLOCK = 128
EPS = 1e-6
ATT_SCALE = HEAD_DIM ** -0.5
FORGET_BIAS_LO = 2.0
FORGET_BIAS_HI = 6.0
D_IN = 3 * D_ATT + N_ATT_HEADS + 2 * D_RNN
SPLIT_IDX = (D_ATT, 2 * D_ATT, 3 * D_ATT, 3 * D_ATT + N_ATT_HEADS, 3 * D_ATT + N_ATT_HEADS + D_RNN)

kernel_name = 'fox_rglru_hymba_decode_step'

def rmsnorm(x, g):
    xf = x.astype(jnp.float32)
    y = xf * lax.rsqrt(jnp.mean(xf * xf, axis=-1, keepdims=True) + EPS) * g.astype(jnp.float32)
    return y.astype(x.dtype)

def causal_dwconv(x, buf, w, b):
    t = x.shape[1]
    width = w.shape[0]
    xp = jnp.concatenate([buf.astype(x.dtype), x], axis=1)
    y = b + sum(w[j] * xp[:, j:j + t] for j in range(width))
    return y, xp[:, t:]

def linear_recurrence(a, u, h0):
    def combine(left, right):
        a_l, u_l = left
        a_r, u_r = right
        return a_l * a_r, a_r * u_l + u_r
    a_cum, u_cum = lax.associative_scan(combine, (a, u), axis=1)
    return a_cum * h0[:, None, :] + u_cum

def forget_attend(q, cq, qpos, k, v, ck, kpos):
    s = jnp.einsum('bqhd,bkhd->bhqk', q, k).astype(jnp.float32) * ATT_SCALE
    s = s + jnp.swapaxes(cq, 1, 2)[:, :, :, None] - jnp.swapaxes(ck, 1, 2)[:, :, None, :]
    s = jnp.where(kpos[None, :] <= qpos[:, None], s, -jnp.inf)
    p = jax.nn.softmax(s, axis=-1)
    return jnp.einsum('bhqk,bkhd->bqhd', p.astype(v.dtype), v)

def prompt_attention(q, k, v, logf):
    b, t = q.shape[:2]
    n_real = t - N_META
    nb = n_real // Q_BLOCK
    c = jnp.cumsum(logf.astype(jnp.float32), axis=1)
    pos = jnp.arange(t)
    o_meta = forget_attend(q[:, :N_META], c[:, :N_META], pos[:N_META],
                           k[:, :N_META], v[:, :N_META], c[:, :N_META], pos[:N_META])
    qb = q[:, N_META:].reshape(b, nb, Q_BLOCK, N_ATT_HEADS, HEAD_DIM).swapaxes(0, 1)
    cb = c[:, N_META:].reshape(b, nb, Q_BLOCK, N_ATT_HEADS).swapaxes(0, 1)
    pb = pos[N_META:].reshape(nb, Q_BLOCK)
    ob = lax.map(lambda blk: forget_attend(blk[0], blk[1], blk[2], k, v, c, pos), (qb, cb, pb))
    o_real = ob.swapaxes(0, 1).reshape(b, n_real, N_ATT_HEADS, HEAD_DIM)
    return jnp.concatenate([o_meta, o_real], axis=1)

def sample_attention(q, k, v, logf, k_past, v_past, logf_past):
    p_len = k_past.shape[1]
    s_len = q.shape[1]
    k_all = jnp.concatenate([k_past.astype(k.dtype), k], axis=1)
    v_all = jnp.concatenate([v_past.astype(v.dtype), v], axis=1)
    c = jnp.cumsum(jnp.concatenate([logf_past.astype(jnp.float32), logf.astype(jnp.float32)], axis=1), axis=1)
    kpos = jnp.arange(p_len + s_len)
    qpos = p_len + jnp.arange(s_len)
    return forget_attend(q, c[:, p_len:], qpos, k_all, v_all, c, kpos)

def rg_lru_branch(xr, gr, conv_buf, h0, lp):
    xc, conv_new = causal_dwconv(xr, conv_buf, lp['rnn_conv_w'], lp['rnn_conv_b'])
    b, t = xc.shape[:2]
    xb = xc.reshape(b, t, N_RNN_BLOCKS, RNN_BLOCK)
    gate_a = jnp.einsum('btnc,ncd->btnd', xb, lp['w_rg_a']).reshape(b, t, D_RNN) + lp['b_rg_a']
    gate_x = jnp.einsum('btnc,ncd->btnd', xb, lp['w_rg_x']).reshape(b, t, D_RNN) + lp['b_rg_x']
    r = jax.nn.sigmoid(gate_a.astype(jnp.float32))
    i = jax.nn.sigmoid(gate_x.astype(jnp.float32))
    log_a = -RG_C * r * jax.nn.softplus(-lp['rg_lambda'].astype(jnp.float32))
    a = jnp.exp(log_a)
    u = jnp.sqrt(-jnp.expm1(2.0 * log_a)) * (i * xc.astype(jnp.float32))
    h = linear_recurrence(a, u, h0.astype(jnp.float32))
    y = h * jax.nn.gelu(gr.astype(jnp.float32))
    return y.astype(xr.dtype), h[:, -1], conv_new

def gated_conv_ffn(hn, buf, lp):
    g_pre, val = jnp.split(hn @ lp['w_ffn_up'], 2, axis=-1)
    g, buf_new = causal_dwconv(g_pre, buf, lp['ffn_conv_w'], lp['ffn_conv_b'])
    return (jax.nn.gelu(g) * val) @ lp['w_ffn_down'], buf_new

def layer_forward(x, attention, rnn_conv_buf, rnn_h0, ffn_buf, lp):
    b, t = x.shape[:2]
    hn = rmsnorm(x, lp['norm_mix'])
    q, k, v, f_logit, xr, gr = jnp.split(hn @ lp['w_in'], SPLIT_IDX, axis=-1)
    q = q.reshape(b, t, N_ATT_HEADS, HEAD_DIM)
    k = k.reshape(b, t, N_ATT_HEADS, HEAD_DIM)
    v = v.reshape(b, t, N_ATT_HEADS, HEAD_DIM)
    logf = jax.nn.log_sigmoid(f_logit.astype(jnp.float32) + lp['b_forget'].astype(jnp.float32))
    att = attention(q, k, v, logf).reshape(b, t, D_ATT)
    rnn, h_last, rnn_conv_new = rg_lru_branch(xr, gr, rnn_conv_buf, rnn_h0, lp)
    merged = jnp.concatenate([rmsnorm(att, lp['norm_att_out']), rmsnorm(rnn, lp['norm_rnn_out'])], axis=-1)
    x = x + merged @ lp['w_out']
    f, ffn_new = gated_conv_ffn(rmsnorm(x, lp['norm_ffn']), ffn_buf, lp)
    x = x + f
    return x, (k, v, logf, h_last, rnn_conv_new, ffn_new)

def setup_inputs(seed: int = 0) -> dict:
    key = jax.random.key(seed)
    ks = jax.random.split(key, 32)
    f32 = jnp.float32
    n_pages = PAST_LEN // PAGE_SIZE
    n_used = DEC_BATCH * n_pages
    n_pool = n_used + max(1, n_used // 4)

    def nrm(k, shape, scale=1.0):
        return scale * jax.random.normal(k, shape, f32)

    head_bias = jnp.linspace(FORGET_BIAS_LO, FORGET_BIAS_HI, N_ATT_HEADS, dtype=f32)
    u = jax.random.uniform(ks[19], (DEPTH, D_RNN), f32, 0.9, 0.999)
    s = u ** (1.0 / RG_C)
    return {
        'x_prompt': nrm(ks[0], (BATCH, SEQ, D_MODEL)),
        'x_sample': nrm(ks[1], (DEC_BATCH, DEC_SEQ, D_MODEL)),
        'cache_k': nrm(ks[2], (DEPTH, n_pool, PAGE_SIZE, N_ATT_HEADS, HEAD_DIM)),
        'cache_v': nrm(ks[3], (DEPTH, n_pool, PAGE_SIZE, N_ATT_HEADS, HEAD_DIM)),
        'cache_logf': jax.nn.log_sigmoid(head_bias + nrm(ks[4], (DEPTH, n_pool, PAGE_SIZE, N_ATT_HEADS))),
        'state_rnn_h': nrm(ks[5], (DEPTH, DEC_BATCH, D_RNN), 0.5),
        'state_rnn_conv': nrm(ks[6], (DEPTH, DEC_BATCH, RNN_CONV - 1, D_RNN)),
        'state_ffn_conv': nrm(ks[7], (DEPTH, DEC_BATCH, FFN_CONV - 1, D_FF)),
        'page_table': jax.random.permutation(ks[8], n_pool)[:n_used].reshape(DEC_BATCH, n_pages).astype(jnp.int32),
        'meta_tokens': nrm(ks[9], (N_META, D_MODEL)),
        'norm_mix': 1.0 + nrm(ks[10], (DEPTH, D_MODEL), 0.02),
        'w_in': nrm(ks[11], (DEPTH, D_MODEL, D_IN), D_MODEL ** -0.5),
        'b_forget': head_bias + nrm(ks[12], (DEPTH, N_ATT_HEADS), 0.1),
        'rnn_conv_w': nrm(ks[13], (DEPTH, RNN_CONV, D_RNN), RNN_CONV ** -0.5),
        'rnn_conv_b': nrm(ks[14], (DEPTH, D_RNN), 0.02),
        'w_rg_a': nrm(ks[15], (DEPTH, N_RNN_BLOCKS, RNN_BLOCK, RNN_BLOCK), RNN_BLOCK ** -0.5),
        'b_rg_a': nrm(ks[16], (DEPTH, D_RNN), 0.02),
        'w_rg_x': nrm(ks[17], (DEPTH, N_RNN_BLOCKS, RNN_BLOCK, RNN_BLOCK), RNN_BLOCK ** -0.5),
        'b_rg_x': nrm(ks[18], (DEPTH, D_RNN), 0.02),
        'rg_lambda': jnp.log(s) - jnp.log1p(-s),
        'norm_att_out': 1.0 + nrm(ks[20], (DEPTH, D_ATT), 0.02),
        'norm_rnn_out': 1.0 + nrm(ks[21], (DEPTH, D_RNN), 0.02),
        'w_out': nrm(ks[22], (DEPTH, D_MIX, D_MODEL), D_MIX ** -0.5),
        'norm_ffn': 1.0 + nrm(ks[23], (DEPTH, D_MODEL), 0.02),
        'w_ffn_up': nrm(ks[24], (DEPTH, D_MODEL, 2 * D_FF), D_MODEL ** -0.5),
        'ffn_conv_w': nrm(ks[25], (DEPTH, FFN_CONV, D_FF), FFN_CONV ** -0.5),
        'ffn_conv_b': nrm(ks[26], (DEPTH, D_FF), 0.02),
        'w_ffn_down': nrm(ks[27], (DEPTH, D_FF, D_MODEL), D_FF ** -0.5),
        'norm_final': 1.0 + nrm(ks[28], (D_MODEL,), 0.02),
    }

def reference(x_prompt, x_sample, cache_k, cache_v, cache_logf, state_rnn_h, state_rnn_conv,
              state_ffn_conv, page_table, meta_tokens, norm_mix, w_in, b_forget, rnn_conv_w,
              rnn_conv_b, w_rg_a, b_rg_a, w_rg_x, b_rg_x, rg_lambda, norm_att_out, norm_rnn_out,
              w_out, norm_ffn, w_ffn_up, ffn_conv_w, ffn_conv_b, w_ffn_down, norm_final):
    b = x_prompt.shape[0]
    db = x_sample.shape[0]
    xp = jnp.concatenate([jnp.broadcast_to(meta_tokens.astype(x_prompt.dtype)[None], (b, N_META, D_MODEL)),
                          x_prompt], axis=1)
    xs = x_sample
    kp_l, vp_l, fp_l, hp_l, rcp_l, fcp_l = [], [], [], [], [], []
    ks_l, vs_l, fs_l, hs_l, rcs_l, fcs_l = [], [], [], [], [], []
    for l in range(DEPTH):
        lp = {
            'norm_mix': norm_mix[l], 'w_in': w_in[l], 'b_forget': b_forget[l],
            'rnn_conv_w': rnn_conv_w[l], 'rnn_conv_b': rnn_conv_b[l],
            'w_rg_a': w_rg_a[l], 'b_rg_a': b_rg_a[l], 'w_rg_x': w_rg_x[l], 'b_rg_x': b_rg_x[l],
            'rg_lambda': rg_lambda[l], 'norm_att_out': norm_att_out[l], 'norm_rnn_out': norm_rnn_out[l],
            'w_out': w_out[l], 'norm_ffn': norm_ffn[l], 'w_ffn_up': w_ffn_up[l],
            'ffn_conv_w': ffn_conv_w[l], 'ffn_conv_b': ffn_conv_b[l], 'w_ffn_down': w_ffn_down[l],
        }
        xp, (kp, vp, fp, hp, rcp, fcp) = layer_forward(
            xp, prompt_attention,
            jnp.zeros((b, RNN_CONV - 1, D_RNN), xp.dtype),
            jnp.zeros((b, D_RNN), jnp.float32),
            jnp.zeros((b, FFN_CONV - 1, D_FF), xp.dtype), lp)
        k_past = cache_k[l][page_table].reshape(db, -1, N_ATT_HEADS, HEAD_DIM)
        v_past = cache_v[l][page_table].reshape(db, -1, N_ATT_HEADS, HEAD_DIM)
        f_past = cache_logf[l][page_table].reshape(db, -1, N_ATT_HEADS)
        att_fn = functools.partial(sample_attention, k_past=k_past, v_past=v_past, logf_past=f_past)
        xs, (kn, vn, fn, hn, rcn, fcn) = layer_forward(
            xs, att_fn, state_rnn_conv[l], state_rnn_h[l], state_ffn_conv[l], lp)
        kp_l.append(kp); vp_l.append(vp); fp_l.append(fp); hp_l.append(hp); rcp_l.append(rcp); fcp_l.append(fcp)
        ks_l.append(kn); vs_l.append(vn); fs_l.append(fn); hs_l.append(hn); rcs_l.append(rcn); fcs_l.append(fcn)
    y_prompt = rmsnorm(xp, norm_final)[:, N_META:]
    y_sample = rmsnorm(xs, norm_final)
    return (y_prompt, y_sample,
            jnp.stack(kp_l), jnp.stack(vp_l), jnp.stack(fp_l), jnp.stack(hp_l), jnp.stack(rcp_l), jnp.stack(fcp_l),
            jnp.stack(ks_l), jnp.stack(vs_l), jnp.stack(fs_l), jnp.stack(hs_l), jnp.stack(rcs_l), jnp.stack(fcs_l))


_drawn_inputs = setup_inputs


def setup_inputs(seed=0):
    import zlib

    import numpy as np

    out = dict(_drawn_inputs(seed))
    spreads = {}
    factors = {'b_rg_a': 8.0,
     'b_rg_x': 8.0,
     'norm_att_out': 17.776,
     'norm_rnn_out': 17.303,
     'norm_ffn': 7.969,
     'ffn_conv_b': 6.887,
     'norm_final': 7.455}
    for name, (base, spread) in spreads.items():
        noise = np.random.default_rng([zlib.crc32(name.encode()), seed]).standard_normal(out[name].shape)
        drawn = base * np.exp(spread * noise) if base else spread * noise
        out[name] = __import__('jax').numpy.asarray(drawn.astype(out[name].dtype))
    for name, factor in factors.items():
        out[name] = (out[name] * factor).astype(out[name].dtype)
    return out
```

```python
from contextlib import ExitStack

import numpy as np
import concourse.bass as bass
from concourse import mybir

F32 = mybir.dt.float32
F32R = mybir.dt.float32r
BF16 = mybir.dt.bfloat16
I32 = mybir.dt.int32
ALU = mybir.AluOpType
ACT = mybir.ActivationFunctionType
AX = mybir.AxisListType

P = 128
DM = 1024
KC = DM // P
DATT = 512
DRNN = 512
NH = 8
HD = 64
DFF = 2816
FC = DFF // P
FH = FC // 2
RING = 16
NMETA = 16
SEQ = 2048
TPR = NMETA + SEQ
NS = 8
TP = 2080
NB = 5
BW = TP // NB
NT = 17
TAIL = TP - (NT - 1) * P
HB = BW // 2
LASTP = TPR - (NB - 1) * BW
PAGES = 32
NPG = NS * PAGES
NIN = 21
EPS = 1e-6
C_K = DATT
C_V = 2 * DATT
C_F = 3 * DATT
C_XR = C_F + NH
C_GR = C_XR + DRNN
BIG = -1e30


class Steps:

    def __init__(self, eng, sem):
        self.eng, self.sem, self.base, self.k = eng, sem, 0, 0

    def inc(self, ins):
        ins.then_inc(self.sem, 1)
        self.k += 1

    def settle(self):
        self.eng.wait_ge(self.sem, self.base + self.k)

    def start(self, i, per):
        self.at, self.per, self.base = self.base + self.k, per, self.base + self.k + i * per
        self.k = 0

    def stop(self, turns):
        assert self.k == self.per, (self.k, self.per)
        self.base, self.k = self.at + turns * self.per, 0


def seg(j):
    return [(0, P), (P, P), (2 * P, P), (3 * P, BW - 3 * P)]


def cols(j, w=BW):
    return slice(j * w, (j + 1) * w)


def score_tiles():
    found = []
    for j in range(NB):
        end = min((j + 1) * BW, TPR)
        for kt in range((end + P - 1) // P):
            q0 = max(j * BW, kt * P)
            found.append((j, kt, q0, end - q0, min(P, TPR - kt * P)))
    return found


def max_pieces():
    found = []
    for qt in range(NT):
        keys = min((qt + 1) * P, TPR)
        for pc in range((keys + 511) // 512):
            n = min(512, keys - 512 * pc)
            found.append((qt, pc, 512 * pc, n, min(P, TP - qt * P), 512 * pc + n == keys))
    return found


TILES = score_tiles()
PIECES = max_pieces()


def build(nc, a, out):
    ctx = ExitStack()
    with ctx:
        def sb(name, shape, dt, stack=ctx):
            return stack.enter_context(nc.sbuf_tensor(name, shape, dt))

        def sem(name):
            return ctx.enter_context(nc.semaphore(name))

        def dram(name, shape):
            return nc.dram_tensor(name, shape, F32, kind="Internal").ap()

        npool = a["cache_k"].shape[1]
        xT = dram("xT", (DM, TP))
        qT = dram("qT", (DATT, TP))
        kT = dram("kT", (DATT, TP))
        decayT = dram("decayT", (2, NH, TP))
        xrT = dram("xrT", (DRNN, TP))
        grT = dram("grT", (DRNN, TP))
        mixT = dram("mixT", (DM, TP))
        x2T = dram("x2T", (DM, TP))
        gT = dram("gT", (DFF, TP))
        qrow = dram("qrow", (NS, DATT))

        identF = sb("identF", [P, P], F32)
        identB = sb("identB", [P, P], BF16)
        maskQ = sb("maskQ", [P, P], BF16)
        maskK = sb("maskK", [P, P], BF16)
        onesF = sb("onesF", [P, P], F32)
        triu = sb("triu", [P, P], F32)
        epsT = sb("epsT", [P, 1], F32)
        gains = sb("gains", [P, 2 * KC], F32)
        rtab = sb("rtab", [P, 4, 8], F32)
        rstate = sb("rstate", [P, 4, 3, NS], F32)
        rh0 = sb("rh0", [P, 4, 16], F32)
        ftab = sb("ftab", [P, FC, 4], F32)
        fstate = sb("fstate", [P, FC, 2, NS], F32)
        bf = sb("bf", [NH, 1], F32)
        hb = sb("hb", [P, 4, 2], F32)
        sp = sb("sp", [P, 4, 8], F32)
        attS = sb("attS", [P, 4, 16], F32)

        m1 = ExitStack()
        XH = sb("XH", [P, KC, TP], F32R, m1)
        XL = sb("XL", [P, KC, TP], F32R, m1)
        m0 = ExitStack()
        xin = sb("xin", [P, 2, DM], F32, m0)
        hn = sb("hn", [P, 2, DM], F32, m0)
        xst = sb("xst", [P, 2, KC, P], F32, m0)
        sqj = sb("sqj", [P, DM], F32, m0)
        gmix = sb("gmix", [P, DM], F32, m0)
        st0 = sb("st0", [P, 2, 4], F32, m0)
        m0.close()
        WR = sb("WR", [P, 2, KC, P], F32, m1)
        WH = sb("WH", [P, 2, KC, P], F32R, m1)
        WL = sb("WL", [P, 2, KC, P], F32R, m1)
        ZS = sb("ZS", [P, NB, BW], F32, m1)
        TS = sb("TS", [P, 2, 4, P], F32, m1)
        RX = sb("RX", [P, TP + 3], F32, m1)
        RC = sb("RC", [P, TP], F32, m1)
        RW = sb("RW", [P, TP], F32, m1)
        RT = sb("RT", [P, 2, BW], F32, m1)
        gw = sb("gw", [P, 2, P], F32, m1)
        FL, FE, FT, FW = (sb(n, [P, NT, NH], F32, m1) for n in ("FL", "FE", "FT", "FW"))
        FD = sb("FD", [P, NT, 2 * NH], F32, m1)
        m1.close()

        m2 = ExitStack()
        QA = sb("QA", [P, 2, TP], F32R, m2)
        QB = sb("QB", [P, 2, TP], F32R, m2)
        KA = sb("KA", [P, 2, TP], F32R, m2)
        KB = sb("KB", [P, 2, TP], F32R, m2)
        Qst = sb("Qst", [P, TP], F32, m2)
        Kst = sb("Kst", [P, TP], F32, m2)
        Kst2 = sb("Kst2", [P, TP], F32, m2)
        VA = sb("VA", [P, 2, NT, P], F32, m2)
        PT = sb("PT", [P, 3, BW], F32, m2)
        AO = sb("AO", [P, 2, BW], F32, m2)
        rden = sb("rden", [P, BW], F32, m2)
        MP = sb("MP", [P, NT, NB], F32, m2)
        MX = sb("MX", [P, NT], F32, m2)
        NM = sb("NM", [P, NT, 66], F32, m2)
        Kpg = sb("Kpg", [P, 4, 2, DATT], F32, m2)
        Vpg = sb("Vpg", [P, 4, 2, DATT], F32, m2)
        prod = sb("prod", [P, 2, 2, DATT], F32, m2)
        cb = sb("cb", [P, NPG, NH], F32, m2)
        cnew = sb("cnew", [P, NS, NH], F32, m2)
        ctot = Kpg[:, 0:2].rearrange("p a b n -> p (a b n)")
        cwith = Kpg[:, 2:4].rearrange("p a b n -> p (a b n)")
        segm = Vpg[:, 0:2].rearrange("p a b n -> p (a b n)")
        xtp = Vpg[:, 2].rearrange("p b n -> p (b n)")
        lpage = prod[:, :, :, :].rearrange("p a b n -> p a (b n)")
        qb = sb("qb", [P, 2, DATT], F32, m2)
        knb = sb("knb", [P, 2, DATT], F32, m2)
        vnew = sb("vnew", [1, 2, DATT], F32, m2)
        sc = sb("sc", [P, 2, PAGES, NH], F32, m2)
        sn = sb("sn", [P, 2, NH], F32, m2)
        mloc = sb("mloc", [P, 2, NH], F32, m2)
        mall = sb("mall", [P, 2, NH], F32, m2)
        dsum = sb("dsum", [P, 2, NH], F32, m2)
        headmask = sb("headmask", [NH, DATT], F32, m2)
        od = sb("od", [NH, DATT], F32, m2)
        dinv = sb("dinv", [NH, 1], F32, m2)
        pgid = sb("pgid", [1, NPG], I32, m2)
        pgcol = sb("pgcol", [P, 2], I32, m2)
        m2.close()

        m3 = ExitStack()
        m3t = ExitStack()
        SQ = sb("SQ", [P, KC, TP], F32, m3t)
        MF = sb("MF", [P, KC, TP], F32, m3t)
        m3t.close()
        MH = sb("MH", [P, KC, TP], F32R, m3)
        ML = sb("ML", [P, KC, TP], F32R, m3)
        VR = sb("VR", [P, 2, KC, P], F32, m3)
        VH = sb("VH", [P, 2, KC, P], F32R, m3)
        VL = sb("VL", [P, 2, KC, P], F32R, m3)
        XS = sb("XS", [P, NB, BW], F32, m3)
        m3a = ExitStack()
        NR = sb("NR", [P, 3, KC, HB], F32, m3a)
        NZ = sb("NZ", [P, 2, 2, HB], F32, m3a)
        NG = sb("NG", [P, 2, 2, HB], F32, m3a)
        m3a.close()
        GP = sb("GP", [P, 2, TP + 2], F32, m3)
        GC = sb("GC", [P, 2, BW], F32, m3)
        GO = sb("GO", [P, 2, BW], F32, m3)
        TT = sb("TT", [TAIL, 2, P], F32, m3)
        m3.close()

        m4 = ExitStack()
        GH = sb("GH", [P, RING, 2, BW], F32R, m4)
        GL = sb("GL", [P, RING, 2, BW], F32R, m4)
        GR = sb("GR", [P, 3, 2, BW], F32, m4)
        DR = sb("DR", [P, 2, FH, P], F32, m4)
        DH = sb("DH", [P, 2, FH, P], F32R, m4)
        DL = sb("DL", [P, 2, FH, P], F32R, m4)
        YX = sb("YX", [P, 2, BW], F32, m4)
        YT = sb("YT", [P, 4, DM], F32, m4)
        ysq = sb("ysq", [P, DM], F32, m4)
        yr = sb("yr", [P, 4], F32, m4)
        gfin = sb("gfin", [P, DM], F32, m4)
        m4.close()

        PS = ctx.enter_context(nc.psum_tensor("PS", [P, 8, 512], F32))

        c_ld = sem("c_ld")
        c_pool = sem("c_pool")
        c_gw = sem("c_gw")
        x_first = sem("x_first")
        x_ld = [sem("x_ld0"), sem("x_ld1")]
        x_pad = sem("x_pad")
        x_last = sem("x_last")
        x_sq = sem("x_sq")
        x_hn = sem("x_hn")
        x_tp = sem("x_tp")
        x_ev = sem("x_ev")
        x_lo = sem("x_lo")
        x_st = [sem("x_st0"), sem("x_st1")]
        a0 = sem("a0")
        d0 = sem("d0")
        w_ld = [sem("w_ld0"), sem("w_ld1")]
        w_hi = sem("w_hi")
        w_lo = sem("w_lo")
        g_mm = sem("g_mm")
        g_ev = sem("g_ev")
        z_st = [sem(f"z_st{j}") for j in range(NB)]
        t_pe = sem("t_pe")
        t_ev = sem("t_ev")
        t_st = [sem("t_st0"), sem("t_st1")]
        l_ax = sem("l_ax")
        l_ex = sem("l_ex")
        f_tp = sem("f_tp")
        f_dv = sem("f_dv")
        f_st = sem("f_st")
        dv = sem("dv")
        r_ld = sem("r_ld")
        r_gw = sem("r_gw")
        r_gl = sem("r_gl")
        r_st = sem("r_st")
        r_ho = sem("r_ho")
        r_conv = sem("r_conv")
        r_gate = sem("r_gate")
        r_act = sem("r_act")
        r_u = sem("r_u")
        r_sc = sem("r_sc")
        r_y = sem("r_y")
        r_h = sem("r_h")
        f_ev = sem("f_ev")
        go = sem("go")
        phase_end = sem("phase_end")
        c_att = sem("c_att")
        c_att2 = sem("c_att2")
        pg_ld = sem("pg_ld")
        lf_ld = sem("lf_ld")
        lf_tp = sem("lf_tp")
        lf_ev = sem("lf_ev")
        lf_dv = sem("lf_dv")
        cb_ok = sem("cb_ok")
        st_ld = sem("st_ld")
        va_ld = [sem("va_ld0"), sem("va_ld1")]
        prep = sem("prep")
        mm_mx = sem("mm_mx")
        mx = sem("mx")
        nm = sem("nm")
        nt = sem("nt")
        na = sem("na")
        sT = sem("sT")
        ex = sem("ex")
        pv = sem("pv")
        rd = sem("rd")
        on = sem("on")
        ao_st = [sem("ao_st0"), sem("ao_st1")]
        kg_ld = [sem(f"kg_ld{s}") for s in range(4)]
        vg_ld = [sem(f"vg_ld{s}") for s in range(4)]
        nw_ld = sem("nw_ld")
        kp = sem("kp")
        kd = sem("kd")
        kf = sem("kf")
        mr = sem("mr")
        de = sem("de")
        dn = sem("dn")
        vd = sem("vd")
        df = sem("df")
        od_s = sem("od_s")
        av = sem("av")
        at_s = sem("at_s")
        kq = sem("kq")
        lf_pg = sem("lf_pg")
        nr_ld = [sem(f"nr_ld{s}") for s in range(3)]
        na_s = sem("na_s")
        nsq = sem("nsq")
        nrd = sem("nrd")
        nmm = sem("nmm")
        nrs = sem("nrs")
        nrc = sem("nrc")
        nst = sem("nst")
        nhi = sem("nhi")
        nlo = sem("nlo")
        v_ld = [sem("v_ld0"), sem("v_ld1")]
        v_hi = sem("v_hi")
        v_lo = sem("v_lo")
        u_mm = sem("u_mm")
        u_ev = sem("u_ev")
        xs_ld = [sem(f"xs_ld{j}") for j in range(NB)]
        xs_st = [sem(f"xs_st{j}") for j in range(NB)]
        gcv = sem("gcv")
        gge = sem("gge")
        go_st = [sem("go_st0"), sem("go_st1")]
        tt_pe = sem("tt_pe")
        tt_ev = sem("tt_ev")
        tt_st = [sem("tt_st0"), sem("tt_st1")]
        nf_ld = sem("nf_ld")
        dr_ld = [sem("dr_ld0"), sem("dr_ld1")]
        d_hi = sem("d_hi")
        d_lo = sem("d_lo")
        dk = sem("dk")
        gr_ld = [sem(f"gr_ld{s}") for s in range(3)]
        gg_hi = sem("gg_hi")
        gg_lo = sem("gg_lo")
        yx_ld = [sem("yx_ld0"), sem("yx_ld1")]
        y_ev = sem("y_ev")
        y_tp = sem("y_tp")
        y_tk = sem("y_tk")
        y_sq = sem("y_sq")
        y_rc = sem("y_rc")
        y_nm = sem("y_nm")
        y_st = sem("y_st")

        block = ctx.enter_context(nc.Block())
        @block.sync
        def _(e):
            e.dma_start(xin[0:NMETA, 0], a["meta_tokens"]).then_inc(x_first, 16)
            e.dma_start(xin[NMETA:P, 0], a["x_prompt"][0][0:P - NMETA, :]).then_inc(x_ld[0], 16)
            e.dma_start(xin[:, 1], a["x_prompt"][0][P - NMETA:2 * P - NMETA, :]).then_inc(x_ld[1], 16)
            with e.Fori(0, 7) as i:
                for v in range(2):
                    e.wait_ge(x_tp, 2 * i + v + 1)
                    e.dma_start(xin[:, v], a["x_prompt"][0][bass.ds((2 * i + 2 + v) * P - NMETA, P), :])\
                        .then_inc(x_ld[v], 16)
            e.wait_ge(x_pad, 1)
            e.dma_start(xin[0:NMETA, 0], a["x_prompt"][0][SEQ - NMETA:SEQ, :]).then_inc(x_ld[0], 16)
            e.dma_start(xin[NMETA:NMETA + NS, 0], a["x_sample"][:, 0, :]).then_inc(x_last, 16)

            e.wait_ge(x_tp, NT)
            e.wait_ge(x_ev, 2 * NT)
            e.wait_ge(x_lo, NT)
            for u in range(2):
                e.wait_ge(x_st[u], 16 * ((NT + 1 - u) // 2))
            for u in range(2):
                e.dma_start(WR[:, u], a["w_stream"][u]).then_inc(w_ld[u], 16)
            with e.Fori(1, 10) as i:
                for u in range(2):
                    e.wait_ge(w_lo, 2 * i + u - 1)
                    e.dma_start(WR[:, u], a["w_stream"][2 * i + u]).then_inc(w_ld[u], 16)
            e.wait_ge(w_lo, NIN - 2)
            e.dma_start(WR[:, 0], a["w_stream"][NIN - 1]).then_inc(w_ld[0], 16)
            def fetch_head(h):
                e.dma_start(Qst[0:HD], qT[bass.ds(h * HD, HD), :]).then_inc(st_ld, 16)
                e.dma_start(Qst[HD:P], qT[bass.ds(h * HD, HD), :]).then_inc(st_ld, 16)
                e.dma_start(Kst[0:HD], kT[bass.ds(h * HD, HD), :]).then_inc(st_ld, 16)
                e.dma_start(Kst[HD + 2:HD + 4], decayT[:, h, :] if isinstance(h, int) else
                            decayT[:, bass.ds(h, 1), :].rearrange("a o n -> (a o) n")).then_inc(st_ld, 16)
                e.dma_start(Kst2[0:HD], kT[bass.ds(h * HD, HD), :]).then_inc(st_ld, 16)
                e.dma_start(Kst2[HD:P], kT[bass.ds(h * HD, HD), :]).then_inc(st_ld, 16)

            vrows = out["v_prompt"][0, 0].rearrange("t h d -> t (h d)")

            def fetch_values(h, v):
                e.dma_start(VA[:, v, 0:16, 0:HD], vrows[0:SEQ, bass.ds(h * HD, HD)].rearrange("(t p) d -> p t d", p=P))\
                    .then_inc(va_ld[v], 16)
                e.dma_start(VA[0:NMETA, v, 16, 0:HD], vrows[SEQ:TPR, bass.ds(h * HD, HD)]).then_inc(va_ld[v], 16)

            def fetch_new(s, v):
                one = bass.ds(s, 1)
                e.dma_start(qb[:, v], qrow[one, :].rearrange("o n -> (o n)").partition_broadcast(P)).then_inc(nw_ld, 16)
                e.dma_start(knb[:, v], out["k_sample"][0][one, 0].rearrange("o h d -> (o h d)").partition_broadcast(P))\
                    .then_inc(nw_ld, 16)
                e.dma_start(vnew[:, v], out["v_sample"][0][one, 0].rearrange("o h d -> o (h d)")).then_inc(nw_ld, 16)

            def fetch_pages(cache, dst, done, s, g):
                for m in range(2):
                    page = e.value_load(pgid[0:1, bass.ds(s * PAGES + 2 * g + m, 1)], min_val=0, max_val=npool - 1)
                    e.dma_start(dst[:, g % 4, m], cache[0][bass.ds(page, 1)].rearrange("o p h d -> (o p) (h d)"))\
                        .then_inc(done[g % 4], 16)

            def sync_head(ii, u, nxt):
                i = 2 * ii + u
                if nxt:
                    e.wait_ge(prep, 7 * i + 7)
                    e.sem_inc(go, 1)
                    fetch_head(i + 1)
                    e.wait_ge(pv, 51 * i)
                    e.sem_inc(go, 1)
                    fetch_values(i + 1, 1 - u)
                    e.wait_ge(kf, 4 * i)
                    e.wait_ge(df, i)
                    e.sem_inc(go, 1)
                    fetch_new(i + 1, 1 - u)
                for g in range(PAGES // 2):
                    e.wait_ge(vd, 16 * i + g)
                    e.sem_inc(go, 1)
                    fetch_pages(a["cache_v"], Vpg, vg_ld, i, g)
                    if nxt:
                        e.wait_ge(kd, 16 * i + 16 + g - 3)
                        e.sem_inc(go, 1)
                        fetch_pages(a["cache_k"], Kpg, kg_ld, i + 1, g)

            e.wait_ge(phase_end, 4)
            e.wait_ge(c_att2, 2)
            e.dma_start(pgid[:], a["page_table"]).then_inc(pg_ld, 16)
            e.dma_start(pgcol[:], a["page_column"]).then_inc(pg_ld, 16)
            e.dma_start(cnew[:].rearrange("p s h -> p (s h)"),
                        out["logf_sample"][0, :, 0].rearrange("s h -> (s h)").partition_broadcast(P)).then_inc(lf_ld, 16)
            fetch_head(0)
            e.wait_ge(c_att, 1)
            fetch_values(0, 0)
            fetch_new(0, 0)
            e.sem_inc(vd, 3)
            e.wait_ge(pg_ld, 32)
            e.wait_ge(cb_ok, 1)
            for g in range(PAGES // 2):
                if g >= 4:
                    e.wait_ge(kd, g - 3)
                fetch_pages(a["cache_k"], Kpg, kg_ld, 0, g)
            with e.Fori(0, 3) as ii:
                for u in range(2):
                    sync_head(ii, u, True)
            sync_head(3, 0, True)
            sync_head(3, 1, False)
            e.wait_ge(phase_end, 8)

            def fetch_v(m, u):
                src = a["w_out"][m] if m < 8 else a["w_up"][(m - 8) // 2, m % 2]
                e.dma_start(VR[:, u], src).then_inc(v_ld[u], 16)

            def fetch_norm(n):
                b, s = n % 10, n % 3
                if n >= 3:
                    e.wait_ge(nst, n - 2)
                src = (x2T if n >= 10 else mixT).rearrange("(k p) n -> p k n", p=P)
                if n >= 10:
                    e.wait_ge(xs_st[b // 2], 16 * KC)
                if n == 9:
                    e.dma_start(NR[:, s, 0:4, 0:TPR - 9 * HB], src[:, 0:4, 9 * HB:TPR]).then_inc(nr_ld[s], 16)
                    e.dma_start(NR[:, s, 4:8], src[:, 4:8, 9 * HB:TP]).then_inc(nr_ld[s], 16)
                else:
                    e.dma_start(NR[:, s], src[:, :, cols(b, HB)]).then_inc(nr_ld[s], 16)

            def fetch_residual(m):
                for j in range(NB):
                    e.wait_ge(xs_st[j], 16 * m)
                    e.dma_start(XS[:, j], xT[bass.ds(m * P, P), cols(j)]).then_inc(xs_ld[j], 16)

            fetch_norm(0)
            fetch_norm(1)
            for m in range(2):
                fetch_v(m, m)
            fetch_norm(2)
            for j in range(NB):
                e.dma_start(XS[:, j], xT[0:P, cols(j)]).then_inc(xs_ld[j], 16)
            for n in range(3, 10):
                fetch_norm(n)
            with e.Fori(0, 3) as i:
                for u in range(2):
                    e.wait_ge(v_lo, 2 * i + u + 1)
                    e.dma_start(VR[:, u], a["w_out"][2 * i + u + 2]).then_inc(v_ld[u], 16)
                    fetch_residual(2 * i + u + 1)
            e.wait_ge(v_lo, 7)
            fetch_v(8, 0)
            fetch_residual(7)
            e.wait_ge(v_lo, 8)
            fetch_v(9, 1)
            for n in range(10, 20):
                fetch_norm(n)
            with e.Fori(1, FC) as f:
                for u in range(2):
                    e.wait_ge(v_lo, 2 * f + 7 + u)
                    e.dma_start(VR[:, u], a["w_up"][f, u]).then_inc(v_ld[u], 16)
            e.wait_ge(phase_end, 12)

            def fetch_down(n, oc, h):
                if not (isinstance(n, int) and n < 2):
                    e.wait_ge(d_lo, n - 1)
                e.dma_start(DR[:, h], a["w_down"][oc, h]).then_inc(dr_ld[h], 16)

            def fetch_inner(j, q):
                f = FH * j + q
                if f >= 3:
                    e.wait_ge(gg_lo, f - 2)
                e.dma_start(GR[:, f % 3], gT[2 * q * P:(2 * q + 2) * P, cols(j)].rearrange("(k p) n -> p k n", p=P))\
                    .then_inc(gr_ld[f % 3], 16)

            def fetch_x2(n, oc, j, v):
                if not (isinstance(n, int) and n < 2):
                    e.wait_ge(y_tp, n - 1)
                e.dma_start(YX[:, v], x2T[bass.ds(oc * P, P), cols(j)]).then_inc(yx_ld[v], 16)

            fetch_inner(0, 0)
            fetch_down(0, 0, 0)
            for q in range(1, 3):
                fetch_inner(0, q)
            fetch_down(1, 0, 1)
            fetch_x2(0, 0, 0, 0)
            e.dma_start(gfin[:], a["norm_final"][0].partition_broadcast(P)).then_inc(nf_ld, 16)
            for q in range(3, FH):
                fetch_inner(0, q)
            for j in range(NB):
                def sync_pair(i, last=False):
                    n, oc = 16 * j + 4 * i, 2 * i
                    ahead = not (last and j == NB - 1)
                    fills = {0: (0, 1, 2), 1: (3, 4), 2: (5, 6, 7, 8, 9), 3: (10,)}
                    for c in range(4):
                        if c < 2:
                            fetch_down(n + c + 2, oc + 1, c)
                        elif ahead:
                            fetch_down(n + c + 2, 0 if last else oc + 2, c - 2)
                        if c == 1:
                            fetch_x2(8 * j + oc + 1, oc + 1, j, 1)
                        if c == 3 and ahead:
                            fetch_x2(8 * j + oc + 2, 0 if last else oc + 2, j + 1 if last else j, 0)
                        if last and ahead:
                            for q in fills[c]:
                                fetch_inner(j + 1, q)

                with e.Fori(0, 3) as i:
                    sync_pair(i)
                sync_pair(3, True)

        @block.gpsimd
        def _(e):
            pool = Steps(e, c_pool)
            for m in (identF, identB, maskQ, maskK, onesF, triu):
                pool.inc(e.memset(m[:], 1.0 if m in (onesF, triu) else 0.0))
            pool.inc(e.memset(epsT[:], EPS))
            pool.inc(e.memset(rh0[:], 0.0))
            pool.inc(e.memset(attS[:], 0.0))
            pool.settle()
            for m in (identF, identB):
                pool.inc(e.affine_select(out=m[:], in_=m[:], compare_op=ALU.not_equal, fill=1.0, base=0,
                                         pattern=[[-1, P]], channel_multiplier=1))
            pool.inc(e.affine_select(out=maskQ[:], in_=maskQ[:], compare_op=ALU.is_ge, fill=BIG, base=0,
                                     pattern=[[-1, P]], channel_multiplier=1))
            pool.inc(e.affine_select(out=maskK[:], in_=maskK[:], compare_op=ALU.is_ge, fill=BIG, base=0,
                                     pattern=[[1, P]], channel_multiplier=-1))
            pool.inc(e.affine_select(out=triu[:], in_=triu[:], compare_op=ALU.is_ge, fill=0.0, base=0,
                                     pattern=[[1, P]], channel_multiplier=-1))
            e.wait_ge(x_tp, 15)
            e.memset(xin[0:TAIL, 0], 0.0).then_inc(x_pad, 1)

            e.wait_ge(x_hn, NT)
            e.wait_ge(x_lo, NT)
            e.wait_ge(x_ev, 2 * NT)
            e.wait_ge(x_st[0], 16 * 9)
            e.wait_ge(x_st[1], 16 * 8)
            e.memset(gw[:], 0.0).then_inc(c_gw, 1)

            def split_w(n, use, u):
                e.wait_ge(w_ld[u], 16 * use + 16)
                if not (isinstance(n, int) and n < 2):
                    e.wait_ge(g_mm, 5 * n - 5)
                e.sem_inc(go, 1)
                e.tensor_copy(WH[:, u], WR[:, u]).then_inc(w_hi, 1)
                e.wait_ge(w_hi, n + 1)
                e.tensor_tensor(WL[:, u], WR[:, u], WH[:, u].bitcast(F32), ALU.subtract).then_inc(w_lo, 1)

            split_w(0, 0, 0)
            split_w(1, 0, 1)
            with e.Fori(1, 10) as i:
                for u in range(2):
                    split_w(2 * i + u, i, u)
            split_w(NIN - 1, 10, 0)
            e.wait_ge(w_lo, NIN)
            e.sem_inc(phase_end, 1)
            e.wait_ge(phase_end, 4)
            e.memset(QA[HD:HD + 4].bitcast(F32), 1.0).then_inc(c_att2, 1)
            e.memset(Kst[HD:HD + 4], 1.0).then_inc(c_att2, 1)
            e.memset(headmask[:], 1.0).then_inc(c_att2, 1)
            e.wait_ge(pg_ld, 32)
            for g in range(2):
                e.indirect_dma_start(out=lpage[:, g], out_offset=None,
                                     in_=a["cache_logf"][0].rearrange("n p h -> n (p h)"),
                                     in_offset=bass.IndirectOffsetOnAxis(ap=pgcol[:, g:g + 1], axis=0))\
                    .then_inc(lf_pg, 16)
            e.wait_ge(c_att2, 3)
            e.affine_select(out=headmask[:], in_=headmask[:], compare_op=ALU.is_ge, fill=0.0, base=0,
                            pattern=[[1, DATT]], channel_multiplier=-HD).then_inc(c_att2, 1)
            e.wait_ge(c_att2, 4)
            e.affine_select(out=headmask[:], in_=headmask[:], compare_op=ALU.is_ge, fill=0.0, base=HD - 1,
                            pattern=[[-1, DATT]], channel_multiplier=HD).then_inc(c_att2, 1)

            def prepare(i, v):
                e.wait_ge(st_ld, 96 * i + 96)
                e.wait_ge(mr, i)
                e.sem_inc(go, 1)
                own = 7 * i
                e.memset(QA[HD:HD + 2, v].bitcast(F32), 0.0).then_inc(prep, 1)
                for n, (dst, src) in enumerate(((KA[0:HD + 4, v], Kst[0:HD + 4]), (QA[0:HD, v], Qst[0:HD]),
                                                (QB[:, v], Qst[:]), (KB[:, v], Kst2[:]))):
                    e.wait_ge(prep, own + n + 1)
                    e.sem_inc(go, 1)
                    e.tensor_copy(dst, src).then_inc(prep, 1)
                e.wait_ge(prep, own + 5)
                e.tensor_tensor(QB[0:HD, v], Qst[0:HD], QB[0:HD, v].bitcast(F32), ALU.subtract).then_inc(prep, 1)
                e.wait_ge(prep, own + 6)
                e.tensor_tensor(KB[HD:P, v], Kst2[HD:P], KB[HD:P, v].bitcast(F32), ALU.subtract).then_inc(prep, 1)

            def sample_max(s, v):
                e.wait_ge(kf, 4 * s + 3)
                e.wait_ge(prep, 7 * s + 7)
                e.sem_inc(go, 1)
                e.partition_all_reduce(mall[:, v], mloc[:, v], P, bass.bass_isa.ReduceOp.max).then_inc(mr, 1)

            e.wait_ge(lf_pg, 32)
            prepare(0, 0)
            sample_max(0, 0)

            def pool_head(ii, u, nxt):
                i = 2 * ii + u
                if nxt:
                    e.wait_ge(pv, 51 * i)
                    prepare(i + 1, 1 - u)
                    sample_max(i + 1, 1 - u)

            with e.Fori(0, 3) as ii:
                for u in range(2):
                    pool_head(ii, u, True)
            pool_head(3, 0, True)
            e.wait_ge(mr, NS)
            e.wait_ge(prep, 7 * NH)
            e.sem_inc(phase_end, 1)
            e.wait_ge(phase_end, 8)

            def split_v(m, u):
                e.wait_ge(v_ld[u], 16 * (m // 2) + 16 if isinstance(m, int) else 8 * (m - u) + 16)
                if not (isinstance(m, int) and m < 2):
                    e.wait_ge(u_mm, 5 * m - 5)
                e.sem_inc(go, 1)
                e.tensor_copy(VH[:, u], VR[:, u]).then_inc(v_hi, 1)
                e.wait_ge(v_hi, m + 1)
                e.tensor_tensor(VL[:, u], VR[:, u], VH[:, u].bitcast(F32), ALU.subtract).then_inc(v_lo, 1)

            def norm_low(n):
                c = cols(n % 10, HB)
                e.wait_ge(nhi, n + 1)
                e.tensor_tensor(ML[:, :, c], MF[:, :, c], MH[:, :, c].bitcast(F32), ALU.subtract)\
                    .then_inc(nlo, 1)

            split_v(0, 0)
            split_v(1, 1)
            for n in range(10):
                norm_low(n)
            with e.Fori(1, 4) as i:
                for u in range(2):
                    split_v(2 * i + u, u)
            split_v(8, 0)
            for n in range(10, 20):
                norm_low(n)
            split_v(9, 1)
            with e.Fori(5, 26) as i:
                for u in range(2):
                    split_v(2 * i + u, u)
            e.wait_ge(nlo, 20)
            e.wait_ge(v_lo, 52)
            e.sem_inc(phase_end, 1)
            e.wait_ge(phase_end, 12)
            with e.Fori(0, 8 * NB) as i:
                for h in range(2):
                    e.wait_ge(d_hi, 2 * i + h + 1)
                    e.tensor_tensor(DL[:, h], DR[:, h], DH[:, h].bitcast(F32), ALU.subtract).then_inc(d_lo, 1)
                    e.wait_ge(d_lo, 2 * i + h + 1)

        @block.scalar
        def _(e):
            for dst, src in (
                (gmix[:], a["norm_mix"][0].partition_broadcast(P)), (gains[:], a["gains"]),
                (rtab[:], a["rnn_table"]), (rstate[:], a["rnn_state"]), (ftab[:], a["ffn_table"]),
                (fstate[:], a["ffn_state"]), (bf[:], a["b_forget"].rearrange("a h -> h a")),
            ):
                e.dma_start(dst, src).then_inc(c_ld, 16)
            e.wait_ge(c_pool, 9)
            e.dma_start(rh0[:, :, 0:NS], a["rnn_h"]).then_inc(c_ld, 16)

            act0 = Steps(e, a0)

            def mean_square(t, u, n, rows=P):
                e.wait_ge(x_ld[u], n)
                act0.inc(e.activation(sqj[0:rows], xin[0:rows, u], ACT.Square, accum_out=st0[0:rows, u, 0:1]))
                act0.settle()
                e.activation(st0[0:rows, u, 1:2], st0[0:rows, u, 0:1], ACT.Sqrt, bias=epsT[0:rows],
                             scale=1.0 / DM).then_inc(x_sq, 1)

            def empty(t, u, st, rows=P):
                e.wait_ge(x_tp, t + 1)
                e.wait_ge(x_st[u], st)
                raw = PS[:, 4 * u:4 * u + 2, :].rearrange("p a (k n) -> p (a k) n", n=P)
                nrm = PS[:, 4 * u + 2:4 * u + 4, :].rearrange("p a (k n) -> p (a k) n", n=P)
                e.activation(xst[:, u, :, 0:rows], raw[:, :, 0:rows], ACT.Copy).then_inc(x_ev, 1)
                e.activation(XH[:, :, bass.ds(t * P, rows)], nrm[:, :, 0:rows], ACT.Copy).then_inc(x_ev, 1)
                e.wait_ge(x_ev, 2 * t + 1)
                e.dma_start(xT.rearrange("(k p) n -> p k n", p=P)[:, :, bass.ds(t * P, rows)],
                            xst[:, u, :, 0:rows]).then_inc(x_st[u], 16)

            e.wait_ge(c_pool, 13)
            e.wait_ge(x_first, 16)
            mean_square(0, 0, 16)
            mean_square(1, 1, 16)
            empty(0, 0, 0)
            with e.Fori(0, 7) as i:
                act0.start(i, 2)
                for v in range(2):
                    e.wait_ge(x_hn, 2 * i + v + 1)
                    mean_square(2 * i + 2 + v, v, 16 * i + 32)
                    empty(2 * i + 1 + v, 1 - v, 16 * (i + v))
                act0.stop(7)
            e.wait_ge(x_last, 16)
            e.wait_ge(x_hn, 15)
            mean_square(16, 0, 16 * 9, TAIL)
            empty(15, 1, 16 * 7)
            empty(16, 0, 16 * 8, TAIL)
            e.wait_ge(l_ax, 1)
            e.activation(sp[:, :, 2], sp[:, :, 1], ACT.Exp, scale=-1.0).then_inc(l_ex, 1)

            def store_block(n, j, dst, done):
                e.wait_ge(g_ev, 5 * n + j + 6)
                e.dma_start(dst[:, cols(j)], ZS[:, j]).then_inc(done[j], 16)

            def take_tail(ev, slot, stored):
                e.wait_ge(t_pe, ev + 1)
                e.wait_ge(t_st[slot], stored)
                e.activation(TS[0:TAIL, slot, 0], PS[0:TAIL, 5, 0:P], ACT.Copy).then_inc(t_ev, 1)
                e.wait_ge(t_ev, ev + 1)

            with e.Fori(0, 4) as c:
                for j in range(NB):
                    store_block(2 * c, j, xrT[bass.ds(c * P, P), :], z_st)
                take_tail(c, 0, 32 * c)
                e.dma_start(out["rnn_conv_prompt"][0, 0][:, bass.ds(c * P, P)],
                            TS[NMETA - 3:NMETA, 0, 0]).then_inc(t_st[0], 16)
                e.dma_start(out["rnn_conv_sample"][0][:, 2, bass.ds(c * P, P)],
                            TS[NMETA:NMETA + NS, 0, 0]).then_inc(t_st[0], 16)
                for j in range(NB):
                    store_block(2 * c + 1, j, grT[bass.ds(c * P, P), :], z_st)
            e.dma_start(out["rnn_conv_sample"][0][:, 0:2, :], a["state_rnn_conv"][0][:, 1:3, :]).then_inc(f_st, 16)

            e.wait_ge(l_ax, 2)
            e.activation(FE[:], FE[:], ACT.Exp, scale=-1.0).then_inc(l_ex, 1)
            e.wait_ge(f_dv, 2)
            lp = out["logf_prompt"][0, 0]
            e.dma_start(lp[0:SEQ, :].rearrange("(t p) h -> p t h", p=P), FL[:, 0:16]).then_inc(f_st, 16)
            e.dma_start(lp[SEQ:TPR, :], FL[0:NMETA, 16]).then_inc(f_st, 16)
            e.dma_start(out["logf_sample"][0, :, 0, :], FL[NMETA:NMETA + NS, 16]).then_inc(f_st, 16)
            e.wait_ge(f_dv, 4)
            e.dma_start(decayT.rearrange("a h n -> (a h) n"), RX[0:16, 3:3 + TP]).then_inc(f_st, 16)
            e.wait_ge(f_st, 80)

            for s in z_st:
                e.wait_ge(s, 16 * 8)
            full_k = [out["k_prompt"][0, 0].rearrange("t h d -> t (h d)"), out["v_prompt"][0, 0].rearrange("t h d -> t (h d)")]
            one_k = [out["k_sample"][0, :, 0].rearrange("s h d -> s (h d)"), out["v_sample"][0, :, 0].rearrange("s h d -> s (h d)")]

            def take_rows(ev, slot, stored, j, kv, c):
                e.wait_ge(t_pe, ev + 1)
                e.wait_ge(t_st[slot], stored)
                e.activation(TS[:, slot, 0:3], PS[:, 5, 0:3 * P].rearrange("p (m n) -> p m n", n=P), ACT.Copy)
                e.activation(TS[0:TAIL, slot, 3], PS[0:TAIL, 5, 3 * P:4 * P], ACT.Copy).then_inc(t_ev, 1)
                e.wait_ge(t_ev, ev + 1)
                rows, f = full_k[kv], bass.ds(c * P, P)
                e.dma_start(rows[j * BW:j * BW + 3 * P, f].rearrange("(m p) n -> p m n", p=P),
                            TS[:, slot, 0:3]).then_inc(t_st[slot], 16)
                r0 = j * BW + 3 * P
                n = min(TAIL, TPR - r0)
                e.dma_start(rows[r0:r0 + n, f], TS[0:n, slot, 3]).then_inc(t_st[slot], 16)
                if j == NB - 1:
                    e.dma_start(one_k[kv][:, f], TS[NMETA:NMETA + NS, slot, 3]).then_inc(t_st[slot], 16)

            with e.Fori(0, 2) as i:
                plan = []
                count = [0, 0]
                for v in range(22):
                    m = v % 11
                    plan.append((v % 2, count[v % 2]))
                    count[v % 2] += 16 * (1 if m == 0 else 3 if m in (5, 10) else 2)
                for u in range(2):
                    c = 2 * i + u
                    n = 9 + 3 * c
                    e.wait_ge(r_st, 16 * c)
                    e.dma_start(RX[:, 3:3 + TP], xrT[bass.ds(c * P, P), :]).then_inc(r_ld, 16)
                    e.wait_ge(r_gate, 5 * c)
                    e.wait_ge(c_gw, 1)
                    for g, w in enumerate((a["w_rg_a"], a["w_rg_x"])):
                        for b in range(2):
                            e.dma_start(gw[64 * b:64 * b + 64, g, 64 * b:64 * b + 64], w[0][2 * c + b])\
                                .then_inc(r_gw, 16)

                    def event(m):
                        slot, before = plan[11 * u + m]
                        return 4 + 22 * i + 11 * u + m, slot, (128 if slot == 0 else 0) + count[slot] * i + before

                    for j in range(NB):
                        store_block(n, j, qT[bass.ds(c * P, P), :], z_st)
                    take_tail(*event(0))
                    slot = event(0)[1]
                    e.dma_start(qrow[:, bass.ds(c * P, P)], TS[NMETA:NMETA + NS, slot, 0]).then_inc(t_st[slot], 16)
                    for j in range(NB):
                        store_block(n + 1, j, kT[bass.ds(c * P, P), :], z_st)
                        e.wait_ge(r_gate, 5 * c + j + 1)
                        if j:
                            e.wait_ge(r_u, 5 * c + j)
                        e.sem_inc(go, 1)
                        e.activation(RT[:, 0], PS[:, 7, 0:BW], ACT.Tanh, bias=hb[:, bass.ds(c, 1), 1], scale=0.5)\
                            .then_inc(r_act, 1)
                        e.activation(RT[:, 1], PS[:, 6, 0:BW], ACT.Tanh, bias=hb[:, bass.ds(c, 1), 0], scale=0.5)\
                            .then_inc(r_act, 1)
                        e.wait_ge(r_act, 17 * c + 3 * j + 2)
                        if j == 0:
                            e.wait_ge(r_ho, 32 * c)
                            e.wait_ge(r_y, c)
                        e.sem_inc(go, 1)
                        e.activation(RW[:, cols(j)], RT[:, 1], ACT.Tanh, bias=sp[:, bass.ds(c, 1), 0],
                                     scale=sp[:, bass.ds(c, 1), 0]).then_inc(r_act, 1)
                        take_rows(*event(1 + j), j, 0, c)
                    e.wait_ge(r_u, 5 * c + 5)
                    e.wait_ge(r_act, 17 * c + 15)
                    e.activation(RC[:], RW[:], ACT.Sqrt).then_inc(r_act, 1)
                    for j in range(NB):
                        take_rows(*event(6 + j), j, 1, c)
                        if j == 2:
                            e.wait_ge(r_sc, c + 1)
                            e.dma_start(RC[:], grT[bass.ds(c * P, P), :]).then_inc(r_gl, 16)
                            e.dma_start(out["rnn_h_prompt"][0].rearrange("o n -> n o")[bass.ds(c * P, P), :],
                                        RW[:, TPR - 1:TPR]).then_inc(r_ho, 16)
                            e.dma_start(out["rnn_h_sample"][0].rearrange("s n -> n s")[bass.ds(c * P, P), :],
                                        RW[:, TPR:TPR + NS], allow_slow_non_contiguous=True).then_inc(r_ho, 16)
                        if j == 3:
                            e.wait_ge(r_gl, 16 * c + 16)
                            e.activation(RC[:], RC[:], ACT.Gelu_apprx_tanh).then_inc(r_act, 1)
                    e.wait_ge(r_y, c + 1)
                    e.dma_start(mixT[bass.ds(DATT + c * P, P), :], RX[:, 3:3 + TP]).then_inc(r_st, 16)
            e.wait_ge(t_st[0], 864)
            e.wait_ge(t_st[1], 736)
            e.wait_ge(r_st, 64)
            e.wait_ge(r_ho, 128)
            for s in z_st:
                e.wait_ge(s, 256)
            e.wait_ge(r_act, 17 * 4)
            e.wait_ge(t_ev, 48)
            e.sem_inc(phase_end, 1)
            e.wait_ge(phase_end, 4)
            e.sem_inc(ex, 4)
            for g in range(2):
                for b in range(2):
                    e.wait_ge(lf_tp, 4 * g + b + 1)
                    e.activation(xtp[:, 512 * b:512 * b + 512], PS[:, b, :], ACT.Copy).then_inc(lf_ev, 1)
                for b in range(2):
                    e.wait_ge(lf_tp, 4 * g + b + 3)
                    for m, dst in ((0, cwith), (1, ctot)):
                        view = dst.rearrange("p (h s) -> p h s", h=NH)
                        ins = e.activation(view[:, 4 * b:4 * b + 4, P * g:P * g + P],
                                           PS[:, 2 + 2 * b + m, :].rearrange("p (h s) -> p h s", h=4), ACT.Copy)
                    ins.then_inc(lf_ev, 1)

            def sample_exp(s, v):
                e.wait_ge(kf, 4 * s + 4)
                e.sem_inc(go, 1)
                e.activation(sc[:, v], sc[:, v], ACT.Exp).then_inc(de, 1)
                e.activation(sn[:, v], sn[:, v], ACT.Exp).then_inc(de, 1)

            sample_exp(0, 0)

            def act_head(ii, u, nxt):
                i = 2 * ii + u
                for g in range(NB):
                    w = min(512, TP - 512 * g)
                    e.wait_ge(nt, 5 * i + g + 1)
                    e.activation(QA[HD:HD + 2, u, 512 * g:512 * g + w], PS[HD:HD + 2, 4 + g % 2, 0:w], ACT.Copy)\
                        .then_inc(na, 1)

                def store_out(j):
                    e.wait_ge(on, 5 * i + j + 6)
                    w = BW if j < NB - 1 else LASTP
                    e.dma_start(mixT[bass.ds(i * HD, HD), j * BW:j * BW + w], AO[0:HD, (u + j) % 2, 0:w])\
                        .then_inc(ao_st[(u + j) % 2], 16)

                for t, (j, kt, q0, n, kr) in enumerate(TILES):
                    e.wait_ge(sT, 51 * i + t + 1)
                    if t >= 3:
                        e.wait_ge(pv, 51 * i + t - 2)
                    e.activation(PT[0:kr, t % 3, 0:n], PS[0:kr, (45 + t) % 4, 0:n], ACT.Exp, scale=0.125).then_inc(ex, 1)
                    if kt == 0 and j > 1:
                        store_out(j - 2)
                store_out(3)
                store_out(4)
                if nxt:
                    sample_exp(i + 1, 1 - u)

            with e.Fori(0, 3) as ii:
                for u in range(2):
                    act_head(ii, u, True)
            act_head(3, 0, True)
            act_head(3, 1, False)
            e.wait_ge(ao_st[0], 16 * 20)
            e.wait_ge(ao_st[1], 16 * 20)
            e.wait_ge(na, 5 * NH)
            e.wait_ge(ex, 51 * NH + 4)
            e.wait_ge(de, 2 * NS)
            e.sem_inc(phase_end, 1)
            e.wait_ge(phase_end, 8)
            def norm_square(n):
                s = n % 3
                e.wait_ge(nr_ld[s], 16 * (n // 3 + 1) + (16 if s == 0 and n >= 9 else 0))
                if n == 9:
                    e.wait_ge(na_s, 1)
                e.activation(SQ[:, :, cols(n % 10, HB)], NR[:, s], ACT.Square).then_inc(nsq, 1)

            def norm_root(n):
                e.wait_ge(nmm, n + 1)
                if n >= 2:
                    e.wait_ge(nst, n - 1)
                parts = 2 if n < 10 else 1
                e.activation(NG[:, n % 2, 0:parts], PS[:, 5 + n % 2, 0:parts * HB].rearrange("p (a n) -> p a n", a=parts),
                             ACT.Sqrt, bias=epsT[:], scale=parts / DM).then_inc(nrs, 1)

            def norm_high(n):
                c = cols(n % 10, HB)
                e.wait_ge(nst, n + 1)
                e.activation(MH[:, :, c], MF[:, :, c], ACT.Copy).then_inc(nhi, 1)

            def store_sum(m, j):
                e.wait_ge(u_ev, 5 * m + j + 6)
                e.dma_start(x2T[bass.ds(m * P, P), cols(j)], XS[:, j]).then_inc(xs_st[j], 16)

            norm_square(0)
            norm_square(1)
            for n in range(10):
                norm_root(n)
                if n < 8:
                    norm_square(n + 2)
                norm_high(n)
            for j in range(NB):
                store_sum(0, j)
            with e.Fori(1, 7) as m:
                for j in range(NB):
                    store_sum(m, j)
            store_sum(7, 0)
            store_sum(7, 1)
            norm_square(10)
            norm_square(11)
            store_sum(7, 2)
            for n in range(10, 20):
                norm_root(n)
                if n < 18:
                    norm_square(n + 2)
                norm_high(n)
                if n < 12:
                    store_sum(7, n - 7)
            def act_up(i, u):
                f = 2 * i + u

                def store_inner(j):
                    e.wait_ge(u_ev, 5 * (9 + 2 * f) + j + 6)
                    e.dma_start(gT[bass.ds(f * P, P), cols(j)], GO[:, (u + j) % 2]).then_inc(go_st[(u + j) % 2], 16)

                for j in range(NB):
                    e.wait_ge(gcv, 5 * f + j + 1)
                    s = (u + j) % 2
                    e.activation(GC[:, s], GC[:, s], ACT.Gelu_apprx_tanh).then_inc(gge, 1)
                    if j == 1:
                        e.wait_ge(tt_pe, f + 1)
                        e.wait_ge(tt_st[u], 32 * i)
                        e.activation(TT[:, u], PS[0:TAIL, 7, 0:P], ACT.Copy).then_inc(tt_ev, 1)
                        e.wait_ge(tt_ev, f + 1)
                        e.dma_start(out["ffn_conv_prompt"][0, 0][:, bass.ds(f * P, P)], TT[NMETA - 2:NMETA, u])\
                            .then_inc(tt_st[u], 16)
                        e.dma_start(out["ffn_conv_sample"][0][:, 1, bass.ds(f * P, P)], TT[NMETA:NMETA + NS, u])\
                            .then_inc(tt_st[u], 16)
                    if j:
                        store_inner(j - 1)
                store_inner(NB - 1)

            e.dma_start(out["ffn_conv_sample"][0][:, 0, :], a["state_ffn_conv"][0][:, 1, :]).then_inc(f_st, 16)
            with e.Fori(0, FC // 2) as i:
                for u in range(2):
                    act_up(i, u)
            for s in go_st:
                e.wait_ge(s, 16 * NB * FC // 2)
            for s in tt_st:
                e.wait_ge(s, 16 * FC)
            e.wait_ge(f_st, 96)
            e.wait_ge(nhi, 20)
            e.sem_inc(phase_end, 1)
            e.wait_ge(phase_end, 12)
            rows_of = [(m * P, w) for m, w in ((0, P), (1, P), (2, P), (3, TAIL))]

            def split_down(n, h):
                e.wait_ge(dr_ld[h], 8 * (n - h) + 16)
                if not (isinstance(n, int) and n < 2):
                    e.wait_ge(dk, FH * (n - 1))
                e.activation(DH[:, h], DR[:, h], ACT.Copy).then_inc(d_hi, 1)

            def inner_high(j, q):
                f = FH * j + q
                e.wait_ge(gr_ld[f % 3], 16 * (f // 3) + 16)
                if f >= RING:
                    e.wait_ge(dk, 176 * (j - 1) + (FH * 14 + 2 * (q - 5) + 2 if q >= 5 else 0))
                e.activation(GH[:, f % RING], GR[:, f % 3], ACT.Copy).then_inc(gg_hi, 1)

            def take_sum(n, oc, v):
                e.wait_ge(y_tp, n + 1)
                e.sem_inc(go, 1)
                src = PS[:, 4 + v, :].rearrange("p (m n) -> p m n", n=P)
                e.activation(YT[:, 0:3, bass.ds(oc * P, P)], src[:, 0:3], ACT.Copy)
                e.activation(YT[0:TAIL, 3, bass.ds(oc * P, P)], src[0:TAIL, 3], ACT.Copy).then_inc(y_tk, 1)

            yst = Steps(e, y_sq)

            def final_root(j):
                e.wait_ge(y_tk, 8 * j + 8)
                if j:
                    e.wait_ge(y_nm, 4 * j)
                for m, (o, w) in enumerate(rows_of):
                    yst.inc(e.activation(ysq[0:w], YT[0:w, m], ACT.Square, accum_out=yr[0:w, m:m + 1]))
                    yst.settle()
                yst.inc(e.activation(yr[:, 0:3], yr[:, 0:3], ACT.Sqrt, bias=epsT[:], scale=1.0 / DM))
                yst.inc(e.activation(yr[0:TAIL, 3:4], yr[0:TAIL, 3:4], ACT.Sqrt, bias=epsT[0:TAIL], scale=1.0 / DM))

            def final_store(j):
                yp = out["y_prompt"][0]
                for m, (o, w) in enumerate(rows_of):
                    e.wait_ge(y_nm, 4 * j + m + 1)
                    t = j * BW + o - NMETA
                    lo = max(0, -t)
                    hi = min(w, SEQ - t)
                    e.dma_start(yp[t + lo:t + hi, :], YT[lo:hi, m]).then_inc(y_st, 16)
                    if hi < w:
                        e.dma_start(out["y_sample"][:, 0, :], YT[hi:hi + NS, m]).then_inc(y_st, 16)

            split_down(0, 0)
            for q in range(3):
                inner_high(0, q)
            split_down(1, 1)
            for q in range(3, FH):
                inner_high(0, q)
            for j in range(NB):
                def act_pair(i, first=False, last=False):
                    n, oc = 16 * j + 4 * i, 8 * j + 2 * i
                    fills = {0: (0, 1, 2), 1: (3, 4), 2: (5, 6, 7, 8, 9), 3: (10,)}
                    for c in range(4):
                        if not (j == NB - 1 and last and c == 3) and not (j == 0 and first and c == 0):
                            split_down(n + c + 1, (c + 1) % 2)
                        if c == 1 and not (first and j == 0):
                            take_sum(oc - 1, 7 if first else 2 * i - 1, 1)
                            if first:
                                final_root(j - 1)
                        if c == 2 and first and j:
                            final_store(j - 1)
                        if c == 3:
                            if first and j:
                                e.wait_ge(y_st, 64 * j)
                            take_sum(oc, 2 * i, 0)
                        if last and j < NB - 1:
                            for q in fills[c]:
                                inner_high(j + 1, q)

                act_pair(0, first=True)
                with e.Fori(1, 3) as i:
                    act_pair(i)
                act_pair(3, last=True)
            take_sum(8 * NB - 1, 7, 1)
            final_root(NB - 1)
            final_store(NB - 1)
            e.wait_ge(y_st, 64 * NB + 16)

        @block.vector
        def _(e):
            e.wait_ge(c_ld, 16 * 8)

            def normalise(t, u, rows=P):
                e.wait_ge(x_sq, t + 1)
                if not (isinstance(t, int) and t < 2):
                    e.wait_ge(x_tp, t - 1)
                e.reciprocal(st0[0:rows, u, 2:3], st0[0:rows, u, 1:2]).then_inc(d0, 1)
                e.wait_ge(d0, t + 1)
                e.scalar_tensor_tensor(out=hn[0:rows, u], in0=xin[0:rows, u], scalar=st0[0:rows, u, 2:3],
                                       in1=gmix[0:rows], op0=ALU.mult, op1=ALU.mult).then_inc(x_hn, 1)

            def low(t, u, rows=P):
                e.wait_ge(x_ev, 2 * t + 2)
                nrm = PS[:, 4 * u + 2:4 * u + 4, :].rearrange("p a (k n) -> p (a k) n", n=P)
                c = bass.ds(t * P, rows)
                e.tensor_tensor(XL[:, :, c], nrm[:, :, 0:rows], XH[:, :, c].bitcast(F32),
                                ALU.subtract).then_inc(x_lo, 1)

            normalise(0, 0)
            normalise(1, 1)
            low(0, 0)
            with e.Fori(0, 7) as i:
                for v in range(2):
                    normalise(2 * i + 2 + v, v)
                    low(2 * i + 1 + v, 1 - v)
            normalise(16, 0, TAIL)
            low(15, 1)
            low(16, 0, TAIL)
            g_steps = Steps(e, dv)

            def half_log1p(z, t, p):
                g_steps.inc(e.tensor_scalar(t, z, 2.0, None, ALU.add))
                g_steps.settle()
                g_steps.inc(e.reciprocal(t, t))
                g_steps.settle()
                g_steps.inc(e.tensor_tensor(z, z, t, ALU.mult))
                g_steps.settle()
                g_steps.inc(e.tensor_tensor(t, z, z, ALU.mult))
                g_steps.settle()
                g_steps.inc(e.tensor_scalar(p, t, 1.0 / 17, None, ALU.mult))
                for k in (15, 13, 11, 9, 7, 5, 3):
                    g_steps.settle()
                    g_steps.inc(e.scalar_tensor_tensor(out=p, in0=p, scalar=1.0 / k, in1=t, op0=ALU.add, op1=ALU.mult))
                g_steps.settle()
                g_steps.inc(e.scalar_tensor_tensor(out=p, in0=p, scalar=1.0, in1=z, op0=ALU.add, op1=ALU.mult))
                g_steps.settle()

            lam = rtab[:, :, 7]
            e.wait_ge(c_ld, 16 * 8)
            e.scalar_tensor_tensor(out=sp[:, :, 1], in0=lam, scalar=-1.0, in1=lam, op0=ALU.mult, op1=ALU.max)\
                .then_inc(l_ax, 1)
            g_steps.inc(e.tensor_scalar(hb[:], rtab[:, :, 5:7], 0.5, None, ALU.mult))
            e.wait_ge(l_ex, 1)
            half_log1p(sp[:, :, 2], sp[:, :, 3], sp[:, :, 4])
            g_steps.inc(e.tensor_scalar(sp[:, :, 5], lam, -2.0, 0.0, ALU.mult, ALU.max))
            g_steps.settle()
            g_steps.inc(e.scalar_tensor_tensor(out=sp[:, :, 0], in0=sp[:, :, 4], scalar=4.0, in1=sp[:, :, 5],
                                               op0=ALU.mult, op1=ALU.add))
            for u in range(2):
                e.wait_ge(x_st[u], 16 * (9 - u))
            e.wait_ge(x_tp, NT)
            g_steps.inc(e.memset(RX[:, 0:3], 0.0))
            e.sem_inc(g_ev, 5)

            def empty_block(n, j):
                e.wait_ge(g_mm, 5 * n + j + 1)
                return e.tensor_copy(ZS[:, j], PS[:, j, 0:BW]).then_inc(g_ev, 1)

            with e.Fori(0, 4) as c:
                for u in range(2):
                    for j in range(NB):
                        e.wait_ge(z_st[j], 32 * c + 16 * u)
                        if u == 1 and j == NB - 1:
                            e.wait_ge(t_pe, c + 1)
                        empty_block(2 * c + u, j)
            for j in range(NB):
                e.wait_ge(g_mm, 40 + j + 1)
                e.tensor_scalar(RX[0:NH, 3 + j * BW:3 + (j + 1) * BW], PS[0:NH, j, 0:BW], bf[:, 0:1], None, ALU.add)\
                    .then_inc(g_ev, 1)
            e.wait_ge(f_tp, 1)
            logit = PS[:, 5, 0:NT * NH].rearrange("p (t h) -> p t h", h=NH)
            g_steps.inc(e.tensor_scalar(FW[:], logit, 0.0, None, ALU.min))
            g_steps.settle()
            e.scalar_tensor_tensor(out=FE[:], in0=FW[:], scalar=-2.0, in1=logit, op0=ALU.mult, op1=ALU.add)\
                .then_inc(l_ax, 1)
            e.wait_ge(l_ax, 2)
            e.sem_inc(f_dv, 1)
            e.wait_ge(l_ex, 2)
            half_log1p(FE[:], FT[:], FL[:])
            e.scalar_tensor_tensor(out=FL[:], in0=FL[:], scalar=-2.0, in1=FW[:], op0=ALU.mult, op1=ALU.add)\
                .then_inc(f_dv, 1)
            e.wait_ge(f_tp, 2)
            within = PS[:, 6, 0:NT * NH].rearrange("p (t h) -> p t h", h=NH)
            total = PS[:, 7, 0:NT * NH].rearrange("p (t h) -> p t h", h=NH)
            g_steps.inc(e.tensor_copy(FT[:], total))
            g_steps.settle()
            g_steps.inc(e.memset(FE[:, 0], 0.0))
            for h in range(NH):
                g_steps.inc(e.tensor_tensor_scan(FE[:, 1:NT, h], onesF[:, 0:NT - 1], FT[:, 0:NT - 1, h], 0.0,
                                                 ALU.mult, ALU.add))
            g_steps.settle()
            g_steps.inc(e.tensor_tensor(FE[:], FE[:], within, ALU.add))
            g_steps.settle()
            hi, lo = FD[:, :, 0:NH], FD[:, :, NH:2 * NH]
            g_steps.inc(e.tensor_scalar(hi.bitcast(F32R), FE[:], -8.0, None, ALU.mult))
            g_steps.settle()
            e.scalar_tensor_tensor(out=lo.bitcast(F32R), in0=FE[:], scalar=-8.0, in1=hi, op0=ALU.mult,
                                   op1=ALU.subtract).then_inc(f_dv, 1)
            for g in range(NB):
                e.wait_ge(f_tp, 3 + g)
                w = min(512, TP - 512 * g)
                e.tensor_copy(RX[0:16, 3 + 512 * g:3 + 512 * g + w], PS[0:16, 5 + g % 3, 0:w]).then_inc(f_ev, 1)
            e.wait_ge(f_ev, NB)
            e.sem_inc(f_dv, 1)
            for s in z_st:
                e.wait_ge(s, 16 * 8)

            with e.Fori(0, 2) as i:
                g_steps.start(i, 2 * 12)
                for u in range(2):
                    c = 2 * i + u
                    n = 9 + 3 * c
                    ev = 4 + 11 * c
                    one = bass.ds(c, 1)

                    def tap(k):
                        return rtab[:, one, k]

                    x, r, w = RX, RC, RW
                    smp = slice(TPR, TPR + NS)
                    for j in range(NB):
                        e.wait_ge(z_st[j], 128 + 32 * c)
                        if j == NB - 1:
                            e.wait_ge(t_pe, ev)
                        else:
                            e.wait_ge(t_pe, ev - (NB - 1) + j)
                        empty_block(n, j)
                        if j == 0:
                            e.wait_ge(r_ld, 16 * c + 16)
                            e.wait_ge(r_act, 17 * c)
                            g_steps.inc(e.tensor_scalar(r[:], x[:, 0:TP], tap(0), tap(4), ALU.mult, ALU.add))
                            g_steps.settle()
                        elif j < 4:
                            g_steps.inc(e.scalar_tensor_tensor(out=r[:], in0=x[:, j:j + TP], scalar=tap(j), in1=r[:],
                                                               op0=ALU.mult, op1=ALU.add))
                            g_steps.settle()
                        else:
                            g_steps.inc(e.tensor_scalar(r[:, smp], rstate[:, one, 0, :].rearrange("p o s -> p (o s)"),
                                                        tap(0), tap(4), ALU.mult, ALU.add))
                            g_steps.settle()
                            for k in (1, 2):
                                g_steps.inc(e.scalar_tensor_tensor(
                                    out=r[:, smp], in0=rstate[:, one, k, :].rearrange("p o s -> p (o s)"),
                                    scalar=tap(k), in1=r[:, smp], op0=ALU.mult, op1=ALU.add))
                                g_steps.settle()
                            e.scalar_tensor_tensor(out=r[:, smp], in0=x[:, 3 + TPR:3 + TPR + NS], scalar=tap(3),
                                                   in1=r[:, smp], op0=ALU.mult, op1=ALU.add).then_inc(r_conv, 1)
                    for j in range(NB):
                        e.wait_ge(z_st[j], 128 + 32 * c + 16)
                        if j == NB - 1:
                            e.wait_ge(t_pe, ev + 1)
                        empty_block(n + 1, j)
                        e.wait_ge(r_conv, c + 1)
                        e.wait_ge(r_act, 17 * c + 3 * j + 1)
                        e.scalar_tensor_tensor(out=x[:, 3 + j * BW:3 + (j + 1) * BW], in0=RT[:, 0], scalar=1.0,
                                               in1=r[:, cols(j)], op0=ALU.add, op1=ALU.mult).then_inc(r_u, 1)
                    for j in range(NB):
                        e.wait_ge(z_st[j], 128 + 32 * c + 32)
                        e.wait_ge(t_pe, ev + 1 + j + 1)
                        empty_block(n + 2, j)
                        if j == 0:
                            e.wait_ge(r_act, 17 * c + 16)
                            g_steps.inc(e.tensor_scalar(w[:], w[:], 1.0, None, ALU.add))
                            g_steps.settle()
                            g_steps.inc(e.reciprocal(w[:], w[:]))
                            g_steps.settle()
                        elif j == 1:
                            g_steps.inc(e.tensor_tensor(r[:], r[:], w[:], ALU.mult))
                            g_steps.settle()
                            e.wait_ge(r_u, 5 * c + 5)
                            g_steps.inc(e.tensor_tensor(x[:, 3:3 + TP], x[:, 3:3 + TP], r[:], ALU.mult))
                            g_steps.settle()
                        elif j == 2:
                            g_steps.inc(e.tensor_scalar(r[:], w[:], 2.0, -1.0, ALU.mult, ALU.add))
                            g_steps.settle()
                            e.tensor_tensor_scan(w[:, 0:TPR], r[:, 0:TPR], x[:, 3:3 + TPR], 0.0, ALU.mult, ALU.add)
                            e.tensor_tensor(w[:, TPR:TP], r[:, TPR:TP], rh0[:, one, :].rearrange("p o s -> p (o s)"),
                                            ALU.mult).then_inc(r_h, 1)
                            e.wait_ge(r_h, c + 1)
                            e.tensor_tensor(w[:, TPR:TP], w[:, TPR:TP], x[:, 3 + TPR:3 + TP], ALU.add)\
                                .then_inc(r_sc, 1)
                    e.wait_ge(r_sc, c + 1)
                    e.wait_ge(r_act, 17 * c + 17)
                    e.tensor_tensor(x[:, 3:3 + TP], w[:], r[:], ALU.mult).then_inc(r_y, 1)
                g_steps.stop(2)
            e.wait_ge(g_ev, 5 * NIN + 5)
            e.wait_ge(r_y, 4)
            e.sem_inc(phase_end, 1)
            e.wait_ge(phase_end, 4)
            e.memset(VA[:, :, :, HD:P].rearrange("p a t d -> p (a t) d"), 1.0).then_inc(c_att, 1)
            g_steps.inc(e.memset(segm, 1.0))
            g_steps.inc(e.memset(MP[:], -3e38))
            g_steps.inc(e.memset(NM[:], 0.0))
            g_steps.settle()
            g_steps.inc(e.memset(segm.rearrange("p (s g) -> p s g", g=PAGES)[:, :, 0], 0.0))
            g_steps.settle()
            e.wait_ge(c_att, 1)
            e.sem_inc(on, 5)
            e.wait_ge(lf_ev, 8)
            incl = prod[:].rearrange("p a b n -> p (a b n)")
            g_steps.inc(e.tensor_tensor_scan(incl, segm, ctot, 0.0, ALU.mult, ALU.add))
            g_steps.settle()
            e.wait_ge(lf_ld, 16)
            last = incl.rearrange("p (h s g) -> p s h g", h=NH, g=PAGES)[:, :, :, PAGES - 1]
            g_steps.inc(e.tensor_tensor(cnew[:], cnew[:], last, ALU.add))
            g_steps.settle()
            g_steps.inc(e.tensor_tensor(incl, incl, ctot, ALU.subtract))
            g_steps.settle()
            e.tensor_tensor(cb[:].rearrange("p s h -> p h s"), incl.rearrange("p (h s) -> p h s", h=NH),
                            cwith.rearrange("p (h s) -> p h s", h=NH), ALU.add).then_inc(cb_ok, 1)
            e.wait_ge(cb_ok, 1)

            def page_scores(s, v, g):
                e.wait_ge(kg_ld[g % 4], 32 * (4 * s + g // 4) + 32)
                if g == 0:
                    e.wait_ge(nw_ld, 48 * s + 48)
                p = prod[:, g % 2]
                e.tensor_tensor(p, Kpg[:, g % 4], qb[:, v].unsqueeze(1).to_broadcast([P, 2, DATT]), ALU.mult)\
                    .then_inc(kp, 1)
                e.wait_ge(kp, 17 * s + g + 1)
                e.tensor_reduce(sc[:, v, 2 * g:2 * g + 2, :], p.rearrange("p b (h d) -> p b h d", d=HD), AX.X, ALU.add)\
                    .then_inc(kd, 1)

            def scores_end(s, v):
                e.wait_ge(kd, 16 * s + 16)
                p = prod[:, 0, 0]
                e.tensor_tensor(p, knb[:, v], qb[:, v], ALU.mult).then_inc(kp, 1)
                e.wait_ge(kp, 17 * s + 17)
                e.tensor_reduce(sn[:, v], p.rearrange("p (h d) -> p h d", d=HD), AX.X, ALU.add).then_inc(kf, 1)
                e.scalar_tensor_tensor(out=sc[:, v], in0=sc[:, v], scalar=0.125, in1=cb[:, bass.ds(s * PAGES, PAGES), :],
                                       op0=ALU.mult, op1=ALU.subtract).then_inc(kf, 1)
                e.wait_ge(kf, 4 * s + 2)
                e.scalar_tensor_tensor(out=sn[:, v], in0=sn[:, v], scalar=0.125,
                                       in1=cnew[:, bass.ds(s, 1), :].rearrange("p o h -> p (o h)"),
                                       op0=ALU.mult, op1=ALU.subtract).then_inc(kq, 1)
                e.tensor_reduce(mloc[:, v], sc[:, v].rearrange("p g h -> p h g"), AX.X, ALU.max).then_inc(kq, 1)
                e.wait_ge(kq, 3 * s + 2)
                e.tensor_tensor(mloc[:, v], mloc[:, v], sn[:, v], ALU.max).then_inc(kf, 1)

            def scores_less(s, v):
                e.wait_ge(mr, s + 1)
                e.tensor_tensor(sc[:, v], sc[:, v], mall[:, v].unsqueeze(1).to_broadcast([P, PAGES, NH]), ALU.subtract)\
                    .then_inc(kq, 1)
                e.tensor_tensor(sn[:, v], sn[:, v], mall[:, v], ALU.subtract).then_inc(kf, 1)

            def sample_sums(s, v):
                e.wait_ge(de, 2 * s + 1)
                e.sem_inc(go, 1)
                e.tensor_reduce(dsum[:, v], sc[:, v].rearrange("p g h -> p h g"), AX.X, ALU.add).then_inc(dn, 1)

            for g in range(PAGES // 2):
                page_scores(0, 0, g)
            scores_end(0, 0)
            scores_less(0, 0)
            sample_sums(0, 0)

            def dve_head(ii, u, nxt):
                i = 2 * ii + u
                for p, (qt, pc, k0, n, rows, _) in enumerate(PIECES):
                    e.wait_ge(mm_mx, 45 * i + p + 1)
                    e.tensor_reduce(MP[0:rows, qt, pc:pc + 1], PS[0:rows, p % 4, 0:n], AX.X, ALU.max).then_inc(mx, 1)
                e.wait_ge(mx, 45 * i + 45)
                e.tensor_reduce(MX[:], MP[:], AX.X, ALU.max).then_inc(nm, 1)
                e.wait_ge(nm, 3 * i + 1)
                e.tensor_scalar(NM[:, :, HD].bitcast(F32R), MX[:], -1.0, None, ALU.mult).then_inc(nm, 1)
                e.wait_ge(nm, 3 * i + 2)
                e.scalar_tensor_tensor(out=NM[:, :, HD + 1].bitcast(F32R), in0=MX[:], scalar=-1.0, in1=NM[:, :, HD],
                                       op0=ALU.mult, op1=ALU.subtract).then_inc(nm, 1)
                ends = [sum(1 for t in TILES if t[0] <= j) for j in range(NB)]
                groups = ((0, 1), (1, 4), (4, 8), (8, 12), (12, 16))
                for j in range(NB):
                    if nxt:
                        for g in range(*groups[j]):
                            page_scores(i + 1, 1 - u, g)
                    w = BW if j < NB - 1 else LASTP
                    bank, s = 4 + (j + 1) % 2, (u + j) % 2
                    e.wait_ge(pv, 51 * i + ends[j])
                    e.wait_ge(on, 5 * i + j + 5)
                    e.reciprocal(rden[0:HD, 0:w], PS[HD:P, bank, 0:w]).then_inc(rd, 1)
                    e.wait_ge(rd, 5 * i + j + 1)
                    e.wait_ge(ao_st[s], 16 * (5 * ii + (5 * u + j) // 2))
                    e.tensor_tensor(AO[0:HD, s, 0:w], PS[0:HD, bank, 0:w], rden[0:HD, 0:w], ALU.mult).then_inc(on, 1)
                    if j == 3:
                        e.wait_ge(df, i + 1)
                        e.reciprocal(dinv[:], PS[0:NH, 6, 0:1]).then_inc(od_s, 1)
                        e.wait_ge(od_s, 2 * i + 1)
                        e.scalar_tensor_tensor(out=od[:], in0=PS[0:NH, 7, :], scalar=dinv[:, 0:1], in1=headmask[:],
                                               op0=ALU.mult, op1=ALU.mult).then_inc(od_s, 1)
                if nxt:
                    scores_end(i + 1, 1 - u)
                e.wait_ge(av, i + 1)
                e.tensor_copy(attS[:, :, bass.ds(i, 1)], PS[:, 6, 8:12].unsqueeze(2)).then_inc(at_s, 1)
                if nxt:
                    scores_less(i + 1, 1 - u)
                    sample_sums(i + 1, 1 - u)

            e.wait_ge(c_att2, 5)
            with e.Fori(0, 3) as ii:
                for u in range(2):
                    dve_head(ii, u, True)
            dve_head(3, 0, True)
            dve_head(3, 1, False)
            e.wait_ge(at_s, NS)
            e.wait_ge(on, 5 * NH + 5)
            e.wait_ge(kf, 4 * NS)
            e.wait_ge(dn, NS)
            e.wait_ge(nm, 3 * NH)
            e.sem_inc(phase_end, 1)
            e.wait_ge(phase_end, 8)
            e.sem_inc(u_ev, 5)
            def norm_sum(n):
                e.wait_ge(nsq, n + 1)
                if n >= 2:
                    e.wait_ge(nmm, n - 1)
                parts = 2 if n < 10 else 1
                sq = SQ[:, :, cols(n % 10, HB)].rearrange("p (a k) n -> p a n k", a=parts)
                e.tensor_reduce(NZ[:, n % 2, 0:parts], sq, AX.X, ALU.add).then_inc(nrd, 1)

            def norm_apply(n):
                c, parts = cols(n % 10, HB), (2 if n < 10 else 1)
                e.wait_ge(nrs, n + 1)
                e.reciprocal(NG[:, n % 2, 0:parts], NG[:, n % 2, 0:parts]).then_inc(nrc, 1)
                e.wait_ge(nrc, n + 1)
                for k in range(KC):
                    gain = gains[:, k:k + 1] if n < 10 else gains[:, KC + k:KC + k + 1]
                    ins = e.scalar_tensor_tensor(out=MF[:, k, c], in0=NR[:, n % 3, k], scalar=gain,
                                                 in1=NG[:, n % 2, k // 4 if n < 10 else 0], op0=ALU.mult, op1=ALU.mult)
                ins.then_inc(nst, 1)

            def add_residual(m, j):
                e.wait_ge(u_mm, 5 * m + j + 1)
                e.wait_ge(xs_ld[j], 16 * m + 16)
                e.tensor_tensor(XS[:, j], XS[:, j], PS[:, j, 0:BW], ALU.add).then_inc(u_ev, 1)

            norm_sum(0)
            for n in range(10):
                if n < 9:
                    norm_sum(n + 1)
                norm_apply(n)
                if n == 6:
                    e.wait_ge(nst, 7)
                    e.tensor_copy(NR[:, 0, 0:4, TPR - 9 * HB:HB], attS[:]).then_inc(na_s, 1)
            for j in range(NB):
                add_residual(0, j)
            with e.Fori(1, 7) as m:
                for j in range(NB):
                    add_residual(m, j)
            add_residual(7, 0)
            add_residual(7, 1)
            add_residual(7, 2)
            norm_sum(10)
            for n in range(10, 20):
                if n < 19:
                    norm_sum(n + 1)
                norm_apply(n)
                if n < 12:
                    add_residual(7, n - 7)
            e.wait_ge(nst, 20)
            e.wait_ge(nmm, 20)
            e.wait_ge(nsq, 20)
            g_steps.inc(e.memset(GP[:, :, 0:2], 0.0))
            g_steps.settle()

            with e.Fori(0, FC // 2) as i:
                g_steps.start(i, 2 * (2 * NB + 3))
                for u in range(2):
                    f = 2 * i + u
                    one = bass.ds(f, 1)

                    def tap(k):
                        return ftab[:, one, k]

                    def state(k):
                        return fstate[:, one, k, :].rearrange("p o s -> p (o s)")

                    def convolve(j):
                        s, o = (u + j) % 2, j * BW
                        d, x = GC[:, s], GP[:, u]
                        if j == 0:
                            e.wait_ge(u_ev, 5 * (8 + 2 * f) + 10)
                        else:
                            e.wait_ge(u_ev, 5 * (9 + 2 * f) + max(j - 2, -1) + 6)
                        g_steps.inc(e.tensor_scalar(d, x[:, o:o + BW], tap(0), tap(3), ALU.mult, ALU.add))
                        g_steps.settle()
                        g_steps.inc(e.scalar_tensor_tensor(out=d, in0=x[:, o + 1:o + 1 + BW], scalar=tap(1), in1=d,
                                                           op0=ALU.mult, op1=ALU.add))
                        g_steps.settle()
                        ins = e.scalar_tensor_tensor(out=d, in0=x[:, o + 2:o + 2 + BW], scalar=tap(2), in1=d,
                                                     op0=ALU.mult, op1=ALU.add)
                        if j == NB - 1:
                            g_steps.inc(ins)
                            d = d[:, LASTP:LASTP + NS]
                            g_steps.settle()
                            g_steps.inc(e.tensor_scalar(d, state(0), tap(0), tap(3), ALU.mult, ALU.add))
                            g_steps.settle()
                            g_steps.inc(e.scalar_tensor_tensor(out=d, in0=state(1), scalar=tap(1), in1=d,
                                                               op0=ALU.mult, op1=ALU.add))
                            g_steps.settle()
                            ins = e.scalar_tensor_tensor(out=d, in0=x[:, 2 + TPR:2 + TPR + NS], scalar=tap(2), in1=d,
                                                         op0=ALU.mult, op1=ALU.add)
                        ins.then_inc(gcv, 1)

                    def multiply(j):
                        s = (u + j) % 2
                        e.wait_ge(u_mm, 5 * (9 + 2 * f) + j + 1)
                        e.wait_ge(gge, 5 * f + j + 1)
                        e.wait_ge(go_st[s], 16 * (5 * i + (5 * u + j) // 2))
                        e.tensor_tensor(GO[:, s], GC[:, s], PS[:, j, 0:BW], ALU.mult).then_inc(u_ev, 1)

                    for j in range(NB):
                        e.wait_ge(u_mm, 5 * (8 + 2 * f) + j + 1)
                        if j == 0:
                            e.wait_ge(gcv, 5 * f)
                        if j == NB - 1:
                            e.wait_ge(tt_pe, f)
                        e.tensor_copy(GP[:, u, 2 + j * BW:2 + (j + 1) * BW], PS[:, j, 0:BW]).then_inc(u_ev, 1)
                    convolve(0)
                    convolve(1)
                    for j in range(NB):
                        multiply(j)
                        if j + 2 < NB:
                            convolve(j + 2)
                g_steps.stop(FC // 2)
            e.wait_ge(u_ev, 5 * 52 + 5)
            e.wait_ge(gcv, 5 * FC)
            e.sem_inc(phase_end, 1)
            e.wait_ge(phase_end, 12)
            rows_of = [(m * P, w) for m, w in ((0, P), (1, P), (2, P), (3, TAIL))]

            def inner_low(j, q):
                f = FH * j + q
                e.wait_ge(gg_hi, f + 1)
                e.tensor_tensor(GL[:, f % RING], GR[:, f % 3], GH[:, f % RING].bitcast(F32), ALU.subtract)\
                    .then_inc(gg_lo, 1)

            def add_x2(n, v):
                e.wait_ge(dk, 22 * n + 22)
                e.wait_ge(yx_ld[v], 8 * (n - v) + 16)
                e.tensor_tensor(YX[:, v], YX[:, v], PS[:, v, 0:BW], ALU.add).then_inc(y_ev, 1)

            def final_apply(j):
                e.wait_ge(y_sq, 6 * j + 6)
                e.reciprocal(yr[:, 0:3], yr[:, 0:3]).then_inc(y_rc, 1)
                e.reciprocal(yr[0:TAIL, 3:4], yr[0:TAIL, 3:4]).then_inc(y_rc, 1)
                e.wait_ge(y_rc, 2 * j + 2)
                for m, (o, w) in enumerate(rows_of):
                    e.scalar_tensor_tensor(out=YT[0:w, m], in0=YT[0:w, m], scalar=yr[0:w, m:m + 1], in1=gfin[0:w],
                                           op0=ALU.mult, op1=ALU.mult).then_inc(y_nm, 1)

            for q in range(FH):
                inner_low(0, q)
            e.wait_ge(nf_ld, 16)
            for j in range(NB):
                def dve_pair(i, first=False, last=False):
                    oc = 8 * j + 2 * i
                    fills = {0: (0, 1, 2), 1: (3, 4), 2: (5, 6, 7, 8, 9), 3: (10,)}
                    for c in range(4):
                        if last and j < NB - 1:
                            for q in fills[c]:
                                inner_low(j + 1, q)
                        if c == 1:
                            add_x2(oc, 0)
                            if first and j:
                                final_apply(j - 1)
                        if c == 3:
                            add_x2(oc + 1, 1)

                dve_pair(0, first=True)
                with e.Fori(1, 3) as i:
                    dve_pair(i)
                dve_pair(3, last=True)
            final_apply(NB - 1)

        @block.tensor
        def _(e):
            e.wait_ge(c_pool, 13)

            def turn(t, u, rows=P):
                e.wait_ge(x_hn, t + 1)
                if not (isinstance(t, int) and t < 2):
                    e.wait_ge(x_ev, 2 * t - 2)
                    e.wait_ge(x_lo, t - 1)
                for src, b in ((xin, 4 * u), (hn, 4 * u + 2)):
                    for k in range(KC):
                        mm = e.transpose(PS[:, b + k // 4, (k % 4) * P:(k % 4) * P + rows],
                                         src[0:rows, u, k * P:(k + 1) * P], identF[0:rows, 0:rows])
                mm.then_inc(x_tp, 1)

            turn(0, 0)
            turn(1, 1)
            with e.Fori(1, 8) as i:
                for u in range(2):
                    turn(2 * i + u, u)
            turn(16, 0, TAIL)
            e.wait_ge(x_ev, 2 * NT)
            e.wait_ge(x_lo, NT)

            def project(n, u, j, hi, lo, w_hi_t, w_lo_t):
                e.wait_ge(g_ev, 5 * n + j + 1)
                for k in range(KC):
                    for q, (w, x) in enumerate(((w_hi_t, hi), (w_hi_t, lo), (w_lo_t, hi))):
                        mm = e.matmul(PS[:, j, 0:BW], w[:, u, k], x[:, k, cols(j)],
                                      start=(k == 0 and q == 0), stop=(k == KC - 1 and q == 2))
                mm.then_inc(g_mm, 1)

            def chunk(n, u, after=None):
                e.wait_ge(w_lo, n + 1)
                for j in range(NB):
                    project(n, u, j, XH, XL, WH, WL)
                    if after:
                        after(j)

            with e.Fori(0, 4) as c:
                chunk(2 * c, 0)

                def tail(j, c=c):
                    if j == 0:
                        e.wait_ge(g_ev, 10 * c + 10)
                        e.wait_ge(t_ev, c)
                        e.transpose(PS[0:TAIL, 5, 0:P], ZS[:, NB - 1, 3 * P:BW], identF[:]).then_inc(t_pe, 1)

                chunk(2 * c + 1, 1, tail)
            chunk(8, 0)
            e.wait_ge(g_ev, 50)
            e.wait_ge(t_ev, 4)
            for t in range(NT):
                w = min(P, TP - t * P)
                mm = e.transpose(PS[0:w, 5, t * NH:(t + 1) * NH], RX[0:NH, 3 + t * P:3 + t * P + w],
                                 identF[0:NH, 0:NH])
            mm.then_inc(f_tp, 1)
            e.wait_ge(f_dv, 2)
            flat = FL[:].rearrange("p t h -> p (t h)")
            e.wait_ge(c_pool, 13)
            e.matmul(PS[:, 6, 0:NT * NH], triu[:], flat, start=True, stop=True)
            e.matmul(PS[:, 7, 0:NT * NH], onesF[:], flat, start=True, stop=True).then_inc(f_tp, 1)
            e.wait_ge(f_dv, 3)
            for g in range(NB):
                if g >= 3:
                    e.wait_ge(f_ev, g - 2)
                for t in range(4 * g, min(4 * g + 4, NT)):
                    w = min(P, TP - t * P)
                    mm = e.transpose(PS[0:16, 5 + g % 3, (t % 4) * P:(t % 4) * P + w], FD[0:w, t, :],
                                     identF[0:w, 0:w])
                mm.then_inc(f_tp, 1)
            e.wait_ge(f_dv, 4)

            with e.Fori(0, 2) as i:
                for u in range(2):
                    c = 2 * i + u
                    n = 9 + 3 * c
                    ev = 4 + 11 * c

                    def turn_rows(done, ev, j):
                        e.wait_ge(g_ev, done)
                        e.wait_ge(t_ev, ev)
                        for m, (o, w) in enumerate(seg(j)):
                            mm = e.transpose(PS[0:w, 5, m * P:(m + 1) * P], ZS[:, j, o:o + w], identF[:])
                        mm.then_inc(t_pe, 1)

                    def after_k(j):
                        if j == 0:
                            e.wait_ge(g_ev, 5 * n + 10)
                            e.wait_ge(t_ev, ev)
                            e.transpose(PS[0:TAIL, 5, 0:P], ZS[:, NB - 1, 3 * P:BW], identF[:]).then_inc(t_pe, 1)
                        else:
                            turn_rows(5 * (n + 1) + j - 1 + 6, ev + j, j - 1)
                        e.wait_ge(r_conv, c + 1)
                        e.wait_ge(r_gw, 64 * c + 64)
                        e.wait_ge(r_act, 17 * c + (3 * j - 1 if j else 0))
                        e.matmul(PS[:, 6, 0:BW], gw[:, 0], RC[:, cols(j)], start=True, stop=True)
                        e.matmul(PS[:, 7, 0:BW], gw[:, 1], RC[:, cols(j)], start=True, stop=True).then_inc(r_gate, 1)

                    def after_v(j):
                        if j == 0:
                            turn_rows(5 * (n + 1) + 4 + 6, ev + 5, NB - 1)
                        else:
                            turn_rows(5 * (n + 2) + j - 1 + 6, ev + 5 + j, j - 1)

                    chunk(n, (1 + u) % 2)
                    chunk(n + 1, u % 2, after_k)
                    chunk(n + 2, (1 + u) % 2, after_v)
                    turn_rows(5 * (n + 2) + 4 + 6, ev + 10, NB - 1)
            e.wait_ge(g_mm, 5 * NIN)
            e.wait_ge(t_pe, 48)
            e.wait_ge(r_gate, 20)
            e.sem_inc(phase_end, 1)
            e.wait_ge(phase_end, 4)
            e.wait_ge(lf_pg, 32)
            for g in range(2):
                by_head = lpage[:, g].rearrange("p (s h) -> p h s", h=NH)
                if g:
                    e.wait_ge(lf_ev, 4)
                for b in range(2):
                    for h in range(4):
                        mm = e.transpose(PS[:, b, h * P:(h + 1) * P], by_head[:, 4 * b + h], identF[:])
                    mm.then_inc(lf_tp, 1)
                e.wait_ge(lf_ev, 4 * g + 2)
                for b in range(2):
                    e.matmul(PS[:, 2 + 2 * b, :], triu[:], xtp[:, 512 * b:512 * b + 512], start=True, stop=True)
                    e.matmul(PS[:, 3 + 2 * b, :], onesF[:], xtp[:, 512 * b:512 * b + 512], start=True, stop=True)\
                        .then_inc(lf_tp, 1)
            e.wait_ge(lf_ev, 8)

            def pe_head(ii, u, nxt):
                i = 2 * ii + u
                e.wait_ge(prep, 7 * i + 7)
                for p, (qt, pc, k0, n, rows, diag) in enumerate(PIECES):
                    if p < 4:
                        e.wait_ge(ex, 51 * i + p + 1)
                    else:
                        e.wait_ge(mx, 45 * i + p - 3)
                    o = PS[0:rows, p % 4]
                    mm = e.matmul(o[:, 0:n], QA[0:HD + 4, u, qt * P:qt * P + rows], KA[0:HD + 4, u, k0:k0 + n],
                                  start=True, stop=not diag)
                    if diag:
                        d = min(P, n)
                        mm = e.matmul(o[:, n - d:n], identB[0:rows, 0:rows], maskQ[0:rows, 0:d], start=False, stop=True)
                    mm.then_inc(mm_mx, 1)
                e.wait_ge(nm, 3 * i + 3)
                for g in range(NB):
                    if g < 2:
                        e.wait_ge(on, 5 * i + 4 + g)
                    else:
                        e.wait_ge(na, 5 * i + g - 1)
                    e.sem_inc(go, 1)
                    for t in range(4 * g, min(4 * g + 4, NT)):
                        w = min(P, TP - t * P)
                        mm = e.transpose(PS[0:HD + 2, 4 + g % 2, (t % 4) * P:(t % 4) * P + w], NM[0:w, t, :],
                                         identF[0:w, 0:w])
                    mm.then_inc(nt, 1)

                def scores(t):
                    j, kt, q0, n, kr = TILES[t]
                    if t < 4:
                        e.wait_ge(mx, 45 * i + 42 + t)
                    else:
                        e.wait_ge(ex, 51 * i + t + 1)
                    o = PS[0:kr, (45 + t) % 4]
                    ks, qs = slice(kt * P, kt * P + kr), slice(q0, q0 + n)
                    e.matmul(o[:, 0:n], KA[0:HD + 4, u, ks], QA[0:HD + 4, u, qs], start=True, stop=False)
                    d = min(n, kt * P + P - q0)
                    mm = e.matmul(o[:, 0:n], KB[:, u, ks], QB[:, u, qs], start=False, stop=d <= 0)
                    if d > 0:
                        m = q0 - kt * P
                        mm = e.matmul(o[:, 0:d], identB[0:kr, 0:kr], maskK[0:kr, m:m + d], start=False, stop=True)
                    mm.then_inc(sT, 1)

                def values(t):
                    j, kt, q0, n, kr = TILES[t]
                    bank = 4 + (j + 1) % 2
                    if kt == 0:
                        if j < 2:
                            e.wait_ge(na, 5 * i + 4 + j)
                        else:
                            e.wait_ge(on, 5 * i + j + 4)
                        if j == 0:
                            e.wait_ge(va_ld[u], 32 * ii + 32)
                    e.wait_ge(ex, 51 * i + t + 5)
                    o = q0 - j * BW
                    last = t + 1 == len(TILES) or TILES[t + 1][0] != j
                    e.matmul(PS[:, bank, o:o + n], VA[0:kr, u, kt], PT[0:kr, t % 3, 0:n], start=(kt == 0), stop=last)\
                        .then_inc(pv, 1)

                def pages(g):
                    if g == 0:
                        e.wait_ge(de, 2 * i + 2)
                        e.wait_ge(dn, i + 1)
                        e.wait_ge(od_s, 2 * i)
                        e.wait_ge(at_s, i)
                    e.wait_ge(vg_ld[g % 4], 32 * (4 * i + g // 4) + 32)
                    for m in range(2):
                        mm = e.matmul(PS[0:NH, 7, :], sc[:, u, 2 * g + m, :], Vpg[:, g % 4, m], start=(g == 0 and m == 0),
                                      stop=False)
                    mm.then_inc(vd, 1)
                    if g == PAGES // 2 - 1:
                        e.wait_ge(nw_ld, 48 * i + 48)
                        e.sem_inc(go, 1)
                        e.matmul(PS[0:NH, 7, :], sn[0:1, u, :], vnew[:, u], start=False, stop=True)
                        e.matmul(PS[0:NH, 6, 0:1], dsum[:, u], onesF[:, 0:1], start=True, stop=False)
                        e.matmul(PS[0:NH, 6, 0:1], sn[0:1, u, :], onesF[0:1, 0:1], start=False, stop=True)\
                            .then_inc(df, 1)

                e.wait_ge(na, 5 * i + 5)
                scores(0)
                for t in range(len(TILES)):
                    if t + 1 < len(TILES):
                        scores(t + 1)
                    values(t)
                    j = TILES[t][0]
                    if j < 4 and TILES[t + 1][0] != j:
                        for g in range(4 * j, 4 * j + 4):
                            pages(g)
                e.wait_ge(od_s, 2 * i + 2)
                for c in range(4):
                    mm = e.matmul(PS[:, 6, 8 + c:9 + c], od[:, c * P:(c + 1) * P], onesF[0:NH, 0:1], start=True, stop=True)
                mm.then_inc(av, 1)

            with e.Fori(0, 3) as ii:
                for u in range(2):
                    pe_head(ii, u, True)
            pe_head(3, 0, True)
            pe_head(3, 1, False)
            e.wait_ge(pv, 51 * NH)
            e.wait_ge(df, NS)
            e.wait_ge(av, NS)
            e.sem_inc(phase_end, 1)
            e.wait_ge(phase_end, 8)

            def norm_total(n):
                e.wait_ge(nrd, n + 1)
                if n >= 2:
                    e.wait_ge(nrs, n - 1)
                w = 2 * HB if n < 10 else HB
                e.matmul(PS[:, 5 + n % 2, 0:w], onesF[:], NZ[:, n % 2].rearrange("p a n -> p (a n)")[:, 0:w],
                         start=True, stop=True).then_inc(nmm, 1)

            def dense(m, u, j):
                e.wait_ge(u_ev, 5 * m + j + 1)
                for k in range(KC):
                    for q, (w, x) in enumerate(((VH, MH), (VH, ML), (VL, MH))):
                        mm = e.matmul(PS[:, j, 0:BW], w[:, u, k], x[:, k, cols(j)], start=(k == 0 and q == 0),
                                      stop=(k == KC - 1 and q == 2))
                mm.then_inc(u_mm, 1)

            norm_total(0)
            norm_total(1)
            e.wait_ge(v_lo, 1)
            for j in range(NB):
                if j < 4:
                    norm_total(2 * j + 2)
                    norm_total(2 * j + 3)
                e.wait_ge(nlo, 2 * j + 2)
                dense(0, 0, j)
            with e.Fori(0, 3) as i:
                for u in range(2):
                    e.wait_ge(v_lo, 2 * i + u + 2)
                    for j in range(NB):
                        dense(2 * i + u + 1, 1 - u, j)
            e.wait_ge(v_lo, 8)
            for j in range(NB):
                dense(7, 1, j)
                if j >= 2:
                    norm_total(8 + j)
            e.wait_ge(v_lo, 9)
            norm_total(13)
            for j in range(NB):
                if 0 < j < 4:
                    norm_total(12 + 2 * j)
                    norm_total(13 + 2 * j)
                e.wait_ge(nlo, 10 + 2 * j + 2)
                dense(8, 0, j)

            def values_chunk(f, u):
                e.wait_ge(v_lo, 2 * f + 10)
                for j in range(NB):
                    dense(9 + 2 * f, 1, j)
                    if j == 0:
                        e.wait_ge(u_ev, 5 * (8 + 2 * f) + 10)
                        e.wait_ge(tt_ev, f)
                        e.sem_inc(go, 1)
                        e.transpose(PS[0:TAIL, 7, 0:P], GP[:, u, 2 + TP - TAIL:2 + TP], identF[:]).then_inc(tt_pe, 1)

            values_chunk(0, 0)
            with e.Fori(0, 10) as i:
                for u in range(2):
                    f = 2 * i + u + 1
                    e.wait_ge(v_lo, 2 * f + 9)
                    for j in range(NB):
                        dense(8 + 2 * f, 0, j)
                    values_chunk(f, 1 - u)
            e.wait_ge(v_lo, 51)
            for j in range(NB):
                dense(50, 0, j)
            values_chunk(21, 1)
            e.wait_ge(u_mm, 5 * 52)
            e.wait_ge(tt_pe, FC)
            e.wait_ge(nmm, 20)
            e.sem_inc(phase_end, 1)
            e.wait_ge(phase_end, 12)
            def turn_sum(n, v):
                e.wait_ge(y_ev, n + 1)
                if not (isinstance(n, int) and n < 2):
                    e.wait_ge(y_tk, n - 1)
                e.sem_inc(go, 1)
                for m, (o, w) in enumerate(seg(0)):
                    mm = e.transpose(PS[0:w, 4 + v, m * P:(m + 1) * P], YX[:, v, o:o + w], identF[:])
                mm.then_inc(y_tp, 1)

            for j in range(NB):
                def pe_pair(i, first=False):
                    n, oc = 16 * j + 4 * i, 8 * j + 2 * i
                    for c in range(4):
                        v, h = c // 2, c % 2
                        e.wait_ge(d_lo, n + c + 1)
                        if h == 0 and not (first and j == 0):
                            e.wait_ge(y_ev, oc + v - 1)
                        for k in range(FH):
                            kk = FH * h + k
                            if first and v == 0 and kk % 2 == 0:
                                e.wait_ge(gg_lo, FH * j + kk // 2 + 1)
                            r, m = (FH * j + kk // 2) % RING, kk % 2
                            e.matmul(PS[:, v, 0:BW], DH[:, h, k], GH[:, r, m], start=(kk == 0), stop=False)
                            e.matmul(PS[:, v, 0:BW], DH[:, h, k], GL[:, r, m], start=False, stop=False)
                            e.matmul(PS[:, v, 0:BW], DL[:, h, k], GH[:, r, m], start=False, stop=(kk == FC - 1))\
                                .then_inc(dk, 1)
                        if c == 0 and not (first and j == 0):
                            turn_sum(oc - 1, 1)
                        if c == 2:
                            turn_sum(oc, 0)

                pe_pair(0, True)
                with e.Fori(1, 4) as i:
                    pe_pair(i)
            turn_sum(8 * NB - 1, 1)




_OUTS = [
    ("y_prompt", (1, SEQ, DM)), ("y_sample", (NS, 1, DM)),
    ("k_prompt", (1, 1, TPR, NH, HD)), ("v_prompt", (1, 1, TPR, NH, HD)), ("logf_prompt", (1, 1, TPR, NH)),
    ("rnn_h_prompt", (1, 1, DRNN)), ("rnn_conv_prompt", (1, 1, 3, DRNN)), ("ffn_conv_prompt", (1, 1, 2, DFF)),
    ("k_sample", (1, NS, 1, NH, HD)), ("v_sample", (1, NS, 1, NH, HD)), ("logf_sample", (1, NS, 1, NH)),
    ("rnn_h_sample", (1, NS, DRNN)), ("rnn_conv_sample", (1, NS, 3, DRNN)), ("ffn_conv_sample", (1, NS, 2, DFF)),
]


def chunked(w):
    rows, columns = w.shape
    return w.reshape(rows // P, P, columns // P, P).transpose(2, 1, 0, 3)


def lay_out(x):
    x = {k: np.asarray(v) for k, v in x.items()}
    w = x["w_in"][0]
    main = np.concatenate([w[:, :C_F], w[:, C_XR:]], axis=1)
    forget = np.concatenate([w[:, C_F:C_XR], np.zeros((DM, P - NH), w.dtype)], axis=1)
    c = chunked(main)
    order = [c[12 + i // 2 + 4 * (i % 2)] for i in range(8)] + [chunked(forget)[0]]
    order += [c[4 * m + i] for i in range(4) for m in range(3)]
    o = {}
    o["w_stream"] = np.stack(order)
    o["w_out"] = chunked(x["w_out"][0])
    up = chunked(x["w_ffn_up"][0])
    o["w_up"] = np.stack([up[:FC], up[FC:]], axis=1)
    down = chunked(x["w_ffn_down"][0])
    o["w_down"] = down.reshape(KC, P, 2, FC // 2, P).transpose(0, 2, 1, 3, 4)
    o["norm_mix"] = x["norm_mix"]
    o["norm_final"] = x["norm_final"][None]
    o["gains"] = np.concatenate([x["norm_att_out"][0], x["norm_rnn_out"][0], x["norm_ffn"][0]]).reshape(16, P).T
    rows = [x["rnn_conv_w"][0][j] for j in range(4)]
    rows += [x["rnn_conv_b"][0], x["b_rg_a"][0], x["b_rg_x"][0], x["rg_lambda"][0]]
    o["rnn_table"] = np.stack(rows).reshape(8, 4, P).transpose(2, 1, 0)
    o["rnn_state"] = x["state_rnn_conv"][0].reshape(NS, 3, 4, P).transpose(3, 2, 1, 0)
    o["rnn_h"] = x["state_rnn_h"][0].reshape(NS, 4, P).transpose(2, 1, 0)
    rows = [x["ffn_conv_w"][0][j] for j in range(3)] + [x["ffn_conv_b"][0]]
    o["ffn_table"] = np.stack(rows).reshape(4, FC, P).transpose(2, 1, 0)
    o["ffn_state"] = x["state_ffn_conv"][0].reshape(NS, 2, FC, P).transpose(3, 2, 1, 0)
    o["page_table"] = x["page_table"].reshape(1, NPG)
    o["page_column"] = x["page_table"].reshape(2, P).T
    for k in ("x_prompt", "x_sample", "meta_tokens", "b_forget", "w_rg_a", "w_rg_x", "cache_k", "cache_v",
              "cache_logf", "state_rnn_conv", "state_ffn_conv"):
        o[k] = x[k]
    return {k: np.ascontiguousarray(v) for k, v in o.items()}


def kernel(**inputs):
    import concourse.bacc as bacc
    from concourse.bass_utils import run_bass_kernel_spmd

    nc = bacc.Bacc("TRN2", target_bir_lowering=False, num_devices=1)
    arrays, args, outs = {}, {}, {}
    for name, v in lay_out(inputs).items():
        arrays["in_" + name] = v
        args[name] = nc.dram_tensor("in_" + name, v.shape, mybir.dt.from_np(v.dtype), kind="ExternalInput").ap()
    for name, shape in _OUTS:
        outs[name] = nc.dram_tensor("out_" + name, shape, F32, kind="ExternalOutput").ap()
    build(nc, args, outs)
    r = run_bass_kernel_spmd(nc, [arrays], core_ids=[0])
    return tuple(r.results[0]["out_" + name] for name, _ in _OUTS)
```

```python
from contextlib import ExitStack

import numpy as np
import concourse.bass as bass
from concourse import mybir

F32 = mybir.dt.float32
F32R = mybir.dt.float32r
BF16 = mybir.dt.bfloat16
I32 = mybir.dt.int32
ALU = mybir.AluOpType
ACT = mybir.ActivationFunctionType
AX = mybir.AxisListType

P = 128
DM = 1024
KC = DM // P
DATT = 512
DRNN = 512
NH = 8
HD = 64
DFF = 2816
FC = DFF // P
FH = FC // 2
RING = 16
NMETA = 16
SEQ = 2048
TPR = NMETA + SEQ
NS = 8
TP = 2080
NB = 5
BW = TP // NB
NT = 17
TAIL = TP - (NT - 1) * P
HB = BW // 2
LASTP = TPR - (NB - 1) * BW
PAGES = 32
NPG = NS * PAGES
NIN = 21
EPS = 1e-6
C_K = DATT
C_V = 2 * DATT
C_F = 3 * DATT
C_XR = C_F + NH
C_GR = C_XR + DRNN
BIG = -1e30


class Steps:

    def __init__(self, eng, sem):
        self.eng, self.sem, self.base, self.k = eng, sem, 0, 0

    def inc(self, ins):
        ins.then_inc(self.sem, 1)
        self.k += 1

    def settle(self):
        self.eng.wait_ge(self.sem, self.base + self.k)

    def start(self, i, per):
        self.at, self.per, self.base = self.base + self.k, per, self.base + self.k + i * per
        self.k = 0

    def stop(self, turns):
        assert self.k == self.per, (self.k, self.per)
        self.base, self.k = self.at + turns * self.per, 0


def seg(j):
    return [(0, P), (P, P), (2 * P, P), (3 * P, BW - 3 * P)]


def cols(j, w=BW):
    return slice(j * w, (j + 1) * w)


def score_tiles():
    found = []
    for j in range(NB):
        end = min((j + 1) * BW, TPR)
        for kt in range((end + P - 1) // P):
            q0 = max(j * BW, kt * P)
            found.append((j, kt, q0, end - q0, min(P, TPR - kt * P)))
    return found


def max_pieces():
    found = []
    for qt in range(NT):
        keys = min((qt + 1) * P, TPR)
        for pc in range((keys + 511) // 512):
            n = min(512, keys - 512 * pc)
            found.append((qt, pc, 512 * pc, n, min(P, TP - qt * P), 512 * pc + n == keys))
    return found


TILES = score_tiles()
PIECES = max_pieces()
ENDS = [max(t for t, tile in enumerate(TILES) if tile[0] == j) for j in range(NB)]


def attention_plan(first, last):
    plan = [[] for _ in TILES]
    for n, at in ((0, (0, 2, 3)), (1, (45, 47, 48))):
        if n == 0 and not first or n == 1 and last:
            for t, step in zip(at, ("divide", "columns", "keep")):
                plan[t].append((step, n))
    for j in range(NB - 1):
        plan[ENDS[j] + 5].append(("store", j))
    if not first:
        plan[4].append(("store last", NB - 1))
    if not last:
        for p in range(len(PIECES)):
            plan[10 + 34 * p // 44].append(("piece", p))
    for j in range(NB - 1):
        plan[ENDS[j] + 1].append(("invert", 2 * j))
        plan[ENDS[j] + 2].append(("invert", 2 * j + 1))
        plan[ENDS[j] + 3].append(("times", j))
    plan[-1] += [("invert", 2 * NB - 2), ("invert", 2 * NB - 1), ("times", NB - 1)]
    for g in range(PAGES // 2):
        if first:
            plan[6 + g].append(("products", g))
            plan[6 + g].append(("scores", g))
            plan[26 + 18 * g // 15].append(("products", 16 + g))
            plan[26 + (18 * g + 9) // 15].append(("scores", 16 + g))
            plan[27 + 23 * g // 15].append(("pages", g))
        else:
            plan[5 + (37 if last else 43) * g // 15].append(("pages", g))
            if not last:
                plan[4 + 5 * g // 2].append(("products", 16 + g))
                plan[5 + 5 * g // 2].append(("scores", 16 + g))
    if first:
        for t, step in ((22, "end"), (24, "less"), (25, "exps"), (26, "sums")):
            plan[t].append((step, 0))
    if not last:
        for t, step in ((45, "end"), (47, "less"), (48, "exps"), (49, "sums")) if first else \
                ((43, "end"), (45, "less"), (47, "exps"), (48, "sums")):
            plan[t].append((step, 1))
        for g in range(NB):
            plan[45 + g].append(("row", g))
    return plan


PLANS = [attention_plan(True, False), attention_plan(False, False), attention_plan(False, True)]


def build(nc, a, out):
    ctx = ExitStack()
    with ctx:
        def sb(name, shape, dt, stack=ctx):
            return stack.enter_context(nc.sbuf_tensor(name, shape, dt))

        def sem(name):
            return ctx.enter_context(nc.semaphore(name))

        def dram(name, shape):
            return nc.dram_tensor(name, shape, F32, kind="Internal").ap()

        npool = a["cache_k"].shape[1]
        xT = dram("xT", (DM, TP))
        qT = dram("qT", (DATT, TP))
        kT = dram("kT", (DATT, TP))
        decayT = dram("decayT", (2, NH, TP))
        xrT = dram("xrT", (DRNN, TP))
        grT = dram("grT", (DRNN, TP))
        mixT = dram("mixT", (DM, TP))
        x2T = dram("x2T", (DM, TP))
        gT = dram("gT", (DFF, TP))
        qrow = dram("qrow", (NS, DATT))

        identF = sb("identF", [P, P], F32)
        identB = sb("identB", [P, P], BF16)
        maskQ = sb("maskQ", [P, P], BF16)
        maskK = sb("maskK", [P, P], BF16)
        onesF = sb("onesF", [P, P], F32)
        triu = sb("triu", [P, P], F32)
        epsT = sb("epsT", [P, 1], F32)
        gains = sb("gains", [P, 2 * KC], F32)
        rtab = sb("rtab", [P, 4, 8], F32)
        rstate = sb("rstate", [P, 4, 3, NS], F32)
        rh0 = sb("rh0", [P, 4, 16], F32)
        bf = sb("bf", [NH, 1], F32)
        hb = sb("hb", [P, 4, 2], F32)
        sp = sb("sp", [P, 4, 8], F32)
        attS = sb("attS", [P, 4, 16], F32)

        m1 = ExitStack()
        XH = sb("XH", [P, KC, TP], F32R, m1)
        XL = sb("XL", [P, KC, TP], F32R, m1)
        WR = sb("WR", [P, 2, KC, P], F32, m1)
        WH = sb("WH", [P, 2, KC, P], F32R, m1)
        WL = sb("WL", [P, 2, KC, P], F32R, m1)
        m0 = ExitStack()
        xin = sb("xin", [P, 2, DM], F32, m0)
        hn = sb("hn", [P, 2, DM], F32, m0)
        xst = sb("xst", [P, 2, KC, P], F32, m0)
        sqj = sb("sqj", [P, DM], F32, m0)
        gmix = sb("gmix", [P, DM], F32, m0)
        st0 = sb("st0", [P, 2, 4], F32, m0)
        m0.close()
        ZS = sb("ZS", [P, NB, BW], F32, m1)
        TS = sb("TS", [P, 2, 4, P], F32, m1)
        RX = sb("RX", [P, TP + 3], F32, m1)
        RC = sb("RC", [P, TP], F32, m1)
        RW = sb("RW", [P, TP], F32, m1)
        RA = sb("RA", [P, TP], F32, m1)
        gw = sb("gw", [P, 2, P], F32, m1)
        m1f = ExitStack()
        FL, FE, FT, FW = (sb(n, [P, NT, NH], F32, m1f) for n in ("FL", "FE", "FT", "FW"))
        FD = sb("FD", [P, NT, 2 * NH], F32, m1f)
        m1f.close()
        RT = sb("RT", [P, 2, BW], F32, m1)
        m1.close()

        m2 = ExitStack()
        QA = sb("QA", [P, 2, TP], F32R, m2)
        QB = sb("QB", [P, 2, TP], F32R, m2)
        KA = sb("KA", [P, 2, TP], F32R, m2)
        KB = sb("KB", [P, 2, TP], F32R, m2)
        Qst = sb("Qst", [P, TP], F32, m2)
        Kst = sb("Kst", [P, TP], F32, m2)
        Kst2 = sb("Kst2", [P, TP], F32, m2)
        VA = sb("VA", [P, 2, NT, P], F32, m2)
        PT = sb("PT", [P, 3, BW], F32, m2)
        AO = sb("AO", [P, 2, BW], F32, m2)
        rden = sb("rden", [P, BW], F32, m2)
        MP = sb("MP", [P, NT, NB], F32, m2)
        MX = sb("MX", [P, NT], F32, m2)
        NM = sb("NM", [P, NT, 66], F32, m2)
        Kpg = sb("Kpg", [P, 4, 2, DATT], F32, m2)
        Vpg = sb("Vpg", [P, 4, 2, DATT], F32, m2)
        prod = sb("prod", [P, 2, 2, DATT], F32, m2)
        cb = sb("cb", [P, NPG, NH], F32, m2)
        cnew = sb("cnew", [P, NS, NH], F32, m2)
        ctot = Kpg[:, 0:2].rearrange("p a b n -> p (a b n)")
        cwith = Kpg[:, 2:4].rearrange("p a b n -> p (a b n)")
        segm = Vpg[:, 0:2].rearrange("p a b n -> p (a b n)")
        xtp = Vpg[:, 2].rearrange("p b n -> p (b n)")
        lpage = prod[:, :, :, :].rearrange("p a b n -> p a (b n)")
        qb = sb("qb", [P, 2, DATT], F32, m2)
        knb = sb("knb", [P, 2, DATT], F32, m2)
        vnew = sb("vnew", [1, 2, DATT], F32, m2)
        sc = sb("sc", [P, 2, PAGES, NH], F32, m2)
        sn = sb("sn", [P, 2, NH], F32, m2)
        mloc = sb("mloc", [P, 2, NH], F32, m2)
        mall = sb("mall", [P, 2, NH], F32, m2)
        dsum = sb("dsum", [P, 2, NH], F32, m2)
        headmask = sb("headmask", [NH, DATT], F32, m2)
        od = sb("od", [NH, DATT], F32, m2)
        dinv = sb("dinv", [NH, 1], F32, m2)
        pgid = sb("pgid", [1, NPG], I32, m2)
        pgcol = sb("pgcol", [P, 2], I32, m2)
        m2.close()

        m3 = ExitStack()
        m3t = ExitStack()
        SQ = sb("SQ", [P, KC, TP], F32, m3t)
        MF = sb("MF", [P, KC, TP], F32, m3t)
        m3t.close()
        MH = sb("MH", [P, KC, TP], F32R, m3)
        ML = sb("ML", [P, KC, TP], F32R, m3)
        VR = sb("VR", [P, 2, KC, P], F32, m3)
        VH = sb("VH", [P, 2, KC, P], F32R, m3)
        VL = sb("VL", [P, 2, KC, P], F32R, m3)
        ftab = sb("ftab", [P, FC, 4], F32, m3)
        fstate = sb("fstate", [P, FC, 2, NS], F32, m3)
        XS = sb("XS", [P, NB, BW], F32, m3)
        m3a = ExitStack()
        NR = sb("NR", [P, 4, KC, HB], F32, m3a)
        NG = sb("NG", [P, 2, 2, HB], F32, m3a)
        m3a.close()
        GP = sb("GP", [P, 2, TP + 2], F32, m3)
        GC = sb("GC", [P, 2, BW], F32, m3)
        GO = sb("GO", [P, 2, BW], F32, m3)
        TT = sb("TT", [TAIL, 2, P], F32, m3)
        m3.close()

        m4 = ExitStack()
        GH = sb("GH", [P, RING, 2, BW], F32R, m4)
        GL = sb("GL", [P, RING, 2, BW], F32R, m4)
        GR = sb("GR", [P, 3, 2, BW], F32, m4)
        DR = sb("DR", [P, 2, FH, P], F32, m4)
        DH = sb("DH", [P, 2, FH, P], F32R, m4)
        DL = sb("DL", [P, 2, FH, P], F32R, m4)
        YX = sb("YX", [P, 2, BW], F32, m4)
        YT = sb("YT", [P, 4, DM], F32, m4)
        ysq = sb("ysq", [P, DM], F32, m4)
        yr = sb("yr", [P, 4], F32, m4)
        gfin = sb("gfin", [P, DM], F32, m4)
        m4.close()

        PS = ctx.enter_context(nc.psum_tensor("PS", [P, 8, 512], F32))

        c_ld = sem("c_ld")
        c_pool = sem("c_pool")
        c_gw = sem("c_gw")
        x_first = sem("x_first")
        x_ld = [sem("x_ld0"), sem("x_ld1")]
        x_pad = sem("x_pad")
        x_last = sem("x_last")
        x_sq = sem("x_sq")
        x_hn = sem("x_hn")
        x_tp = sem("x_tp")
        x_ev = sem("x_ev")
        x_lo = sem("x_lo")
        x_st = [sem("x_st0"), sem("x_st1")]
        a0 = sem("a0")
        d0 = sem("d0")
        w_ld = [sem("w_ld0"), sem("w_ld1")]
        w_hi = sem("w_hi")
        w_lo = sem("w_lo")
        g_mm = sem("g_mm")
        g_ev = sem("g_ev")
        z_st = [sem(f"z_st{j}") for j in range(NB)]
        t_pe = sem("t_pe")
        t_ev = sem("t_ev")
        t_st = [sem("t_st0"), sem("t_st1")]
        l_ax = sem("l_ax")
        l_ex = sem("l_ex")
        f_tp = sem("f_tp")
        f_dv = sem("f_dv")
        f_st = sem("f_st")
        dv = sem("dv")
        r_ld = sem("r_ld")
        r_gw = sem("r_gw")
        r_gl = sem("r_gl")
        r_st = sem("r_st")
        r_ho = sem("r_ho")
        r_conv = sem("r_conv")
        r_gate = sem("r_gate")
        r_act = sem("r_act")
        r_u = sem("r_u")
        r_sc = sem("r_sc")
        r_y = sem("r_y")
        r_h = sem("r_h")
        f_ev = sem("f_ev")
        go = sem("go")
        phase_end = sem("phase_end")
        c_att = sem("c_att")
        c_att2 = sem("c_att2")
        pg_ld = sem("pg_ld")
        lf_ld = sem("lf_ld")
        lf_tp = sem("lf_tp")
        lf_ev = sem("lf_ev")
        lf_dv = sem("lf_dv")
        cb_ok = sem("cb_ok")
        st_ld = sem("st_ld")
        va_ld = [sem("va_ld0"), sem("va_ld1")]
        prep = sem("prep")
        mm_mx = sem("mm_mx")
        mx = sem("mx")
        nm = sem("nm")
        nt = sem("nt")
        na = sem("na")
        sT = sem("sT")
        ex = sem("ex")
        pv = sem("pv")
        rd = sem("rd")
        on = sem("on")
        ao_st = [sem("ao_st0"), sem("ao_st1")]
        kg_ld = [sem(f"kg_ld{s}") for s in range(4)]
        vg_ld = [sem(f"vg_ld{s}") for s in range(4)]
        nw_ld = sem("nw_ld")
        kp = sem("kp")
        kpp = sem("kpp")
        kd = sem("kd")
        kf = sem("kf")
        mr = sem("mr")
        de = sem("de")
        dn = sem("dn")
        vd = sem("vd")
        df = sem("df")
        od_s = sem("od_s")
        av = sem("av")
        at_s = sem("at_s")
        kq = sem("kq")
        lf_pg = sem("lf_pg")
        nr_ld = [sem(f"nr_ld{s}") for s in range(4)]
        na_s = sem("na_s")
        nsq = sem("nsq")
        nmm = sem("nmm")
        nrs = sem("nrs")
        nrc = sem("nrc")
        nst = sem("nst")
        nhi = sem("nhi")
        nlo = sem("nlo")
        v_ld = [sem("v_ld0"), sem("v_ld1")]
        v_gn = sem("v_gn")
        v_hi = sem("v_hi")
        v_lo = sem("v_lo")
        u_mm = sem("u_mm")
        u_ev = sem("u_ev")
        xs_ld = [sem(f"xs_ld{j}") for j in range(NB)]
        xs_st = [sem(f"xs_st{j}") for j in range(NB)]
        gcv = sem("gcv")
        gge = sem("gge")
        go_st = [sem("go_st0"), sem("go_st1")]
        tt_pe = sem("tt_pe")
        tt_ev = sem("tt_ev")
        tt_st = [sem("tt_st0"), sem("tt_st1")]
        nf_ld = sem("nf_ld")
        dr_ld = [sem("dr_ld0"), sem("dr_ld1")]
        d_hi = sem("d_hi")
        d_lo = sem("d_lo")
        dk = sem("dk")
        gr_ld = [sem(f"gr_ld{s}") for s in range(3)]
        gg_hi = sem("gg_hi")
        gg_lo = sem("gg_lo")
        yx_ld = [sem("yx_ld0"), sem("yx_ld1")]
        y_ev = sem("y_ev")
        y_tp = sem("y_tp")
        y_tk = sem("y_tk")
        y_sq = sem("y_sq")
        y_rc = sem("y_rc")
        y_nm = sem("y_nm")
        y_st = sem("y_st")

        block = ctx.enter_context(nc.Block())
        @block.sync
        def _(e):
            for s in (*x_st, *t_st, *z_st, r_st, r_gate, r_act, r_ho, r_y, t_pe, t_ev, pv, kf, df, vd, mr, *ao_st, od_s,
                      at_s, *tt_st, tt_ev, *go_st, gcv, tt_pe, y_tp, y_tk):
                e.sem_inc(s, 1)

            e.dma_start(xin[0:NMETA, 0], a["meta_tokens"]).then_inc(x_first, 16)
            e.dma_start(xin[NMETA:P, 0], a["x_prompt"][0][0:P - NMETA, :]).then_inc(x_ld[0], 16)
            e.dma_start(xin[:, 1], a["x_prompt"][0][P - NMETA:2 * P - NMETA, :]).then_inc(x_ld[1], 16)
            for u in range(2):
                e.dma_start(WR[:, u], a["w_stream"][u]).then_inc(w_ld[u], 16)
            with e.Fori(0, 7) as i:
                for v in range(2):
                    e.wait_ge(x_tp, 2 * i + v + 1)
                    e.dma_start(xin[:, v], a["x_prompt"][0][bass.ds((2 * i + 2 + v) * P - NMETA, P), :])\
                        .then_inc(x_ld[v], 16)
            e.wait_ge(x_pad, 1)
            e.dma_start(xin[0:NMETA, 0], a["x_prompt"][0][SEQ - NMETA:SEQ, :]).then_inc(x_ld[0], 16)
            e.dma_start(xin[NMETA:NMETA + NS, 0], a["x_sample"][:, 0, :]).then_inc(x_last, 16)

            with e.Fori(1, 10) as i:
                for u in range(2):
                    e.wait_ge(w_lo, 2 * i + u - 1)
                    e.dma_start(WR[:, u], a["w_stream"][2 * i + u]).then_inc(w_ld[u], 16)
            e.wait_ge(w_lo, NIN - 2)
            e.dma_start(WR[:, 0], a["w_stream"][NIN - 1]).then_inc(w_ld[0], 16)
            def fetch_head(h):
                e.dma_start(Qst[0:HD], qT[bass.ds(h * HD, HD), :]).then_inc(st_ld, 16)
                e.dma_start(Qst[HD:P], qT[bass.ds(h * HD, HD), :]).then_inc(st_ld, 16)
                e.dma_start(Kst[0:HD], kT[bass.ds(h * HD, HD), :]).then_inc(st_ld, 16)
                e.dma_start(Kst[HD + 2:HD + 4], decayT[:, h, :] if isinstance(h, int) else
                            decayT[:, bass.ds(h, 1), :].rearrange("a o n -> (a o) n")).then_inc(st_ld, 16)
                e.dma_start(Kst2[0:HD], kT[bass.ds(h * HD, HD), :]).then_inc(st_ld, 16)
                e.dma_start(Kst2[HD:P], kT[bass.ds(h * HD, HD), :]).then_inc(st_ld, 16)

            vrows = out["v_prompt"][0, 0].rearrange("t h d -> t (h d)")

            def fetch_values(h, v):
                e.dma_start(VA[:, v, 0:16, 0:HD], vrows[0:SEQ, bass.ds(h * HD, HD)].rearrange("(t p) d -> p t d", p=P))\
                    .then_inc(va_ld[v], 16)
                e.dma_start(VA[0:NMETA, v, 16, 0:HD], vrows[SEQ:TPR, bass.ds(h * HD, HD)]).then_inc(va_ld[v], 16)

            def fetch_new(s, v):
                one = bass.ds(s, 1)
                e.dma_start(qb[:, v], qrow[one, :].rearrange("o n -> (o n)").partition_broadcast(P)).then_inc(nw_ld, 16)
                e.dma_start(knb[:, v], out["k_sample"][0][one, 0].rearrange("o h d -> (o h d)").partition_broadcast(P))\
                    .then_inc(nw_ld, 16)
                e.dma_start(vnew[:, v], out["v_sample"][0][one, 0].rearrange("o h d -> o (h d)")).then_inc(nw_ld, 16)

            def fetch_pages(cache, dst, done, s, g):
                for m in range(2):
                    page = e.value_load(pgid[0:1, bass.ds(s * PAGES + 2 * g + m, 1)], min_val=0, max_val=npool - 1)
                    e.dma_start(dst[:, g % 4, m], cache[0][bass.ds(page, 1)].rearrange("o p h d -> (o p) (h d)"))\
                        .then_inc(done[g % 4], 16)

            def sync_head(i, u, more):
                if more > 0:
                    e.wait_ge(kf, 4 * i + 1)
                    e.sem_inc(go, 1)
                    e.wait_ge(df, i + 1)
                    e.sem_inc(go, 1)
                    fetch_new(i + 1, 1 - u)
                    e.wait_ge(pv, 51 * i + 1)
                    e.sem_inc(go, 1)
                    fetch_values(i + 1, 1 - u)
                for g in range(PAGES // 2):
                    e.wait_ge(vd, 16 * i + g + 1)
                    e.sem_inc(go, 1)
                    fetch_pages(a["cache_v"], Vpg, vg_ld, i, g)
                    if more > 0:
                        e.wait_ge(kd, 16 * i + 16 + g - 3)
                        e.sem_inc(go, 1)
                        fetch_pages(a["cache_k"], Kpg, kg_ld, i + 1, g)
                    if more > 1 and g == 11:
                        e.wait_ge(prep, 7 * i + 14)
                        e.sem_inc(go, 1)
                        fetch_head(i + 2)

            e.wait_ge(g_mm, 5 * NIN)
            for st in z_st:
                e.wait_ge(st, 128 + 32 + 1)
            e.wait_ge(f_st, 80)
            e.wait_ge(c_att2, 2)
            fetch_head(0)
            e.wait_ge(phase_end, 4)
            e.dma_start(pgcol[:], a["page_column"]).then_inc(pg_ld, 16)
            e.dma_start(pgid[:], a["page_table"]).then_inc(pg_ld, 16)
            e.dma_start(cnew[:].rearrange("p s h -> p (s h)"),
                        out["logf_sample"][0, :, 0].rearrange("s h -> (s h)").partition_broadcast(P)).then_inc(lf_ld, 16)
            e.wait_ge(c_att, 1)
            fetch_values(0, 0)
            fetch_new(0, 0)
            e.sem_inc(vd, 3)
            e.wait_ge(prep, 7)
            fetch_head(1)
            e.wait_ge(pg_ld, 32)
            e.wait_ge(cb_ok, 1)
            for g in range(PAGES // 2):
                if g >= 4:
                    e.wait_ge(kd, g - 3)
                fetch_pages(a["cache_k"], Kpg, kg_ld, 0, g)
            sync_head(0, 0, 2)
            with e.Fori(0, 2) as ii:
                for v in range(2):
                    sync_head(2 * ii + 1 + v, 1 - v, 2)
            sync_head(5, 1, 2)
            sync_head(6, 0, 1)
            sync_head(7, 1, 0)
            e.wait_ge(phase_end, 8)

            def fetch_v(m, u):
                src = a["w_out"][m] if m < 8 else a["w_up"][(m - 8) // 2, m % 2]
                e.dma_start(VR[:, u], src).then_inc(v_ld[u], 16)

            def fetch_norm(n):
                b, s = n % 10, n % 4
                if n >= 4:
                    e.wait_ge(nst, n - 3)
                src = (x2T if n >= 10 else mixT).rearrange("(k p) n -> p k n", p=P)
                if n >= 10:
                    e.wait_ge(xs_st[b // 2], 16 * KC)
                if n == 9:
                    e.dma_start(NR[:, s, 0:4, 0:TPR - 9 * HB], src[:, 0:4, 9 * HB:TPR]).then_inc(nr_ld[s], 16)
                    e.dma_start(NR[:, s, 4:8], src[:, 4:8, 9 * HB:TP]).then_inc(nr_ld[s], 16)
                else:
                    e.dma_start(NR[:, s], src[:, :, cols(b, HB)]).then_inc(nr_ld[s], 16)

            def fetch_residual(m):
                for j in range(NB):
                    e.wait_ge(xs_st[j], 16 * m)
                    e.dma_start(XS[:, j], xT[bass.ds(m * P, P), cols(j)]).then_inc(xs_ld[j], 16)

            fetch_norm(0)
            fetch_v(0, 0)
            fetch_norm(1)
            fetch_norm(2)
            fetch_v(1, 1)
            for j in range(NB):
                e.dma_start(XS[:, j], xT[0:P, cols(j)]).then_inc(xs_ld[j], 16)
            for n in range(3, 10):
                fetch_norm(n)
            e.dma_start(ftab[:], a["ffn_table"]).then_inc(c_ld, 16)
            e.dma_start(fstate[:], a["ffn_state"]).then_inc(c_ld, 16)
            with e.Fori(0, 3) as i:
                for u in range(2):
                    e.wait_ge(v_lo, 2 * i + u + 1)
                    e.dma_start(VR[:, u], a["w_out"][2 * i + u + 2]).then_inc(v_ld[u], 16)
                    fetch_residual(2 * i + u + 1)
            e.wait_ge(v_lo, 7)
            fetch_v(8, 0)
            fetch_residual(7)
            e.wait_ge(v_lo, 8)
            fetch_v(9, 1)
            for n in range(10, 20):
                fetch_norm(n)
            with e.Fori(1, FC) as f:
                for u in range(2):
                    e.wait_ge(v_lo, 2 * f + 7 + u)
                    e.dma_start(VR[:, u], a["w_up"][f, u]).then_inc(v_ld[u], 16)
            e.wait_ge(phase_end, 12)

            def fetch_down(n, oc, h):
                if not (isinstance(n, int) and n < 2):
                    e.wait_ge(d_lo, n - 1)
                e.dma_start(DR[:, h], a["w_down"][oc, h]).then_inc(dr_ld[h], 16)

            def fetch_inner(j, q):
                f = FH * j + q
                if f >= 3:
                    e.wait_ge(gg_lo, f - 2)
                e.dma_start(GR[:, f % 3], gT[2 * q * P:(2 * q + 2) * P, cols(j)].rearrange("(k p) n -> p k n", p=P))\
                    .then_inc(gr_ld[f % 3], 16)

            def fetch_x2(n, oc, j, v):
                if not (isinstance(n, int) and n < 2):
                    e.wait_ge(y_tp, n)
                e.dma_start(YX[:, v], x2T[bass.ds(oc * P, P), cols(j)]).then_inc(yx_ld[v], 16)

            fetch_inner(0, 0)
            fetch_down(0, 0, 0)
            for q in range(1, 3):
                fetch_inner(0, q)
            fetch_down(1, 0, 1)
            fetch_x2(0, 0, 0, 0)
            e.dma_start(gfin[:], a["norm_final"][0].partition_broadcast(P)).then_inc(nf_ld, 16)
            for q in range(3, FH):
                fetch_inner(0, q)
            for j in range(NB):
                def sync_pair(i, last=False):
                    n, oc = 16 * j + 4 * i, 2 * i
                    ahead = not (last and j == NB - 1)
                    fills = {0: (0, 1, 2), 1: (3, 4), 2: (5, 6, 7, 8, 9), 3: (10,)}
                    for c in range(4):
                        if c < 2:
                            fetch_down(n + c + 2, oc + 1, c)
                        elif ahead:
                            fetch_down(n + c + 2, 0 if last else oc + 2, c - 2)
                        if c == 1:
                            fetch_x2(8 * j + oc + 1, oc + 1, j, 1)
                        if c == 3 and ahead:
                            fetch_x2(8 * j + oc + 2, 0 if last else oc + 2, j + 1 if last else j, 0)
                        if last and ahead:
                            for q in fills[c]:
                                fetch_inner(j + 1, q)

                with e.Fori(0, 3) as i:
                    sync_pair(i)
                sync_pair(3, True)

        @block.gpsimd
        def _(e):
            pool = Steps(e, c_pool)
            pool.inc(e.memset(identF[:], 0.0))
            pool.inc(e.memset(epsT[:], EPS))
            pool.settle()
            pool.inc(e.affine_select(out=identF[:], in_=identF[:], compare_op=ALU.not_equal, fill=1.0, base=0,
                                     pattern=[[-1, P]], channel_multiplier=1))
            for m in (identB, maskQ, maskK, onesF, triu, rh0, attS):
                pool.inc(e.memset(m[:], 1.0 if m in (onesF, triu) else 0.0))
            pool.settle()
            pool.inc(e.affine_select(out=identB[:], in_=identB[:], compare_op=ALU.not_equal, fill=1.0, base=0,
                                     pattern=[[-1, P]], channel_multiplier=1))
            pool.inc(e.affine_select(out=maskQ[:], in_=maskQ[:], compare_op=ALU.is_ge, fill=BIG, base=0,
                                     pattern=[[-1, P]], channel_multiplier=1))
            pool.inc(e.affine_select(out=maskK[:], in_=maskK[:], compare_op=ALU.is_ge, fill=BIG, base=0,
                                     pattern=[[1, P]], channel_multiplier=-1))
            pool.inc(e.affine_select(out=triu[:], in_=triu[:], compare_op=ALU.is_ge, fill=0.0, base=0,
                                     pattern=[[1, P]], channel_multiplier=-1))

            def split_w(n, use, u):
                e.wait_ge(w_ld[u], 16 * use + 16)
                if not (isinstance(n, int) and n < 2):
                    e.wait_ge(g_mm, 5 * n - 5)
                e.sem_inc(go, 1)
                e.tensor_copy(WH[:, u], WR[:, u]).then_inc(w_hi, 1)
                e.wait_ge(w_hi, n + 1)
                e.tensor_tensor(WL[:, u], WR[:, u], WH[:, u].bitcast(F32), ALU.subtract).then_inc(w_lo, 1)

            split_w(0, 0, 0)
            split_w(1, 0, 1)
            e.wait_ge(x_tp, 15)
            e.memset(xin[0:TAIL, 0], 0.0).then_inc(x_pad, 1)
            e.wait_ge(x_hn, NT)
            e.wait_ge(x_lo, NT)
            e.wait_ge(x_ev, 2 * NT)
            e.wait_ge(x_st[0], 16 * 9 + 1)
            e.wait_ge(x_st[1], 16 * 8 + 1)
            e.memset(gw[:], 0.0).then_inc(c_gw, 1)
            with e.Fori(1, 10) as i:
                for u in range(2):
                    split_w(2 * i + u, i, u)
            split_w(NIN - 1, 10, 0)
            e.wait_ge(w_lo, NIN)
            e.sem_inc(phase_end, 1)
            e.wait_ge(g_mm, 5 * NIN)
            e.memset(Kst[HD:HD + 4], 1.0).then_inc(c_att2, 1)
            e.memset(QA[HD:HD + 4].bitcast(F32), 1.0).then_inc(c_att2, 1)
            e.wait_ge(c_att2, 2)

            def prepare(i, v, first=0, last=7):
                own = 7 * i
                if first == 0:
                    e.wait_ge(st_ld, 96 * i + 96)
                for n in range(first, last):
                    if not (isinstance(i, int) and i == 0 and n == 0):
                        e.wait_ge(prep, own + n)
                    e.sem_inc(go, 1)
                    if n == 0:
                        e.memset(QA[HD:HD + 2, v].bitcast(F32), 0.0).then_inc(prep, 1)
                    elif n == 1:
                        e.tensor_copy(KA[0:HD + 4, v], Kst[0:HD + 4]).then_inc(prep, 1)
                    elif n == 2:
                        e.tensor_copy(QA[0:HD, v], Qst[0:HD]).then_inc(prep, 1)
                    elif n == 3:
                        e.tensor_copy(QB[:, v], Qst[:]).then_inc(prep, 1)
                    elif n == 4:
                        e.tensor_copy(KB[:, v], Kst2[:]).then_inc(prep, 1)
                    elif n == 5:
                        e.tensor_tensor(QB[0:HD, v], Qst[0:HD], QB[0:HD, v].bitcast(F32), ALU.subtract).then_inc(prep, 1)
                    else:
                        e.tensor_tensor(KB[HD:P, v], Kst2[HD:P], KB[HD:P, v].bitcast(F32), ALU.subtract)\
                            .then_inc(prep, 1)

            def pool_products(s, v):
                for g in range(8, 16):
                    e.wait_ge(kg_ld[g % 4], 32 * (4 * s + g // 4) + 32)
                    e.wait_ge(nw_ld, 48 * s + 48)
                    e.wait_ge(kd, 16 * s + g - 1)
                    if g > 8:
                        e.wait_ge(kpp, 8 * s + g - 16)
                    e.sem_inc(go, 1)
                    e.tensor_tensor(prod[:, g % 2], Kpg[:, g % 4], qb[:, v].unsqueeze(1).to_broadcast([P, 2, DATT]),
                                    ALU.mult).then_inc(kpp, 1)

            def sample_max(s, v):
                e.wait_ge(kf, 4 * s + 4)
                if isinstance(s, int) and s == 0:
                    e.wait_ge(prep, 14)
                else:
                    e.wait_ge(kpp, 8 * s)
                e.sem_inc(go, 1)
                e.partition_all_reduce(mall[:, v], mloc[:, v], P, bass.bass_isa.ReduceOp.max).then_inc(mr, 1)

            prepare(0, 0, 0, 1)
            e.wait_ge(phase_end, 4)
            e.memset(headmask[:], 1.0).then_inc(c_att2, 1)
            e.wait_ge(pg_ld, 32)
            for g in range(2):
                e.indirect_dma_start(out=lpage[:, g], out_offset=None,
                                     in_=a["cache_logf"][0].rearrange("n p h -> n (p h)"),
                                     in_offset=bass.IndirectOffsetOnAxis(ap=pgcol[:, g:g + 1], axis=0))\
                    .then_inc(lf_pg, 16)
            e.wait_ge(c_att2, 3)
            e.affine_select(out=headmask[:], in_=headmask[:], compare_op=ALU.is_ge, fill=0.0, base=0,
                            pattern=[[1, DATT]], channel_multiplier=-HD).then_inc(c_att2, 1)
            e.wait_ge(c_att2, 4)
            e.affine_select(out=headmask[:], in_=headmask[:], compare_op=ALU.is_ge, fill=0.0, base=HD - 1,
                            pattern=[[-1, DATT]], channel_multiplier=HD).then_inc(c_att2, 1)
            e.wait_ge(lf_pg, 32)
            prepare(0, 0, 3, 7)
            prepare(1, 1)
            sample_max(0, 0)
            e.wait_ge(mr, 2)
            pool_products(1, 1)
            sample_max(1, 1)
            with e.Fori(0, 3) as ii:
                for v in range(2):
                    i = 2 * ii + 1 + v
                    e.wait_ge(mr, i + 2)
                    e.wait_ge(pv, 51 * i + 1)
                    prepare(i + 1, v)
                    e.wait_ge(prep, 7 * i + 14)
                    pool_products(i + 1, v)
                    sample_max(i + 1, v)
            e.wait_ge(mr, NS + 1)
            e.wait_ge(prep, 7 * NH)
            e.sem_inc(phase_end, 1)
            e.wait_ge(phase_end, 8)

            def split_v(m, u, of_out=False):
                e.wait_ge(v_ld[u], 16 * (m // 2) + 16 if isinstance(m, int) else 8 * (m - u) + 16)
                if not (isinstance(m, int) and m < 2):
                    e.wait_ge(u_mm, 5 * m - 5)
                e.sem_inc(go, 1)
                gain = gains[:, 0:KC] if of_out or isinstance(m, int) and m < 8 else gains[:, KC:2 * KC]
                e.tensor_tensor(VR[:, u], VR[:, u], gain.unsqueeze(2).to_broadcast([P, KC, P]), ALU.mult)\
                    .then_inc(v_gn, 1)
                e.wait_ge(v_gn, m + 1)
                e.sem_inc(go, 1)
                e.tensor_copy(VH[:, u], VR[:, u]).then_inc(v_hi, 1)
                e.wait_ge(v_hi, m + 1)
                e.tensor_tensor(VL[:, u], VR[:, u], VH[:, u].bitcast(F32), ALU.subtract).then_inc(v_lo, 1)

            def norm_low(n):
                c = cols(n % 10, HB)
                e.wait_ge(nhi, n + 1)
                e.tensor_tensor(ML[:, :, c], MF[:, :, c], MH[:, :, c].bitcast(F32), ALU.subtract)\
                    .then_inc(nlo, 1)

            split_v(0, 0)
            split_v(1, 1)
            for n in range(10):
                norm_low(n)
            with e.Fori(1, 4) as i:
                for u in range(2):
                    split_v(2 * i + u, u, True)
            split_v(8, 0)
            for n in range(10, 20):
                norm_low(n)
            split_v(9, 1)
            with e.Fori(5, 26) as i:
                for u in range(2):
                    split_v(2 * i + u, u)
            e.wait_ge(nlo, 20)
            e.wait_ge(v_lo, 52)
            e.sem_inc(phase_end, 1)
            e.wait_ge(phase_end, 12)
            with e.Fori(0, 8 * NB) as i:
                for h in range(2):
                    e.wait_ge(d_hi, 2 * i + h + 1)
                    e.tensor_tensor(DL[:, h], DR[:, h], DH[:, h].bitcast(F32), ALU.subtract).then_inc(d_lo, 1)
                    e.wait_ge(d_lo, 2 * i + h + 1)

        @block.scalar
        def _(e):
            for dst, src in (
                (gmix[:], a["norm_mix"][0].partition_broadcast(P)), (gains[:], a["gains"]),
                (rtab[:], a["rnn_table"]), (rstate[:], a["rnn_state"]), (bf[:], a["b_forget"].rearrange("a h -> h a")),
            ):
                e.dma_start(dst, src).then_inc(c_ld, 16)
            act0 = Steps(e, a0)

            def mean_square(t, u, n, rows=P):
                e.wait_ge(x_ld[u], n)
                act0.inc(e.activation(sqj[0:rows], xin[0:rows, u], ACT.Square, accum_out=st0[0:rows, u, 0:1]))
                act0.settle()
                e.activation(st0[0:rows, u, 1:2], st0[0:rows, u, 0:1], ACT.Sqrt, bias=epsT[0:rows],
                             scale=1.0 / DM).then_inc(x_sq, 1)

            def empty(t, u, st, rows=P):
                e.wait_ge(x_tp, t + 1)
                e.wait_ge(x_st[u], st + 1)
                raw = PS[:, 4 * u:4 * u + 2, :].rearrange("p a (k n) -> p (a k) n", n=P)
                nrm = PS[:, 4 * u + 2:4 * u + 4, :].rearrange("p a (k n) -> p (a k) n", n=P)
                e.activation(xst[:, u, :, 0:rows], raw[:, :, 0:rows], ACT.Copy).then_inc(x_ev, 1)
                e.activation(XH[:, :, bass.ds(t * P, rows)], nrm[:, :, 0:rows], ACT.Copy).then_inc(x_ev, 1)
                e.wait_ge(x_ev, 2 * t + 1)
                e.dma_start(xT.rearrange("(k p) n -> p k n", p=P)[:, :, bass.ds(t * P, rows)],
                            xst[:, u, :, 0:rows]).then_inc(x_st[u], 16)

            e.wait_ge(c_pool, 3)
            e.wait_ge(x_first, 16)
            mean_square(0, 0, 16)
            mean_square(1, 1, 16)
            empty(0, 0, 0)
            with e.Fori(0, 7) as i:
                act0.start(i, 2)
                for v in range(2):
                    e.wait_ge(x_hn, 2 * i + v + 1)
                    mean_square(2 * i + 2 + v, v, 16 * i + 32)
                    empty(2 * i + 1 + v, 1 - v, 16 * (i + v))
                act0.stop(7)
            e.wait_ge(x_last, 16)
            e.wait_ge(x_hn, 15)
            mean_square(16, 0, 16 * 9, TAIL)
            empty(15, 1, 16 * 7)
            empty(16, 0, 16 * 8, TAIL)
            e.wait_ge(c_pool, 14)
            e.dma_start(rh0[:, :, 0:NS], a["rnn_h"]).then_inc(c_ld, 16)
            e.wait_ge(l_ax, 1)
            e.activation(sp[:, :, 2], sp[:, :, 1], ACT.Exp, scale=-1.0).then_inc(l_ex, 1)

            def store_block(n, j, dst, done):
                e.wait_ge(g_ev, 5 * n + j + 6)
                e.dma_start(dst[:, cols(j)], ZS[:, j]).then_inc(done[j], 16)

            def take_tail(ev, slot, stored):
                e.wait_ge(t_pe, ev + 2)
                e.wait_ge(t_st[slot], stored + 1)
                e.activation(TS[0:TAIL, slot, 0], PS[0:TAIL, 5, 0:P], ACT.Copy).then_inc(t_ev, 1)
                e.wait_ge(t_ev, ev + 2)

            with e.Fori(0, 4) as c:
                for j in range(NB):
                    store_block(2 * c, j, xrT[bass.ds(c * P, P), :], z_st)
                take_tail(c, 0, 32 * c)
                e.dma_start(out["rnn_conv_prompt"][0, 0][:, bass.ds(c * P, P)],
                            TS[NMETA - 3:NMETA, 0, 0]).then_inc(t_st[0], 16)
                e.dma_start(out["rnn_conv_sample"][0][:, 2, bass.ds(c * P, P)],
                            TS[NMETA:NMETA + NS, 0, 0]).then_inc(t_st[0], 16)
                for j in range(NB):
                    store_block(2 * c + 1, j, grT[bass.ds(c * P, P), :], z_st)
            e.dma_start(out["rnn_conv_sample"][0][:, 0:2, :], a["state_rnn_conv"][0][:, 1:3, :]).then_inc(f_st, 16)

            e.wait_ge(l_ax, 2)
            e.activation(FE[:], FE[:], ACT.Exp, scale=-1.0).then_inc(l_ex, 1)
            e.wait_ge(f_dv, 2)
            lp = out["logf_prompt"][0, 0]
            e.dma_start(lp[0:SEQ, :].rearrange("(t p) h -> p t h", p=P), FL[:, 0:16]).then_inc(f_st, 16)
            e.dma_start(lp[SEQ:TPR, :], FL[0:NMETA, 16]).then_inc(f_st, 16)
            e.dma_start(out["logf_sample"][0, :, 0, :], FL[NMETA:NMETA + NS, 16]).then_inc(f_st, 16)
            e.wait_ge(f_dv, 4)
            e.dma_start(decayT.rearrange("a h n -> (a h) n"), RX[0:16, 3:3 + TP]).then_inc(f_st, 16)
            e.wait_ge(f_st, 80)

            for s in z_st:
                e.wait_ge(s, 16 * 8 + 1)
            full_k = [out["k_prompt"][0, 0].rearrange("t h d -> t (h d)"), out["v_prompt"][0, 0].rearrange("t h d -> t (h d)")]
            one_k = [out["k_sample"][0, :, 0].rearrange("s h d -> s (h d)"), out["v_sample"][0, :, 0].rearrange("s h d -> s (h d)")]

            def take_rows(ev, slot, stored, j, kv, c):
                e.wait_ge(t_pe, ev + 2)
                e.wait_ge(t_st[slot], stored + 1)
                e.activation(TS[:, slot, 0:3], PS[:, 5, 0:3 * P].rearrange("p (m n) -> p m n", n=P), ACT.Copy)
                e.activation(TS[0:TAIL, slot, 3], PS[0:TAIL, 5, 3 * P:4 * P], ACT.Copy).then_inc(t_ev, 1)
                e.wait_ge(t_ev, ev + 2)
                rows, f = full_k[kv], bass.ds(c * P, P)
                e.dma_start(rows[j * BW:j * BW + 3 * P, f].rearrange("(m p) n -> p m n", p=P),
                            TS[:, slot, 0:3]).then_inc(t_st[slot], 16)
                r0 = j * BW + 3 * P
                n = min(TAIL, TPR - r0)
                e.dma_start(rows[r0:r0 + n, f], TS[0:n, slot, 3]).then_inc(t_st[slot], 16)
                if j == NB - 1:
                    e.dma_start(one_k[kv][:, f], TS[NMETA:NMETA + NS, slot, 3]).then_inc(t_st[slot], 16)

            with e.Fori(0, 2) as i:
                plan = []
                count = [0, 0]
                for v in range(22):
                    m = v % 11
                    plan.append((v % 2, count[v % 2]))
                    count[v % 2] += 16 * (1 if m == 0 else 3 if m in (5, 10) else 2)
                for u in range(2):
                    c = 2 * i + u
                    n = 9 + 3 * c
                    e.wait_ge(r_st, 16 * c + 1)
                    e.dma_start(RX[:, 3:3 + TP], xrT[bass.ds(c * P, P), :]).then_inc(r_ld, 16)
                    e.wait_ge(r_gate, 5 * c + 1)
                    e.wait_ge(c_gw, 1)
                    for g, w in enumerate((a["w_rg_a"], a["w_rg_x"])):
                        for b in range(2):
                            e.dma_start(gw[64 * b:64 * b + 64, g, 64 * b:64 * b + 64], w[0][2 * c + b])\
                                .then_inc(r_gw, 16)

                    def event(m):
                        slot, before = plan[11 * u + m]
                        return 4 + 22 * i + 11 * u + m, slot, (128 if slot == 0 else 0) + count[slot] * i + before

                    for j in range(NB):
                        store_block(n, j, qT[bass.ds(c * P, P), :], z_st)
                    take_tail(*event(0))
                    slot = event(0)[1]
                    e.dma_start(qrow[:, bass.ds(c * P, P)], TS[NMETA:NMETA + NS, slot, 0]).then_inc(t_st[slot], 16)
                    for j in range(NB):
                        store_block(n + 1, j, kT[bass.ds(c * P, P), :], z_st)
                        e.wait_ge(r_gate, 5 * c + j + 2)
                        if j:
                            e.wait_ge(r_u, 5 * c + j)
                        e.sem_inc(go, 1)
                        e.activation(RT[:, 0], PS[:, 7, 0:BW], ACT.Tanh, bias=hb[:, bass.ds(c, 1), 1], scale=0.5)\
                            .then_inc(r_act, 1)
                        e.activation(RT[:, 1], PS[:, 6, 0:BW], ACT.Tanh, bias=hb[:, bass.ds(c, 1), 0], scale=0.5)\
                            .then_inc(r_act, 1)
                        e.wait_ge(r_act, 22 * c + 4 * j + 3)
                        if j == 0:
                            e.wait_ge(r_ho, 32 * c + 1)
                            e.wait_ge(r_y, c + 1)
                        e.sem_inc(go, 1)
                        e.activation(RW[:, cols(j)], RT[:, 1], ACT.Tanh, bias=sp[:, bass.ds(c, 1), 0],
                                     scale=sp[:, bass.ds(c, 1), 0]).then_inc(r_act, 1)
                        e.activation(RA[:, cols(j)], RT[:, 1], ACT.Exp, bias=sp[:, bass.ds(c, 1), 6],
                                     scale=sp[:, bass.ds(c, 1), 6]).then_inc(r_act, 1)
                        take_rows(*event(1 + j), j, 0, c)
                    e.wait_ge(r_u, 5 * c + 5)
                    e.dma_start(RC[:], grT[bass.ds(c * P, P), :]).then_inc(r_gl, 16)
                    e.wait_ge(r_act, 22 * c + 21)
                    e.activation(RW[:], RW[:], ACT.Sqrt, scale=0.25).then_inc(r_act, 1)
                    for j in range(NB):
                        take_rows(*event(6 + j), j, 1, c)
                        if j == 1:
                            e.wait_ge(r_gl, 16 * c + 16)
                            e.activation(RC[:], RC[:], ACT.Gelu_apprx_tanh).then_inc(r_act, 1)
                        if j == 2:
                            e.wait_ge(r_sc, c + 1)
                            e.dma_start(out["rnn_h_prompt"][0].rearrange("o n -> n o")[bass.ds(c * P, P), :],
                                        RW[:, TPR - 1:TPR]).then_inc(r_ho, 16)
                            e.dma_start(out["rnn_h_sample"][0].rearrange("s n -> n s")[bass.ds(c * P, P), :],
                                        RW[:, TPR:TPR + NS], allow_slow_non_contiguous=True).then_inc(r_ho, 16)
                        if j == 3:
                            e.wait_ge(r_y, c + 2)
                            e.dma_start(mixT[bass.ds(DATT + c * P, P), :], RX[:, 3:3 + TP]).then_inc(r_st, 16)
            e.wait_ge(t_st[0], 865)
            e.wait_ge(t_st[1], 737)
            e.wait_ge(r_st, 65)
            e.wait_ge(r_ho, 129)
            for s in z_st:
                e.wait_ge(s, 257)
            e.wait_ge(r_act, 22 * 4 + 1)
            e.wait_ge(t_ev, 49)
            e.sem_inc(phase_end, 1)
            e.wait_ge(c_att2, 2)
            e.wait_ge(st_ld, 96)
            e.activation(KA[0:HD + 4, 0], Kst[0:HD + 4], ACT.Copy).then_inc(prep, 1)
            e.wait_ge(phase_end, 4)
            e.sem_inc(ex, 4)
            for g in range(2):
                for b in range(2):
                    e.wait_ge(lf_tp, 4 * g + b + 1)
                    e.activation(xtp[:, 512 * b:512 * b + 512], PS[:, b, :], ACT.Copy).then_inc(lf_ev, 1)
                for b in range(2):
                    e.wait_ge(lf_tp, 4 * g + b + 3)
                    for m, dst in ((0, cwith), (1, ctot)):
                        view = dst.rearrange("p (h s) -> p h s", h=NH)
                        ins = e.activation(view[:, 4 * b:4 * b + 4, P * g:P * g + P],
                                           PS[:, 4 + 2 * b + m, :].rearrange("p (h s) -> p h s", h=4), ACT.Copy)
                    ins.then_inc(lf_ev, 1)

            def sample_exp(s, v):
                e.wait_ge(kf, 4 * s + 5)
                e.sem_inc(go, 1)
                e.activation(sc[:, v], sc[:, v], ACT.Exp).then_inc(de, 1)
                e.activation(sn[:, v], sn[:, v], ACT.Exp).then_inc(de, 1)

            def maxima_row(i, v, g):
                w = min(512, TP - 512 * g)
                e.wait_ge(nt, 5 * i + g + 1)
                e.activation(QA[HD:HD + 2, v, 512 * g:512 * g + w], PS[HD:HD + 2, 3 - g % 2, 0:w], ACT.Copy)\
                    .then_inc(na, 1)

            for g in range(NB):
                maxima_row(0, 0, g)

            def store_out(i, u, j):
                e.wait_ge(on, 5 * i + j + 6)
                w = BW if j < NB - 1 else LASTP
                e.dma_start(mixT[bass.ds(i * HD, HD), j * BW:j * BW + w], AO[0:HD, (u + j) % 2, 0:w])\
                    .then_inc(ao_st[(u + j) % 2], 16)

            def act_head(i, u, plan):
                for t, (j, kt, q0, n, kr) in enumerate(TILES):
                    e.wait_ge(sT, 51 * i + t + 1)
                    if t >= 3:
                        e.wait_ge(pv, 51 * i + t - 1)
                    e.activation(PT[0:kr, t % 3, 0:n], PS[0:kr, (u + t) % 2, 0:n], ACT.Exp, scale=0.125).then_inc(ex, 1)
                    for what, n in plan[t - 1] if t else ():
                        if what == "row":
                            maxima_row(i + 1, 1 - u, n)
                        if what == "exps":
                            sample_exp(i + n, (u + n) % 2)
                        if what == "store":
                            store_out(i, u, n)
                        if what == "store last":
                            store_out(i - 1, 1 - u, n)

            act_head(0, 0, PLANS[0])
            with e.Fori(0, 3) as ii:
                for v in range(2):
                    act_head(2 * ii + 1 + v, 1 - v, PLANS[1])
            act_head(7, 1, PLANS[2])
            store_out(7, 1, NB - 1)
            e.wait_ge(ao_st[0], 16 * 20 + 1)
            e.wait_ge(ao_st[1], 16 * 20 + 1)
            e.wait_ge(na, 5 * NH)
            e.wait_ge(ex, 51 * NH + 4)
            e.wait_ge(de, 2 * NS)
            e.sem_inc(phase_end, 1)
            e.wait_ge(phase_end, 8)
            def norm_square(n):
                s = n % 4
                e.wait_ge(nr_ld[s], 16 * (n // 4 + 1) + (16 if s == 1 and n >= 9 else 0))
                if n == 9:
                    e.wait_ge(na_s, 1)
                e.activation(SQ[:, :, cols(n % 10, HB)], NR[:, s], ACT.Square).then_inc(nsq, 1)

            def norm_root(n):
                e.wait_ge(nmm, n + 1)
                if n >= 2:
                    e.wait_ge(nst, n - 1)
                parts = 2 if n < 10 else 1
                e.activation(NG[:, n % 2, 0:parts], PS[:, 5 + n % 2, 0:parts * HB].rearrange("p (a n) -> p a n", a=parts),
                             ACT.Sqrt, bias=epsT[:], scale=parts / DM).then_inc(nrs, 1)

            def norm_high(n):
                c = cols(n % 10, HB)
                e.wait_ge(nst, n + 1)
                e.activation(MH[:, :, c], MF[:, :, c], ACT.Copy).then_inc(nhi, 1)

            def store_sum(m, j):
                e.wait_ge(u_ev, 5 * m + j + 6)
                e.dma_start(x2T[bass.ds(m * P, P), cols(j)], XS[:, j]).then_inc(xs_st[j], 16)

            norm_square(0)
            norm_square(1)
            for n in range(10):
                norm_root(n)
                if n:
                    norm_high(n - 1)
                if n < 8:
                    norm_square(n + 2)
            norm_high(9)
            for j in range(NB):
                store_sum(0, j)
            with e.Fori(1, 7) as m:
                for j in range(NB):
                    store_sum(m, j)
            store_sum(7, 0)
            store_sum(7, 1)
            norm_square(10)
            norm_square(11)
            store_sum(7, 2)
            for n in range(10, 20):
                norm_root(n)
                if n > 10:
                    norm_high(n - 1)
                if n < 12:
                    store_sum(7, n - 7)
                if n < 18:
                    norm_square(n + 2)
            norm_high(19)
            def act_up(i, u):
                f = 2 * i + u

                def store_inner(j):
                    e.wait_ge(u_ev, 5 * (9 + 2 * f) + j + 6)
                    e.dma_start(gT[bass.ds(f * P, P), cols(j)], GO[:, (u + j) % 2]).then_inc(go_st[(u + j) % 2], 16)

                for j in range(NB):
                    e.wait_ge(gcv, 5 * f + j + 2)
                    s = (u + j) % 2
                    e.activation(GC[:, s], GC[:, s], ACT.Gelu_apprx_tanh).then_inc(gge, 1)
                    if j == 1:
                        e.wait_ge(tt_pe, f + 2)
                        e.wait_ge(tt_st[u], 32 * i + 1)
                        e.activation(TT[:, u], PS[0:TAIL, 7, 0:P], ACT.Copy).then_inc(tt_ev, 1)
                        e.wait_ge(tt_ev, f + 2)
                        e.dma_start(out["ffn_conv_prompt"][0, 0][:, bass.ds(f * P, P)], TT[NMETA - 2:NMETA, u])\
                            .then_inc(tt_st[u], 16)
                        e.dma_start(out["ffn_conv_sample"][0][:, 1, bass.ds(f * P, P)], TT[NMETA:NMETA + NS, u])\
                            .then_inc(tt_st[u], 16)
                    if j:
                        store_inner(j - 1)
                store_inner(NB - 1)

            e.dma_start(out["ffn_conv_sample"][0][:, 0, :], a["state_ffn_conv"][0][:, 1, :]).then_inc(f_st, 16)
            with e.Fori(0, FC // 2) as i:
                for u in range(2):
                    act_up(i, u)
            for s in go_st:
                e.wait_ge(s, 16 * NB * FC // 2 + 1)
            for s in tt_st:
                e.wait_ge(s, 16 * FC + 1)
            e.wait_ge(f_st, 96)
            e.wait_ge(nhi, 20)
            e.sem_inc(phase_end, 1)
            e.wait_ge(phase_end, 12)
            rows_of = [(m * P, w) for m, w in ((0, P), (1, P), (2, P), (3, TAIL))]

            def split_down(n, h):
                e.wait_ge(dr_ld[h], 8 * (n - h) + 16)
                if not (isinstance(n, int) and n < 2):
                    e.wait_ge(dk, FH * (n - 1))
                e.activation(DH[:, h], DR[:, h], ACT.Copy).then_inc(d_hi, 1)

            def inner_high(j, q):
                f = FH * j + q
                e.wait_ge(gr_ld[f % 3], 16 * (f // 3) + 16)
                if f >= RING:
                    e.wait_ge(dk, 176 * (j - 1) + (FH * 14 + 2 * (q - 5) + 2 if q >= 5 else 0))
                e.activation(GH[:, f % RING], GR[:, f % 3], ACT.Copy).then_inc(gg_hi, 1)

            def take_sum(n, oc, v):
                e.wait_ge(y_tp, n + 2)
                e.sem_inc(go, 1)
                src = PS[:, 4 + v, :].rearrange("p (m n) -> p m n", n=P)
                e.activation(YT[:, 0:3, bass.ds(oc * P, P)], src[:, 0:3], ACT.Copy)
                e.activation(YT[0:TAIL, 3, bass.ds(oc * P, P)], src[0:TAIL, 3], ACT.Copy).then_inc(y_tk, 1)

            yst = Steps(e, y_sq)

            def final_root(j):
                e.wait_ge(y_tk, 8 * j + 9)
                if j:
                    e.wait_ge(y_nm, 4 * j)
                for m, (o, w) in enumerate(rows_of):
                    yst.inc(e.activation(ysq[0:w], YT[0:w, m], ACT.Square, accum_out=yr[0:w, m:m + 1]))
                    yst.settle()
                yst.inc(e.activation(yr[:, 0:3], yr[:, 0:3], ACT.Sqrt, bias=epsT[:], scale=1.0 / DM))
                yst.inc(e.activation(yr[0:TAIL, 3:4], yr[0:TAIL, 3:4], ACT.Sqrt, bias=epsT[0:TAIL], scale=1.0 / DM))

            def final_store(j):
                yp = out["y_prompt"][0]
                for m, (o, w) in enumerate(rows_of):
                    e.wait_ge(y_nm, 4 * j + m + 1)
                    t = j * BW + o - NMETA
                    lo = max(0, -t)
                    hi = min(w, SEQ - t)
                    e.dma_start(yp[t + lo:t + hi, :], YT[lo:hi, m]).then_inc(y_st, 16)
                    if hi < w:
                        e.dma_start(out["y_sample"][:, 0, :], YT[hi:hi + NS, m]).then_inc(y_st, 16)

            split_down(0, 0)
            for q in range(3):
                inner_high(0, q)
            split_down(1, 1)
            for q in range(3, FH):
                inner_high(0, q)
            for j in range(NB):
                def act_pair(i, first=False, last=False):
                    n, oc = 16 * j + 4 * i, 8 * j + 2 * i
                    fills = {0: (0, 1, 2), 1: (3, 4), 2: (5, 6, 7, 8, 9), 3: (10,)}
                    for c in range(4):
                        if not (j == NB - 1 and last and c == 3) and not (j == 0 and first and c == 0):
                            split_down(n + c + 1, (c + 1) % 2)
                        if c == 1 and not (first and j == 0):
                            take_sum(oc - 1, 7 if first else 2 * i - 1, 1)
                            if first:
                                final_root(j - 1)
                        if c == 2 and first and j:
                            final_store(j - 1)
                        if c == 3:
                            if first and j:
                                e.wait_ge(y_st, 64 * j)
                            take_sum(oc, 2 * i, 0)
                        if last and j < NB - 1:
                            for q in fills[c]:
                                inner_high(j + 1, q)

                act_pair(0, first=True)
                with e.Fori(1, 3) as i:
                    act_pair(i)
                act_pair(3, last=True)
            take_sum(8 * NB - 1, 7, 1)
            final_root(NB - 1)
            final_store(NB - 1)
            e.wait_ge(y_st, 64 * NB + 16)

        @block.vector
        def _(e):
            e.wait_ge(c_ld, 16 * 5)

            def normalise(t, u, rows=P):
                e.wait_ge(x_sq, t + 1)
                if not (isinstance(t, int) and t < 2):
                    e.wait_ge(x_tp, t - 1)
                e.reciprocal(st0[0:rows, u, 2:3], st0[0:rows, u, 1:2]).then_inc(d0, 1)
                e.wait_ge(d0, t + 1)
                e.scalar_tensor_tensor(out=hn[0:rows, u], in0=xin[0:rows, u], scalar=st0[0:rows, u, 2:3],
                                       in1=gmix[0:rows], op0=ALU.mult, op1=ALU.mult).then_inc(x_hn, 1)

            def low(t, u, rows=P):
                e.wait_ge(x_ev, 2 * t + 2)
                nrm = PS[:, 4 * u + 2:4 * u + 4, :].rearrange("p a (k n) -> p (a k) n", n=P)
                c = bass.ds(t * P, rows)
                e.tensor_tensor(XL[:, :, c], nrm[:, :, 0:rows], XH[:, :, c].bitcast(F32),
                                ALU.subtract).then_inc(x_lo, 1)

            normalise(0, 0)
            normalise(1, 1)
            low(0, 0)
            with e.Fori(0, 7) as i:
                for v in range(2):
                    normalise(2 * i + 2 + v, v)
                    low(2 * i + 1 + v, 1 - v)
            normalise(16, 0, TAIL)
            low(15, 1)
            low(16, 0, TAIL)
            g_steps = Steps(e, dv)

            def half_log1p(z, t, p):
                g_steps.inc(e.tensor_scalar(t, z, 2.0, None, ALU.add))
                g_steps.settle()
                g_steps.inc(e.reciprocal(t, t))
                g_steps.settle()
                g_steps.inc(e.tensor_tensor(z, z, t, ALU.mult))
                g_steps.settle()
                g_steps.inc(e.tensor_tensor(t, z, z, ALU.mult))
                g_steps.settle()
                g_steps.inc(e.tensor_scalar(p, t, 1.0 / 17, None, ALU.mult))
                for k in (15, 13, 11, 9, 7, 5, 3):
                    g_steps.settle()
                    g_steps.inc(e.scalar_tensor_tensor(out=p, in0=p, scalar=1.0 / k, in1=t, op0=ALU.add, op1=ALU.mult))
                g_steps.settle()
                g_steps.inc(e.scalar_tensor_tensor(out=p, in0=p, scalar=1.0, in1=z, op0=ALU.add, op1=ALU.mult))
                g_steps.settle()

            lam = rtab[:, :, 7]
            e.wait_ge(c_ld, 16 * 6)
            e.scalar_tensor_tensor(out=sp[:, :, 1], in0=lam, scalar=-1.0, in1=lam, op0=ALU.mult, op1=ALU.max)\
                .then_inc(l_ax, 1)
            g_steps.inc(e.tensor_scalar(hb[:], rtab[:, :, 5:7], 0.5, None, ALU.mult))
            e.wait_ge(l_ex, 1)
            half_log1p(sp[:, :, 2], sp[:, :, 3], sp[:, :, 4])
            g_steps.inc(e.tensor_scalar(sp[:, :, 5], lam, -2.0, 0.0, ALU.mult, ALU.max))
            g_steps.settle()
            g_steps.inc(e.scalar_tensor_tensor(out=sp[:, :, 0], in0=sp[:, :, 4], scalar=4.0, in1=sp[:, :, 5],
                                               op0=ALU.mult, op1=ALU.add))
            g_steps.settle()
            g_steps.inc(e.tensor_scalar(sp[:, :, 6], sp[:, :, 0], -2.0, None, ALU.mult))
            for u in range(2):
                e.wait_ge(x_st[u], 16 * (9 - u) + 1)
            e.wait_ge(x_tp, NT)
            g_steps.inc(e.memset(RX[:, 0:3], 0.0))
            e.sem_inc(g_ev, 5)

            def empty_block(n, j):
                e.wait_ge(g_mm, 5 * n + j + 1)
                return e.tensor_copy(ZS[:, j], PS[:, j, 0:BW]).then_inc(g_ev, 1)

            with e.Fori(0, 4) as c:
                for u in range(2):
                    for j in range(NB):
                        e.wait_ge(z_st[j], 32 * c + 16 * u + 1)
                        if u == 1 and j == NB - 1:
                            e.wait_ge(t_pe, c + 2)
                        empty_block(2 * c + u, j)
            for j in range(NB):
                e.wait_ge(g_mm, 40 + j + 1)
                e.tensor_scalar(RX[0:NH, 3 + j * BW:3 + (j + 1) * BW], PS[0:NH, j, 0:BW], bf[:, 0:1], None, ALU.add)\
                    .then_inc(g_ev, 1)
            e.wait_ge(f_tp, 1)
            logit = PS[:, 5, 0:NT * NH].rearrange("p (t h) -> p t h", h=NH)
            g_steps.inc(e.tensor_scalar(FW[:], logit, 0.0, None, ALU.min))
            g_steps.settle()
            e.scalar_tensor_tensor(out=FE[:], in0=FW[:], scalar=-2.0, in1=logit, op0=ALU.mult, op1=ALU.add)\
                .then_inc(l_ax, 1)
            e.wait_ge(l_ax, 2)
            e.sem_inc(f_dv, 1)
            e.wait_ge(l_ex, 2)
            half_log1p(FE[:], FT[:], FL[:])
            e.scalar_tensor_tensor(out=FL[:], in0=FL[:], scalar=-2.0, in1=FW[:], op0=ALU.mult, op1=ALU.add)\
                .then_inc(f_dv, 1)
            e.wait_ge(f_tp, 2)
            within = PS[:, 6, 0:NT * NH].rearrange("p (t h) -> p t h", h=NH)
            total = PS[:, 7, 0:NT * NH].rearrange("p (t h) -> p t h", h=NH)
            g_steps.inc(e.tensor_copy(FT[:], total))
            g_steps.settle()
            g_steps.inc(e.memset(FE[:, 0], 0.0))
            for h in range(NH):
                g_steps.inc(e.tensor_tensor_scan(FE[:, 1:NT, h], onesF[:, 0:NT - 1], FT[:, 0:NT - 1, h], 0.0,
                                                 ALU.mult, ALU.add))
            g_steps.settle()
            g_steps.inc(e.tensor_tensor(FE[:], FE[:], within, ALU.add))
            g_steps.settle()
            hi, lo = FD[:, :, 0:NH], FD[:, :, NH:2 * NH]
            g_steps.inc(e.tensor_scalar(hi.bitcast(F32R), FE[:], -8.0, None, ALU.mult))
            g_steps.settle()
            e.scalar_tensor_tensor(out=lo.bitcast(F32R), in0=FE[:], scalar=-8.0, in1=hi, op0=ALU.mult,
                                   op1=ALU.subtract).then_inc(f_dv, 1)
            for g in range(NB):
                e.wait_ge(f_tp, 3 + g)
                w = min(512, TP - 512 * g)
                e.tensor_copy(RX[0:16, 3 + 512 * g:3 + 512 * g + w], PS[0:16, 5 + g % 3, 0:w]).then_inc(f_ev, 1)
            e.wait_ge(f_ev, NB)
            e.sem_inc(f_dv, 1)
            for s in z_st:
                e.wait_ge(s, 16 * 8 + 1)

            with e.Fori(0, 2) as i:
                g_steps.start(i, 2 * 13)
                for u in range(2):
                    c = 2 * i + u
                    n = 9 + 3 * c
                    ev = 4 + 11 * c
                    one = bass.ds(c, 1)

                    def tap(k):
                        return rtab[:, one, k]

                    x, r, w, al = RX, RC, RW, RA
                    smp = slice(TPR, TPR + NS)
                    for j in range(NB):
                        e.wait_ge(z_st[j], 128 + 32 * c + 1)
                        if j == NB - 1:
                            e.wait_ge(t_pe, ev + 1)
                        else:
                            e.wait_ge(t_pe, ev - (NB - 1) + j + 1)
                        empty_block(n, j)
                        if j == 0:
                            e.wait_ge(r_ld, 16 * c + 16)
                            e.wait_ge(r_act, 22 * c + 1)
                            g_steps.inc(e.tensor_scalar(r[:], x[:, 0:TP], tap(0), tap(4), ALU.mult, ALU.add))
                            g_steps.settle()
                        elif j < 4:
                            g_steps.inc(e.scalar_tensor_tensor(out=r[:], in0=x[:, j:j + TP], scalar=tap(j), in1=r[:],
                                                               op0=ALU.mult, op1=ALU.add))
                            g_steps.settle()
                        else:
                            g_steps.inc(e.tensor_scalar(r[:, smp], rstate[:, one, 0, :].rearrange("p o s -> p (o s)"),
                                                        tap(0), tap(4), ALU.mult, ALU.add))
                            g_steps.settle()
                            for k in (1, 2):
                                g_steps.inc(e.scalar_tensor_tensor(
                                    out=r[:, smp], in0=rstate[:, one, k, :].rearrange("p o s -> p (o s)"),
                                    scalar=tap(k), in1=r[:, smp], op0=ALU.mult, op1=ALU.add))
                                g_steps.settle()
                            e.scalar_tensor_tensor(out=r[:, smp], in0=x[:, 3 + TPR:3 + TPR + NS], scalar=tap(3),
                                                   in1=r[:, smp], op0=ALU.mult, op1=ALU.add).then_inc(r_conv, 1)
                    def times_one_plus_a(j):
                        e.wait_ge(r_act, 22 * c + 4 * j + 5)
                        e.wait_ge(r_u, 5 * c + j + 1)
                        xj = x[:, 3 + j * BW:3 + (j + 1) * BW]
                        g_steps.inc(e.scalar_tensor_tensor(out=xj, in0=al[:, cols(j)], scalar=1.0, in1=xj,
                                                           op0=ALU.add, op1=ALU.mult))

                    for j in range(NB):
                        e.wait_ge(z_st[j], 128 + 32 * c + 17)
                        if j == NB - 1:
                            e.wait_ge(t_pe, ev + 2)
                        empty_block(n + 1, j)
                        e.wait_ge(r_conv, c + 1)
                        e.wait_ge(r_act, 22 * c + 4 * j + 2)
                        e.scalar_tensor_tensor(out=x[:, 3 + j * BW:3 + (j + 1) * BW], in0=RT[:, 0], scalar=1.0,
                                               in1=r[:, cols(j)], op0=ALU.add, op1=ALU.mult).then_inc(r_u, 1)
                        if j:
                            times_one_plus_a(j - 1)
                    for j in range(NB):
                        e.wait_ge(z_st[j], 128 + 32 * c + 33)
                        e.wait_ge(t_pe, ev + 1 + j + 2)
                        empty_block(n + 2, j)
                        if j == 0:
                            times_one_plus_a(NB - 1)
                            e.wait_ge(r_act, 22 * c + 22)
                            g_steps.settle()
                            g_steps.inc(e.tensor_tensor(x[:, 3:3 + TP], x[:, 3:3 + TP], w[:], ALU.mult))
                            g_steps.settle()
                        elif j == 1:
                            e.tensor_tensor_scan(w[:, 0:TPR], al[:, 0:TPR], x[:, 3:3 + TPR], 0.0, ALU.mult, ALU.add)
                            e.tensor_tensor(w[:, TPR:TP], al[:, TPR:TP], rh0[:, one, :].rearrange("p o s -> p (o s)"),
                                            ALU.mult).then_inc(r_h, 1)
                            e.wait_ge(r_h, c + 1)
                            e.tensor_tensor(w[:, TPR:TP], w[:, TPR:TP], x[:, 3 + TPR:3 + TP], ALU.add)\
                                .then_inc(r_sc, 1)
                        elif j == 2:
                            e.wait_ge(r_sc, c + 1)
                            e.wait_ge(r_act, 22 * c + 23)
                            e.tensor_tensor(x[:, 3:3 + TP], w[:], r[:], ALU.mult).then_inc(r_y, 1)
                g_steps.stop(2)
            e.wait_ge(g_ev, 5 * NIN + 5)
            e.wait_ge(r_y, 5)
            e.sem_inc(phase_end, 1)
            e.wait_ge(g_mm, 5 * NIN)
            g_steps.inc(e.memset(MP[:], -3e38))
            g_steps.inc(e.memset(NM[:], 0.0))
            e.wait_ge(st_ld, 96)
            e.tensor_copy(QA[0:HD, 0], Qst[0:HD]).then_inc(prep, 1)
            e.memset(VA[:, :, :, HD:P].rearrange("p a t d -> p (a t) d"), 1.0).then_inc(c_att, 1)
            g_steps.settle()
            e.wait_ge(c_att, 1)

            def piece_max(i, p):
                qt, pc, k0, n, rows, _ = PIECES[p]
                e.wait_ge(mm_mx, 45 * i + p + 1)
                e.tensor_reduce(MP[0:rows, qt, pc:pc + 1], PS[0:rows, 2 + p % 2, 0:n], AX.X, ALU.max).then_inc(mx, 1)
                if p == len(PIECES) - 1:
                    e.wait_ge(mx, 45 * i + 45)
                    e.tensor_reduce(MX[:], MP[:], AX.X, ALU.max).then_inc(nm, 1)
                    e.wait_ge(nm, 3 * i + 1)
                    e.tensor_scalar(NM[:, :, HD].bitcast(F32R), MX[:], -1.0, None, ALU.mult).then_inc(nm, 1)
                    e.wait_ge(nm, 3 * i + 2)
                    e.scalar_tensor_tensor(out=NM[:, :, HD + 1].bitcast(F32R), in0=MX[:], scalar=-1.0, in1=NM[:, :, HD],
                                           op0=ALU.mult, op1=ALU.subtract).then_inc(nm, 1)

            for p in range(len(PIECES)):
                piece_max(0, p)
            e.wait_ge(phase_end, 4)
            g_steps.inc(e.memset(segm, 1.0))
            g_steps.settle()
            g_steps.inc(e.memset(segm.rearrange("p (s g) -> p s g", g=PAGES)[:, :, 0], 0.0))
            g_steps.settle()
            e.sem_inc(on, 5)
            e.wait_ge(lf_ev, 8)
            incl = prod[:].rearrange("p a b n -> p (a b n)")
            g_steps.inc(e.tensor_tensor_scan(incl, segm, ctot, 0.0, ALU.mult, ALU.add))
            g_steps.settle()
            e.wait_ge(lf_ld, 16)
            last = incl.rearrange("p (h s g) -> p s h g", h=NH, g=PAGES)[:, :, :, PAGES - 1]
            g_steps.inc(e.tensor_tensor(cnew[:], cnew[:], last, ALU.add))
            g_steps.settle()
            g_steps.inc(e.tensor_tensor(incl, incl, ctot, ALU.subtract))
            g_steps.settle()
            e.tensor_tensor(cb[:].rearrange("p s h -> p h s"), incl.rearrange("p (h s) -> p h s", h=NH),
                            cwith.rearrange("p (h s) -> p h s", h=NH), ALU.add).then_inc(cb_ok, 1)
            e.wait_ge(cb_ok, 1)

            def page_products(s, v, g):
                e.wait_ge(kg_ld[g % 4], 32 * (4 * s + g // 4) + 32)
                if g == 0:
                    e.wait_ge(nw_ld, 48 * s + 48)
                p = prod[:, g % 2]
                e.tensor_tensor(p, Kpg[:, g % 4], qb[:, v].unsqueeze(1).to_broadcast([P, 2, DATT]), ALU.mult)\
                    .then_inc(kp, 1)

            def page_scores(s, v, g):
                p = prod[:, g % 2]
                if g < 8 or isinstance(s, int) and s == 0:
                    e.wait_ge(kp, 9 * s + g + (1 if isinstance(s, int) and s == 0 else 9))
                else:
                    e.wait_ge(kpp, 8 * s - 8 + g - 7)
                e.tensor_reduce(sc[:, v, 2 * g:2 * g + 2, :], p.rearrange("p b (h d) -> p b h d", d=HD), AX.X, ALU.add)\
                    .then_inc(kd, 1)

            def scores_end(s, v):
                e.wait_ge(kd, 16 * s + 16)
                p = prod[:, 0, 0]
                e.tensor_tensor(p, knb[:, v], qb[:, v], ALU.mult).then_inc(kp, 1)
                e.wait_ge(kp, 9 * s + 17)
                e.tensor_reduce(sn[:, v], p.rearrange("p (h d) -> p h d", d=HD), AX.X, ALU.add).then_inc(kf, 1)
                e.scalar_tensor_tensor(out=sc[:, v], in0=sc[:, v], scalar=0.125, in1=cb[:, bass.ds(s * PAGES, PAGES), :],
                                       op0=ALU.mult, op1=ALU.subtract).then_inc(kf, 1)
                e.wait_ge(kf, 4 * s + 3)
                e.scalar_tensor_tensor(out=sn[:, v], in0=sn[:, v], scalar=0.125,
                                       in1=cnew[:, bass.ds(s, 1), :].rearrange("p o h -> p (o h)"),
                                       op0=ALU.mult, op1=ALU.subtract).then_inc(kq, 1)
                e.tensor_reduce(mloc[:, v], sc[:, v].rearrange("p g h -> p h g"), AX.X, ALU.max).then_inc(kq, 1)
                e.wait_ge(kq, 3 * s + 2)
                e.tensor_tensor(mloc[:, v], mloc[:, v], sn[:, v], ALU.max).then_inc(kf, 1)

            def scores_less(s, v):
                e.wait_ge(mr, s + 2)
                e.tensor_tensor(sc[:, v], sc[:, v], mall[:, v].unsqueeze(1).to_broadcast([P, PAGES, NH]), ALU.subtract)\
                    .then_inc(kq, 1)
                e.tensor_tensor(sn[:, v], sn[:, v], mall[:, v], ALU.subtract).then_inc(kf, 1)

            def sample_sums(s, v):
                e.wait_ge(de, 2 * s + 1)
                e.sem_inc(go, 1)
                e.tensor_reduce(dsum[:, v], sc[:, v].rearrange("p g h -> p h g"), AX.X, ALU.add).then_inc(dn, 1)

            def dve_head(i, u, plan):
                def invert(j, half):
                    w = (BW if j < NB - 1 else LASTP) // 2
                    at = slice(half * w, half * w + w)
                    if half == 0:
                        e.wait_ge(pv, 51 * i + ENDS[j] + 2)
                        e.wait_ge(on, 5 * i + j + 5)
                    e.reciprocal(rden[0:HD, at], PS[HD:P, 4 + (u + j) % 2, at]).then_inc(rd, 1)

                def normalise(j):
                    w = BW if j < NB - 1 else LASTP
                    s = (u + j) % 2
                    e.wait_ge(rd, 10 * i + 2 * j + 2)
                    e.wait_ge(ao_st[s], 40 * (i - u) + 16 * ((5 * u + j) // 2) + 1)
                    e.tensor_tensor(AO[0:HD, s, 0:w], PS[0:HD, 4 + s, 0:w], rden[0:HD, 0:w], ALU.mult).then_inc(on, 1)

                for t in range(len(TILES)):
                    for what, n in plan[t]:
                        v = (u + n) % 2
                        if what == "divide":
                            sample_divide(i - 1 + n)
                        if what == "keep":
                            sample_keep(i - 1 + n)
                        if what == "piece":
                            piece_max(i + 1, n)
                        if what == "products":
                            if n < 24:
                                page_products(i + n // 16, (u + n // 16) % 2, n % 16)
                        if what == "scores":
                            page_scores(i + n // 16, (u + n // 16) % 2, n % 16)
                        if what == "end":
                            scores_end(i + n, v)
                        if what == "less":
                            scores_less(i + n, v)
                        if what == "sums":
                            sample_sums(i + n, v)
                        if what == "invert":
                            invert(n // 2, n % 2)
                        if what == "times":
                            normalise(n)

            def sample_divide(s):
                e.wait_ge(df, s + 2)
                e.reciprocal(dinv[:], PS[0:NH, 6, 0:1]).then_inc(od_s, 1)
                e.wait_ge(od_s, 2 * s + 2)
                e.scalar_tensor_tensor(out=od[:], in0=PS[0:NH, 7, :], scalar=dinv[:, 0:1], in1=headmask[:],
                                       op0=ALU.mult, op1=ALU.mult).then_inc(od_s, 1)

            def sample_keep(s):
                e.wait_ge(av, s + 1)
                e.tensor_copy(attS[:, :, bass.ds(s, 1)], PS[:, 6, 8:12].unsqueeze(2)).then_inc(at_s, 1)

            e.wait_ge(c_att2, 5)
            dve_head(0, 0, PLANS[0])
            with e.Fori(0, 3) as ii:
                for v in range(2):
                    dve_head(2 * ii + 1 + v, 1 - v, PLANS[1])
            dve_head(7, 1, PLANS[2])
            e.wait_ge(at_s, NS + 1)
            e.wait_ge(on, 5 * NH + 5)
            e.wait_ge(kf, 4 * NS + 1)
            e.wait_ge(dn, NS)
            e.wait_ge(nm, 3 * NH)
            e.sem_inc(phase_end, 1)
            e.wait_ge(phase_end, 8)
            e.sem_inc(u_ev, 5)
            def norm_apply(n):
                parts = 2 if n < 10 else 1
                e.wait_ge(nrs, n + 1)
                e.reciprocal(NG[:, n % 2, 0:parts], NG[:, n % 2, 0:parts]).then_inc(nrc, 1)
                e.wait_ge(nrc, n + 1)
                e.tensor_tensor(
                    MF[:, :, cols(n % 10, HB)].rearrange("p (a k) n -> p a k n", a=parts),
                    NR[:, n % 4].rearrange("p (a k) n -> p a k n", a=parts),
                    NG[:, n % 2, 0:parts].unsqueeze(2).to_broadcast([P, parts, KC // parts, HB]), ALU.mult)\
                    .then_inc(nst, 1)

            def add_residual(m, j):
                e.wait_ge(u_mm, 5 * m + j + 1)
                e.wait_ge(xs_ld[j], 16 * m + 16)
                e.tensor_tensor(XS[:, j], XS[:, j], PS[:, j, 0:BW], ALU.add).then_inc(u_ev, 1)

            for n in range(10):
                norm_apply(n)
                if n == 5:
                    e.wait_ge(nst, 6)
                    e.tensor_copy(NR[:, 1, 0:4, TPR - 9 * HB:HB], attS[:]).then_inc(na_s, 1)
            for j in range(NB):
                add_residual(0, j)
            with e.Fori(1, 7) as m:
                for j in range(NB):
                    add_residual(m, j)
            add_residual(7, 0)
            add_residual(7, 1)
            add_residual(7, 2)
            for n in range(10, 20):
                norm_apply(n)
                if n < 12:
                    add_residual(7, n - 7)
            e.wait_ge(nst, 20)
            e.wait_ge(nmm, 20)
            e.wait_ge(nsq, 20)
            e.wait_ge(c_ld, 16 * 8)
            g_steps.inc(e.memset(GP[:, :, 0:2], 0.0))
            g_steps.settle()

            with e.Fori(0, FC // 2) as i:
                g_steps.start(i, 2 * (2 * NB + 3))
                for u in range(2):
                    f = 2 * i + u
                    one = bass.ds(f, 1)

                    def tap(k):
                        return ftab[:, one, k]

                    def state(k):
                        return fstate[:, one, k, :].rearrange("p o s -> p (o s)")

                    def convolve(j):
                        s, o = (u + j) % 2, j * BW
                        d, x = GC[:, s], GP[:, u]
                        if j == 0:
                            e.wait_ge(u_ev, 5 * (8 + 2 * f) + 10)
                        else:
                            e.wait_ge(u_ev, 5 * (9 + 2 * f) + max(j - 2, -1) + 6)
                        g_steps.inc(e.tensor_scalar(d, x[:, o:o + BW], tap(0), tap(3), ALU.mult, ALU.add))
                        g_steps.settle()
                        g_steps.inc(e.scalar_tensor_tensor(out=d, in0=x[:, o + 1:o + 1 + BW], scalar=tap(1), in1=d,
                                                           op0=ALU.mult, op1=ALU.add))
                        g_steps.settle()
                        ins = e.scalar_tensor_tensor(out=d, in0=x[:, o + 2:o + 2 + BW], scalar=tap(2), in1=d,
                                                     op0=ALU.mult, op1=ALU.add)
                        if j == NB - 1:
                            g_steps.inc(ins)
                            d = d[:, LASTP:LASTP + NS]
                            g_steps.settle()
                            g_steps.inc(e.tensor_scalar(d, state(0), tap(0), tap(3), ALU.mult, ALU.add))
                            g_steps.settle()
                            g_steps.inc(e.scalar_tensor_tensor(out=d, in0=state(1), scalar=tap(1), in1=d,
                                                               op0=ALU.mult, op1=ALU.add))
                            g_steps.settle()
                            ins = e.scalar_tensor_tensor(out=d, in0=x[:, 2 + TPR:2 + TPR + NS], scalar=tap(2), in1=d,
                                                         op0=ALU.mult, op1=ALU.add)
                        ins.then_inc(gcv, 1)

                    def multiply(j):
                        s = (u + j) % 2
                        e.wait_ge(u_mm, 5 * (9 + 2 * f) + j + 1)
                        e.wait_ge(gge, 5 * f + j + 1)
                        e.wait_ge(go_st[s], 16 * (5 * i + (5 * u + j) // 2) + 1)
                        e.tensor_tensor(GO[:, s], GC[:, s], PS[:, j, 0:BW], ALU.mult).then_inc(u_ev, 1)

                    for j in range(NB):
                        e.wait_ge(u_mm, 5 * (8 + 2 * f) + j + 1)
                        if j == 0:
                            e.wait_ge(gcv, 5 * f + 1)
                        if j == NB - 1:
                            e.wait_ge(tt_pe, f + 1)
                        e.tensor_copy(GP[:, u, 2 + j * BW:2 + (j + 1) * BW], PS[:, j, 0:BW]).then_inc(u_ev, 1)
                    convolve(0)
                    convolve(1)
                    for j in range(NB):
                        multiply(j)
                        if j + 2 < NB:
                            convolve(j + 2)
                g_steps.stop(FC // 2)
            e.wait_ge(u_ev, 5 * 52 + 5)
            e.wait_ge(gcv, 5 * FC + 1)
            e.sem_inc(phase_end, 1)
            e.wait_ge(phase_end, 12)
            rows_of = [(m * P, w) for m, w in ((0, P), (1, P), (2, P), (3, TAIL))]

            def inner_low(j, q):
                f = FH * j + q
                e.wait_ge(gg_hi, f + 1)
                e.tensor_tensor(GL[:, f % RING], GR[:, f % 3], GH[:, f % RING].bitcast(F32), ALU.subtract)\
                    .then_inc(gg_lo, 1)

            def add_x2(n, v):
                e.wait_ge(dk, 22 * n + 22)
                e.wait_ge(yx_ld[v], 8 * (n - v) + 16)
                e.tensor_tensor(YX[:, v], YX[:, v], PS[:, v, 0:BW], ALU.add).then_inc(y_ev, 1)

            def final_apply(j):
                e.wait_ge(y_sq, 6 * j + 6)
                e.reciprocal(yr[:, 0:3], yr[:, 0:3]).then_inc(y_rc, 1)
                e.reciprocal(yr[0:TAIL, 3:4], yr[0:TAIL, 3:4]).then_inc(y_rc, 1)
                e.wait_ge(y_rc, 2 * j + 2)
                for m, (o, w) in enumerate(rows_of):
                    e.scalar_tensor_tensor(out=YT[0:w, m], in0=YT[0:w, m], scalar=yr[0:w, m:m + 1], in1=gfin[0:w],
                                           op0=ALU.mult, op1=ALU.mult).then_inc(y_nm, 1)

            for q in range(FH):
                inner_low(0, q)
            e.wait_ge(nf_ld, 16)
            for j in range(NB):
                def dve_pair(i, first=False, last=False):
                    oc = 8 * j + 2 * i
                    fills = {0: (0, 1, 2), 1: (3, 4), 2: (5, 6, 7, 8, 9), 3: (10,)}
                    for c in range(4):
                        if last and j < NB - 1:
                            for q in fills[c]:
                                inner_low(j + 1, q)
                        if c == 1:
                            add_x2(oc, 0)
                            if first and j:
                                final_apply(j - 1)
                        if c == 3:
                            add_x2(oc + 1, 1)

                dve_pair(0, first=True)
                with e.Fori(1, 3) as i:
                    dve_pair(i)
                dve_pair(3, last=True)
            final_apply(NB - 1)

        @block.tensor
        def _(e):
            e.wait_ge(c_pool, 3)

            def turn(t, u, rows=P):
                e.wait_ge(x_hn, t + 1)
                if not (isinstance(t, int) and t < 2):
                    e.wait_ge(x_ev, 2 * t - 2)
                    e.wait_ge(x_lo, t - 1)
                for src, b in ((xin, 4 * u), (hn, 4 * u + 2)):
                    for k in range(KC):
                        mm = e.transpose(PS[:, b + k // 4, (k % 4) * P:(k % 4) * P + rows],
                                         src[0:rows, u, k * P:(k + 1) * P], identF[0:rows, 0:rows])
                mm.then_inc(x_tp, 1)

            turn(0, 0)
            turn(1, 1)
            with e.Fori(1, 8) as i:
                for u in range(2):
                    turn(2 * i + u, u)
            turn(16, 0, TAIL)
            e.wait_ge(x_ev, 2 * NT)
            e.wait_ge(x_lo, NT)

            def project(n, u, j, hi, lo, w_hi_t, w_lo_t):
                e.wait_ge(g_ev, 5 * n + j + 1)
                for k in range(KC):
                    for q, (w, x) in enumerate(((w_hi_t, hi), (w_hi_t, lo), (w_lo_t, hi))):
                        mm = e.matmul(PS[:, j, 0:BW], w[:, u, k], x[:, k, cols(j)],
                                      start=(k == 0 and q == 0), stop=(k == KC - 1 and q == 2))
                mm.then_inc(g_mm, 1)

            def chunk(n, u, after=None):
                e.wait_ge(w_lo, n + 1)
                for j in range(NB):
                    project(n, u, j, XH, XL, WH, WL)
                    if after:
                        after(j)

            with e.Fori(0, 4) as c:
                chunk(2 * c, 0)

                def tail(j, c=c):
                    if j == 0:
                        e.wait_ge(g_ev, 10 * c + 10)
                        e.wait_ge(t_ev, c + 1)
                        e.transpose(PS[0:TAIL, 5, 0:P], ZS[:, NB - 1, 3 * P:BW], identF[:]).then_inc(t_pe, 1)

                chunk(2 * c + 1, 1, tail)
            chunk(8, 0)
            e.wait_ge(g_ev, 50)
            e.wait_ge(t_ev, 5)
            for t in range(NT):
                w = min(P, TP - t * P)
                mm = e.transpose(PS[0:w, 5, t * NH:(t + 1) * NH], RX[0:NH, 3 + t * P:3 + t * P + w],
                                 identF[0:NH, 0:NH])
            mm.then_inc(f_tp, 1)
            e.wait_ge(f_dv, 2)
            flat = FL[:].rearrange("p t h -> p (t h)")
            e.wait_ge(c_pool, 14)
            e.matmul(PS[:, 6, 0:NT * NH], triu[:], flat, start=True, stop=True)
            e.matmul(PS[:, 7, 0:NT * NH], onesF[:], flat, start=True, stop=True).then_inc(f_tp, 1)
            e.wait_ge(f_dv, 3)
            for g in range(NB):
                if g >= 3:
                    e.wait_ge(f_ev, g - 2)
                for t in range(4 * g, min(4 * g + 4, NT)):
                    w = min(P, TP - t * P)
                    mm = e.transpose(PS[0:16, 5 + g % 3, (t % 4) * P:(t % 4) * P + w], FD[0:w, t, :],
                                     identF[0:w, 0:w])
                mm.then_inc(f_tp, 1)
            e.wait_ge(f_dv, 4)

            with e.Fori(0, 2) as i:
                for u in range(2):
                    c = 2 * i + u
                    n = 9 + 3 * c
                    ev = 4 + 11 * c

                    def turn_rows(done, ev, j):
                        e.wait_ge(g_ev, done)
                        e.wait_ge(t_ev, ev + 1)
                        for m, (o, w) in enumerate(seg(j)):
                            mm = e.transpose(PS[0:w, 5, m * P:(m + 1) * P], ZS[:, j, o:o + w], identF[:])
                        mm.then_inc(t_pe, 1)

                    def after_k(j):
                        if j == 0:
                            e.wait_ge(g_ev, 5 * n + 10)
                            e.wait_ge(t_ev, ev + 1)
                            e.transpose(PS[0:TAIL, 5, 0:P], ZS[:, NB - 1, 3 * P:BW], identF[:]).then_inc(t_pe, 1)
                        else:
                            turn_rows(5 * (n + 1) + j - 1 + 6, ev + j, j - 1)
                        e.wait_ge(r_conv, c + 1)
                        e.wait_ge(r_gw, 64 * c + 64)
                        e.wait_ge(r_act, 22 * c + (4 * j - 1 if j else 1))
                        e.matmul(PS[:, 6, 0:BW], gw[:, 0], RC[:, cols(j)], start=True, stop=True)
                        e.matmul(PS[:, 7, 0:BW], gw[:, 1], RC[:, cols(j)], start=True, stop=True).then_inc(r_gate, 1)

                    def after_v(j):
                        if j == 0:
                            turn_rows(5 * (n + 1) + 4 + 6, ev + 5, NB - 1)
                        else:
                            turn_rows(5 * (n + 2) + j - 1 + 6, ev + 5 + j, j - 1)

                    chunk(n, (1 + u) % 2)
                    chunk(n + 1, u % 2, after_k)
                    chunk(n + 2, (1 + u) % 2, after_v)
                    turn_rows(5 * (n + 2) + 4 + 6, ev + 10, NB - 1)
            e.wait_ge(g_mm, 5 * NIN)
            e.wait_ge(t_pe, 49)
            e.wait_ge(r_gate, 21)
            e.sem_inc(phase_end, 1)
            def max_piece(i, v, p):
                qt, pc, k0, n, rows, diag = PIECES[p]
                if p == 0:
                    e.wait_ge(prep, 7 * i + 3)
                if p >= 2:
                    e.wait_ge(mx, 45 * i + p - 1)
                elif not (isinstance(i, int) and i == 0):
                    e.wait_ge(na, 5 * i)
                o = PS[0:rows, 2 + p % 2]
                mm = e.matmul(o[:, 0:n], QA[0:HD + 4, v, qt * P:qt * P + rows], KA[0:HD + 4, v, k0:k0 + n],
                              start=True, stop=not diag)
                if diag:
                    d = min(P, n)
                    mm = e.matmul(o[:, n - d:n], identB[0:rows, 0:rows], maskQ[0:rows, 0:d], start=False, stop=True)
                mm.then_inc(mm_mx, 1)

            def maxima_rows(i, g):
                if g == 0:
                    e.wait_ge(nm, 3 * i + 3)
                if g >= 2:
                    e.wait_ge(na, 5 * i + g - 1)
                e.sem_inc(go, 1)
                for t in range(4 * g, min(4 * g + 4, NT)):
                    w = min(P, TP - t * P)
                    mm = e.transpose(PS[0:HD + 2, 3 - g % 2, (t % 4) * P:(t % 4) * P + w], NM[0:w, t, :],
                                     identF[0:w, 0:w])
                mm.then_inc(nt, 1)

            def cached_rows(g):
                by_head = lpage[:, g].rearrange("p (s h) -> p h s", h=NH)
                if g:
                    e.wait_ge(lf_ev, 4)
                for b in range(2):
                    for h in range(4):
                        mm = e.transpose(PS[:, b, h * P:(h + 1) * P], by_head[:, 4 * b + h], identF[:])
                    mm.then_inc(lf_tp, 1)

            def cached_sums(g):
                e.wait_ge(lf_ev, 4 * g + 2)
                for b in range(2):
                    e.matmul(PS[:, 4 + 2 * b, :], triu[:], xtp[:, 512 * b:512 * b + 512], start=True, stop=True)
                    e.matmul(PS[:, 5 + 2 * b, :], onesF[:], xtp[:, 512 * b:512 * b + 512], start=True, stop=True)\
                        .then_inc(lf_tp, 1)

            e.wait_ge(g_ev, 5 * NIN + 5)
            for p in range(len(PIECES)):
                max_piece(0, 0, p)
                if p == 20:
                    e.wait_ge(phase_end, 4)
                    e.wait_ge(lf_pg, 32)
                if p in (20, 32):
                    cached_rows(p // 32)
                if p in (26, 38):
                    cached_sums(p // 38)
            for g in range(NB):
                maxima_rows(0, g)
            e.wait_ge(lf_ev, 8)

            def pe_head(i, u, plan):
                def scores(t):
                    j, kt, q0, n, kr = TILES[t]
                    if t == 0:
                        e.wait_ge(na, 5 * i + 5)
                        e.wait_ge(prep, 7 * i + 7)
                    e.wait_ge(ex, 51 * i + t + 3)
                    o = PS[0:kr, (u + t) % 2]
                    ks, qs = slice(kt * P, kt * P + kr), slice(q0, q0 + n)
                    e.matmul(o[:, 0:n], KA[0:HD + 4, u, ks], QA[0:HD + 4, u, qs], start=True, stop=False)
                    d = min(n, kt * P + P - q0)
                    mm = e.matmul(o[:, 0:n], KB[:, u, ks], QB[:, u, qs], start=False, stop=d <= 0)
                    if d > 0:
                        m = q0 - kt * P
                        mm = e.matmul(o[:, 0:d], identB[0:kr, 0:kr], maskK[0:kr, m:m + d], start=False, stop=True)
                    mm.then_inc(sT, 1)

                def values(t):
                    j, kt, q0, n, kr = TILES[t]
                    if kt == 0:
                        e.wait_ge(on, 5 * i + j + 4)
                        if j == 0:
                            e.wait_ge(va_ld[u], 16 * (i - u) + 32)
                    e.wait_ge(ex, 51 * i + t + 5)
                    o = q0 - j * BW
                    e.matmul(PS[:, 4 + (u + j) % 2, o:o + n], VA[0:kr, u, kt], PT[0:kr, t % 3, 0:n], start=(kt == 0),
                             stop=t in ENDS).then_inc(pv, 1)

                def pages(g):
                    if g == 0:
                        e.wait_ge(de, 2 * i + 2)
                        e.wait_ge(dn, i + 1)
                        e.wait_ge(od_s, 2 * i + 1)
                        e.wait_ge(at_s, i + 1)
                    e.wait_ge(vg_ld[g % 4], 32 * (4 * i + g // 4) + 32)
                    for m in range(2):
                        mm = e.matmul(PS[0:NH, 7, :], sc[:, u, 2 * g + m, :], Vpg[:, g % 4, m], start=(g == 0 and m == 0),
                                      stop=False)
                    mm.then_inc(vd, 1)
                    if g == PAGES // 2 - 1:
                        e.wait_ge(nw_ld, 48 * i + 48)
                        e.sem_inc(go, 1)
                        e.matmul(PS[0:NH, 7, :], sn[0:1, u, :], vnew[:, u], start=False, stop=True)
                        e.matmul(PS[0:NH, 6, 0:1], dsum[:, u], onesF[:, 0:1], start=True, stop=False)
                        e.matmul(PS[0:NH, 6, 0:1], sn[0:1, u, :], onesF[0:1, 0:1], start=False, stop=True)\
                            .then_inc(df, 1)

                scores(0)
                for t in range(len(TILES)):
                    if t + 1 < len(TILES):
                        scores(t + 1)
                    values(t)
                    for what, n in plan[t]:
                        if what == "columns":
                            sample_columns(i - 1 + n)
                        if what == "piece":
                            max_piece(i + 1, 1 - u, n)
                        if what == "row":
                            maxima_rows(i + 1, n)
                        if what == "pages":
                            pages(n)

            def sample_columns(s):
                e.wait_ge(od_s, 2 * s + 3)
                for c in range(4):
                    mm = e.matmul(PS[:, 6, 8 + c:9 + c], od[:, c * P:(c + 1) * P], onesF[0:NH, 0:1], start=True, stop=True)
                mm.then_inc(av, 1)

            pe_head(0, 0, PLANS[0])
            with e.Fori(0, 3) as ii:
                for v in range(2):
                    pe_head(2 * ii + 1 + v, 1 - v, PLANS[1])
            pe_head(7, 1, PLANS[2])
            e.wait_ge(pv, 51 * NH + 1)
            e.wait_ge(df, NS + 1)
            e.wait_ge(av, NS)
            e.sem_inc(phase_end, 1)
            e.wait_ge(phase_end, 8)

            def norm_total(n):
                e.wait_ge(nsq, n + 1)
                if n >= 2:
                    e.wait_ge(nrs, n - 1)
                parts = 2 if n < 10 else 1
                for k in range(KC):
                    p, q = divmod(k, KC // parts)
                    mm = e.matmul(PS[:, 5 + n % 2, p * HB:(p + 1) * HB], onesF[:], SQ[:, k, cols(n % 10, HB)],
                                  start=(q == 0), stop=(q == KC // parts - 1))
                mm.then_inc(nmm, 1)

            def dense(m, u, j):
                e.wait_ge(u_ev, 5 * m + j + 1)
                for k in range(KC):
                    for q, (w, x) in enumerate(((VH, MH), (VH, ML), (VL, MH))):
                        mm = e.matmul(PS[:, j, 0:BW], w[:, u, k], x[:, k, cols(j)], start=(k == 0 and q == 0),
                                      stop=(k == KC - 1 and q == 2))
                mm.then_inc(u_mm, 1)

            for n in range(3):
                norm_total(n)
            for j in range(NB):
                for n in range(2 * j + 3, min(2 * j + 5, 10)):
                    norm_total(n)
                e.wait_ge(v_lo, 1)
                e.wait_ge(nlo, 2 * j + 2)
                dense(0, 0, j)
            with e.Fori(0, 3) as i:
                for u in range(2):
                    e.wait_ge(v_lo, 2 * i + u + 2)
                    for j in range(NB):
                        dense(2 * i + u + 1, 1 - u, j)
            e.wait_ge(v_lo, 8)
            for j in range(NB):
                dense(7, 1, j)
                if j >= 2:
                    norm_total(8 + j)
            e.wait_ge(v_lo, 9)
            for j in range(NB):
                for n in range(2 * j + 13, min(2 * j + 15, 20)):
                    norm_total(n)
                e.wait_ge(nlo, 10 + 2 * j + 2)
                dense(8, 0, j)

            def values_chunk(f, u):
                e.wait_ge(v_lo, 2 * f + 10)
                for j in range(NB):
                    dense(9 + 2 * f, 1, j)
                    if j == 0:
                        e.wait_ge(u_ev, 5 * (8 + 2 * f) + 10)
                        e.wait_ge(tt_ev, f + 1)
                        e.sem_inc(go, 1)
                        e.transpose(PS[0:TAIL, 7, 0:P], GP[:, u, 2 + TP - TAIL:2 + TP], identF[:]).then_inc(tt_pe, 1)

            values_chunk(0, 0)
            with e.Fori(0, 10) as i:
                for u in range(2):
                    f = 2 * i + u + 1
                    e.wait_ge(v_lo, 2 * f + 9)
                    for j in range(NB):
                        dense(8 + 2 * f, 0, j)
                    values_chunk(f, 1 - u)
            e.wait_ge(v_lo, 51)
            for j in range(NB):
                dense(50, 0, j)
            values_chunk(21, 1)
            e.wait_ge(u_mm, 5 * 52)
            e.wait_ge(tt_pe, FC + 1)
            e.wait_ge(nmm, 20)
            e.sem_inc(phase_end, 1)
            e.wait_ge(phase_end, 12)
            def turn_sum(n, v):
                e.wait_ge(y_ev, n + 1)
                if not (isinstance(n, int) and n < 2):
                    e.wait_ge(y_tk, n)
                e.sem_inc(go, 1)
                for m, (o, w) in enumerate(seg(0)):
                    mm = e.transpose(PS[0:w, 4 + v, m * P:(m + 1) * P], YX[:, v, o:o + w], identF[:])
                mm.then_inc(y_tp, 1)

            for j in range(NB):
                def pe_pair(i, first=False):
                    n, oc = 16 * j + 4 * i, 8 * j + 2 * i
                    for c in range(4):
                        v, h = c // 2, c % 2
                        e.wait_ge(d_lo, n + c + 1)
                        if h == 0 and not (first and j == 0):
                            e.wait_ge(y_ev, oc + v - 1)
                        for k in range(FH):
                            kk = FH * h + k
                            if first and v == 0 and kk % 2 == 0:
                                e.wait_ge(gg_lo, FH * j + kk // 2 + 1)
                            r, m = (FH * j + kk // 2) % RING, kk % 2
                            e.matmul(PS[:, v, 0:BW], DH[:, h, k], GH[:, r, m], start=(kk == 0), stop=False)
                            e.matmul(PS[:, v, 0:BW], DH[:, h, k], GL[:, r, m], start=False, stop=False)
                            e.matmul(PS[:, v, 0:BW], DL[:, h, k], GH[:, r, m], start=False, stop=(kk == FC - 1))\
                                .then_inc(dk, 1)
                        if c == 0 and not (first and j == 0):
                            turn_sum(oc - 1, 1)
                        if c == 2:
                            turn_sum(oc, 0)

                pe_pair(0, True)
                with e.Fori(1, 4) as i:
                    pe_pair(i)
            turn_sum(8 * NB - 1, 1)




_OUTS = [
    ("y_prompt", (1, SEQ, DM)), ("y_sample", (NS, 1, DM)),
    ("k_prompt", (1, 1, TPR, NH, HD)), ("v_prompt", (1, 1, TPR, NH, HD)), ("logf_prompt", (1, 1, TPR, NH)),
    ("rnn_h_prompt", (1, 1, DRNN)), ("rnn_conv_prompt", (1, 1, 3, DRNN)), ("ffn_conv_prompt", (1, 1, 2, DFF)),
    ("k_sample", (1, NS, 1, NH, HD)), ("v_sample", (1, NS, 1, NH, HD)), ("logf_sample", (1, NS, 1, NH)),
    ("rnn_h_sample", (1, NS, DRNN)), ("rnn_conv_sample", (1, NS, 3, DRNN)), ("ffn_conv_sample", (1, NS, 2, DFF)),
]


def chunked(w):
    rows, columns = w.shape
    return w.reshape(rows // P, P, columns // P, P).transpose(2, 1, 0, 3)


def lay_out(x):
    x = {k: np.asarray(v) for k, v in x.items()}
    w = x["w_in"][0]
    main = np.concatenate([w[:, :C_F], w[:, C_XR:]], axis=1)
    forget = np.concatenate([w[:, C_F:C_XR], np.zeros((DM, P - NH), w.dtype)], axis=1)
    c = chunked(main)
    order = [c[12 + i // 2 + 4 * (i % 2)] for i in range(8)] + [chunked(forget)[0]]
    order += [c[4 * m + i] for i in range(4) for m in range(3)]
    o = {}
    o["w_stream"] = np.stack(order)
    o["w_out"] = chunked(x["w_out"][0])
    up = chunked(x["w_ffn_up"][0])
    o["w_up"] = np.stack([up[:FC], up[FC:]], axis=1)
    down = chunked(x["w_ffn_down"][0])
    o["w_down"] = down.reshape(KC, P, 2, FC // 2, P).transpose(0, 2, 1, 3, 4)
    o["norm_mix"] = x["norm_mix"]
    o["norm_final"] = x["norm_final"][None]
    o["gains"] = np.concatenate([x["norm_att_out"][0], x["norm_rnn_out"][0], x["norm_ffn"][0]]).reshape(16, P).T
    rows = [x["rnn_conv_w"][0][j] for j in range(4)]
    rows += [x["rnn_conv_b"][0], x["b_rg_a"][0], x["b_rg_x"][0], x["rg_lambda"][0]]
    o["rnn_table"] = np.stack(rows).reshape(8, 4, P).transpose(2, 1, 0)
    o["rnn_state"] = x["state_rnn_conv"][0].reshape(NS, 3, 4, P).transpose(3, 2, 1, 0)
    o["rnn_h"] = x["state_rnn_h"][0].reshape(NS, 4, P).transpose(2, 1, 0)
    rows = [x["ffn_conv_w"][0][j] for j in range(3)] + [x["ffn_conv_b"][0]]
    o["ffn_table"] = np.stack(rows).reshape(4, FC, P).transpose(2, 1, 0)
    o["ffn_state"] = x["state_ffn_conv"][0].reshape(NS, 2, FC, P).transpose(3, 2, 1, 0)
    o["page_table"] = x["page_table"].reshape(1, NPG)
    o["page_column"] = x["page_table"].reshape(2, P).T
    for k in ("x_prompt", "x_sample", "meta_tokens", "b_forget", "w_rg_a", "w_rg_x", "cache_k", "cache_v",
              "cache_logf", "state_rnn_conv", "state_ffn_conv"):
        o[k] = x[k]
    return {k: np.ascontiguousarray(v) for k, v in o.items()}


def kernel(**inputs):
    import concourse.bacc as bacc
    from concourse.bass_utils import run_bass_kernel_spmd

    nc = bacc.Bacc("TRN2", target_bir_lowering=False, num_devices=1)
    arrays, args, outs = {}, {}, {}
    for name, v in lay_out(inputs).items():
        arrays["in_" + name] = v
        args[name] = nc.dram_tensor("in_" + name, v.shape, mybir.dt.from_np(v.dtype), kind="ExternalInput").ap()
    for name, shape in _OUTS:
        outs[name] = nc.dram_tensor("out_" + name, shape, F32, kind="ExternalOutput").ap()
    build(nc, args, outs)
    r = run_bass_kernel_spmd(nc, [arrays], core_ids=[0])
    return tuple(r.results[0]["out_" + name] for name, _ in _OUTS)
```
